# Optimizing a Trainium2 kernel written in Bass

```python
import jax, jax.numpy as jnp
from jax import lax
import numpy as np

D_MODEL = 2048
BATCH = 1
SEQ = 256
DEPTH = 1

HEAD_DIM = 128
N_ATTN_HEADS = 8
ATTN_WIDTH = N_ATTN_HEADS * HEAD_DIM
N_CONV_GROUPS = 8
CONV_CH = N_CONV_GROUPS * HEAD_DIM
MIX_WIDTH = ATTN_WIDTH + CONV_CH
IN_COLS = 3 * ATTN_WIDTH + 2 * CONV_CH
CONV_K = 31
MOBA_BLOCK = 256
MOBA_TOPK = 3
Q_CHUNK = 128
D_FF = -(-8 * D_MODEL // (3 * 256)) * 256
N_MOD = 6
RMS_EPS = 1e-6
LN_EPS = 1e-5
NEG_INF = -1e30


def rms_norm(x, g):
    x32 = x.astype(jnp.float32)
    y = x32 * lax.rsqrt(jnp.mean(x32 * x32, axis=-1, keepdims=True) + RMS_EPS)
    return (y * g.astype(jnp.float32)).astype(x.dtype)

def layer_norm(x, g, b):
    x32 = x.astype(jnp.float32)
    mu = jnp.mean(x32, axis=-1, keepdims=True)
    var = jnp.mean(jnp.square(x32 - mu), axis=-1, keepdims=True)
    y = (x32 - mu) * lax.rsqrt(var + LN_EPS) * g.astype(jnp.float32) + b.astype(jnp.float32)
    return y.astype(x.dtype)

def causal_depthwise_conv(u, w, b):
    k = w.shape[0]
    y = lax.conv_general_dilated(
        u, w[:, None, :].astype(u.dtype), window_strides=(1,),
        padding=((k - 1, 0),), dimension_numbers=('NWC', 'WIO', 'NWC'),
        feature_group_count=u.shape[-1])
    return y + b.astype(u.dtype)

def moba_attention(q, k, v):
    B, H, S, Dh = q.shape
    nb = -(-S // MOBA_BLOCK)
    n_sel = min(MOBA_TOPK, nb)
    pad = nb * MOBA_BLOCK - S
    kb = jnp.pad(k, ((0, 0), (0, 0), (0, pad), (0, 0))).reshape(B, H, nb, MOBA_BLOCK, Dh)
    vb = jnp.pad(v, ((0, 0), (0, 0), (0, pad), (0, 0))).reshape(B, H, nb, MOBA_BLOCK, Dh)
    k_mean = jnp.mean(kb.astype(jnp.float32), axis=3)
    n_chunks = S // Q_CHUNK
    q_chunks = q.reshape(B, H, n_chunks, Q_CHUNK, Dh).transpose(2, 0, 1, 3, 4)
    scale = HEAD_DIM ** -0.5
    b_idx = jnp.arange(B)[:, None, None]
    h_idx = jnp.arange(H)[None, :, None]
    blk_ids = jnp.arange(nb)

    def one_chunk(args):
        qc, ci = args
        q_pos = ci * Q_CHUNK + jnp.arange(Q_CHUNK)
        blk = (ci * Q_CHUNK) // MOBA_BLOCK
        gate = jnp.einsum('bhqd,bhnd->bhqn', qc.astype(jnp.float32), k_mean)
        gate = jnp.where(blk_ids < blk, gate, NEG_INF)
        _, sel = lax.top_k(gate, n_sel)
        k_own = lax.dynamic_index_in_dim(kb, blk, axis=2, keepdims=False)
        v_own = lax.dynamic_index_in_dim(vb, blk, axis=2, keepdims=False)
        k_pos = blk * MOBA_BLOCK + jnp.arange(MOBA_BLOCK)
        s_own = jnp.einsum('bhqd,bhkd->bhqk', qc, k_own,
                           preferred_element_type=jnp.float32) * scale
        s_own = jnp.where(k_pos[None, :] <= q_pos[:, None], s_own, NEG_INF)
        scores = [s_own]
        for j in range(n_sel):
            k_sel = kb[b_idx, h_idx, sel[..., j]]
            s_j = jnp.einsum('bhqd,bhqkd->bhqk', qc, k_sel,
                             preferred_element_type=jnp.float32) * scale
            scores.append(jnp.where(j < blk, s_j, NEG_INF))
        p = jax.nn.softmax(jnp.concatenate(scores, axis=-1), axis=-1).astype(v.dtype)
        p = p.reshape(B, H, Q_CHUNK, n_sel + 1, MOBA_BLOCK)
        out = jnp.einsum('bhqk,bhkd->bhqd', p[..., 0, :], v_own,
                         preferred_element_type=jnp.float32)
        for j in range(n_sel):
            v_sel = vb[b_idx, h_idx, sel[..., j]]
            out = out + jnp.einsum('bhqk,bhqkd->bhqd', p[..., j + 1, :], v_sel,
                                   preferred_element_type=jnp.float32)
        return out.astype(q.dtype)

    out = lax.map(one_chunk, (q_chunks, jnp.arange(n_chunks)))
    return out.transpose(1, 2, 0, 3, 4).reshape(B, H, S, Dh)

def hybrid_mixer(h, w_in, conv_w, conv_b, conv_ln_g, conv_ln_b, w_out):
    B, S, _ = h.shape
    proj = h @ w_in
    q, k, v, a, g = jnp.split(
        proj, [ATTN_WIDTH, 2 * ATTN_WIDTH, 3 * ATTN_WIDTH, 3 * ATTN_WIDTH + CONV_CH], axis=-1)

    def heads(t):
        return t.reshape(B, S, N_ATTN_HEADS, HEAD_DIM).transpose(0, 2, 1, 3)

    attn = moba_attention(heads(q), heads(k), heads(v))
    attn = attn.transpose(0, 2, 1, 3).reshape(B, S, ATTN_WIDTH)
    u = a * jax.nn.sigmoid(g)
    u = causal_depthwise_conv(u, conv_w, conv_b)
    u = jax.nn.silu(layer_norm(u, conv_ln_g, conv_ln_b))
    mix = jnp.concatenate([attn, u], axis=-1)
    return mix @ w_out

def swiglu_ffn(h, w_gate, w_up, w_down):
    return (jax.nn.silu(h @ w_gate) * (h @ w_up)) @ w_down

def first_inputs(seed: int = 0) -> dict:
    key = jax.random.key(seed)
    ks = jax.random.split(key, 18)

    def nrm(k, shape, s):
        return jax.random.normal(k, shape, jnp.float32) * s

    L, D = DEPTH, D_MODEL
    return {
        'x': nrm(ks[0], (BATCH, SEQ, D), 1.0),
        'c': nrm(ks[1], (BATCH, D), 1.0),
        'ada_w': nrm(ks[2], (L, D, N_MOD * D), 0.5 * D ** -0.5),
        'ada_b': nrm(ks[3], (L, N_MOD * D), 0.02),
        'mix_pre_g': 1.0 + nrm(ks[4], (L, D), 0.02),
        'mix_post_g': 1.0 + nrm(ks[5], (L, D), 0.02),
        'w_in': nrm(ks[6], (L, D, IN_COLS), D ** -0.5),
        'conv_w': nrm(ks[7], (L, CONV_K, CONV_CH), CONV_K ** -0.5),
        'conv_b': nrm(ks[8], (L, CONV_CH), 0.02),
        'conv_ln_g': 1.0 + nrm(ks[9], (L, CONV_CH), 0.02),
        'conv_ln_b': nrm(ks[10], (L, CONV_CH), 0.02),
        'w_out': nrm(ks[11], (L, MIX_WIDTH, D), MIX_WIDTH ** -0.5),
        'ffn_pre_g': 1.0 + nrm(ks[12], (L, D), 0.02),
        'ffn_post_g': 1.0 + nrm(ks[13], (L, D), 0.02),
        'w_gate': nrm(ks[14], (L, D, D_FF), D ** -0.5),
        'w_up': nrm(ks[15], (L, D, D_FF), D ** -0.5),
        'w_down': nrm(ks[16], (L, D_FF, D), D_FF ** -0.5),
    }

def first_block(x, c, ada_w, ada_b, mix_pre_g, mix_post_g, w_in, conv_w, conv_b,
              conv_ln_g, conv_ln_b, w_out, ffn_pre_g, ffn_post_g, w_gate, w_up, w_down):
    c_act = jax.nn.silu(c)
    for l in range(DEPTH):
        mod = c_act @ ada_w[l] + ada_b[l]
        sh1, sc1, g1, sh2, sc2, g2 = jnp.split(mod, N_MOD, axis=-1)
        h = rms_norm(x, mix_pre_g[l]) * (1.0 + sc1[:, None, :]) + sh1[:, None, :]
        y = hybrid_mixer(h, w_in[l], conv_w[l], conv_b[l], conv_ln_g[l], conv_ln_b[l], w_out[l])
        x = x + g1[:, None, :] * rms_norm(y, mix_post_g[l])
        h = rms_norm(x, ffn_pre_g[l]) * (1.0 + sc2[:, None, :]) + sh2[:, None, :]
        y = swiglu_ffn(h, w_gate[l], w_up[l], w_down[l])
        x = x + g2[:, None, :] * rms_norm(y, ffn_post_g[l])
    return x


CHUNK = 64
N_META = 16
D_ATTN = D_MODEL // 2
ATTN_HEADS = D_ATTN // HEAD_DIM
POOL_WINDOWS = (2, 4, 8, 16)
N_POOL_GROUPS = len(POOL_WINDOWS)
D_POOL = D_MODEL // 2
POOL_GROUP_DIM = D_POOL // N_POOL_GROUPS
D_FF_2 = 11 * D_MODEL // 4
CONV_WIDTH = 3
Q_BLOCK = 128
EPS = 1e-6

SPLIT_SIZES = (D_ATTN, D_ATTN, D_ATTN, ATTN_HEADS, D_POOL, D_MODEL, D_MODEL)
SPLIT_IDX = tuple(int(i) for i in np.cumsum(SPLIT_SIZES)[:-1])
D_IN = sum(SPLIT_SIZES)
F_OFF = 3 * D_ATTN


def rmsnorm(x, g):
    xf = x.astype(jnp.float32)
    y = xf * lax.rsqrt(jnp.mean(xf * xf, axis=-1, keepdims=True) + EPS)
    return (y * g.astype(jnp.float32)).astype(x.dtype)

def forgetting_attention(q, k, v, logf):
    B, L, H, Dh = q.shape
    n_blocks = -(-L // Q_BLOCK)
    Lp = n_blocks * Q_BLOCK
    pad = ((0, 0), (0, Lp - L), (0, 0), (0, 0))
    q = jnp.pad(q, pad)
    k = jnp.pad(k, pad)
    v = jnp.pad(v, pad)
    logf = jnp.pad(logf, ((0, 0), (0, Lp - L), (0, 0)))
    c = jnp.cumsum(logf, axis=1)
    c = jnp.transpose(c, (0, 2, 1))
    scale = HEAD_DIM ** -0.5
    pos = jnp.arange(Lp)
    outs = []
    for i in range(n_blocks):
        q0, q1 = i * Q_BLOCK, (i + 1) * Q_BLOCK
        qb = q[:, q0:q1]
        kb = k[:, :q1]
        vb = v[:, :q1]
        s = jnp.einsum('bqhd,bkhd->bhqk', qb, kb).astype(jnp.float32) * scale
        bias = c[:, :, q0:q1, None] - c[:, :, None, :q1]
        mask = pos[q0:q1, None] >= pos[None, :q1]
        s = jnp.where(mask[None, None], s + bias, -jnp.inf)
        p = jax.nn.softmax(s, axis=-1).astype(vb.dtype)
        outs.append(jnp.einsum('bhqk,bkhd->bqhd', p, vb))
    o = jnp.concatenate(outs, axis=1)[:, :L]
    return o.reshape(B, L, H * Dh)

def multiscale_pool(u, pool_w, pool_scale):
    B, L, _ = u.shape
    uf = u.astype(jnp.float32).reshape(B, L, N_POOL_GROUPS, POOL_GROUP_DIM)
    csum = jnp.cumsum(uf, axis=1)
    pos = jnp.arange(L)
    outs = []
    for g, w in enumerate(POOL_WINDOWS):
        cg = csum[:, :, g]
        prev = jnp.pad(cg[:, :L - w], ((0, 0), (w, 0), (0, 0)))
        cnt = jnp.minimum(pos + 1, w).astype(jnp.float32)[None, :, None]
        outs.append((cg - prev) / cnt - uf[:, :, g])
    d = jnp.stack(outs, axis=2).astype(u.dtype)
    y = jnp.einsum('blgc,gcd->blgd', d, pool_w).reshape(B, L, D_POOL)
    return y * pool_scale

def mixer_block(h, w_in, b_in, w_attn_o, pool_w, pool_scale, w_pool_o, w_out):
    B, L, _ = h.shape
    z = h @ w_in + b_in
    q, k, v, f_logit, u, g_attn, g_pool = jnp.split(z, SPLIT_IDX, axis=-1)
    q = q.reshape(B, L, ATTN_HEADS, HEAD_DIM)
    k = k.reshape(B, L, ATTN_HEADS, HEAD_DIM)
    v = v.reshape(B, L, ATTN_HEADS, HEAD_DIM)
    logf = jax.nn.log_sigmoid(f_logit.astype(jnp.float32))
    attn = forgetting_attention(q, k, v, logf)
    pool = multiscale_pool(u, pool_w, pool_scale)
    m = jax.nn.sigmoid(g_attn) * (attn @ w_attn_o) + jax.nn.sigmoid(g_pool) * (pool @ w_pool_o)
    return m @ w_out

def causal_dwconv(a, conv_w, conv_b):
    L = a.shape[1]
    ap = jnp.pad(a, ((0, 0), (CONV_WIDTH - 1, 0), (0, 0)))
    out = conv_b
    for j in range(CONV_WIDTH):
        out = out + ap[:, j:j + L] * conv_w[j]
    return out

def conv_ffn(h, w_up, conv_w, conv_b, w_down):
    a = causal_dwconv(h @ w_up, conv_w, conv_b)
    gate, val = jnp.split(a, 2, axis=-1)
    return (jax.nn.gelu(gate, approximate=True) * val) @ w_down

def second_inputs(seed: int = 0) -> dict:
    key = jax.random.key(seed)
    ks = jax.random.split(key, 18)
    f32 = jnp.float32
    nrm = lambda k, shape, s: jax.random.normal(k, shape, f32) * s
    gain = lambda k, n: jnp.ones((DEPTH, n), f32) + nrm(k, (DEPTH, n), 0.02)
    b_in = nrm(ks[4], (DEPTH, D_IN), 0.02)
    f_bias = jax.random.uniform(ks[5], (DEPTH, ATTN_HEADS), f32, 1.0, 5.0)
    b_in = b_in.at[:, F_OFF:F_OFF + ATTN_HEADS].add(f_bias)
    return {
        'x': nrm(ks[0], (BATCH, SEQ, D_MODEL), 1.0),
        'meta_tokens': nrm(ks[1], (N_META, D_MODEL), 1.0),
        'mix_pre_g': gain(ks[2], D_MODEL),
        'w_in': nrm(ks[3], (DEPTH, D_MODEL, D_IN), D_MODEL ** -0.5),
        'b_in': b_in,
        'w_attn_o': nrm(ks[6], (DEPTH, D_ATTN, D_MODEL), D_ATTN ** -0.5),
        'pool_w': nrm(ks[7], (DEPTH, N_POOL_GROUPS, POOL_GROUP_DIM, POOL_GROUP_DIM), POOL_GROUP_DIM ** -0.5),
        'pool_scale': jnp.ones((DEPTH, D_POOL), f32) + nrm(ks[8], (DEPTH, D_POOL), 0.1),
        'w_pool_o': nrm(ks[9], (DEPTH, D_POOL, D_MODEL), D_POOL ** -0.5),
        'w_out': nrm(ks[10], (DEPTH, D_MODEL, D_MODEL), D_MODEL ** -0.5),
        'mix_post_g': gain(ks[11], D_MODEL),
        'ffn_pre_g': gain(ks[12], D_MODEL),
        'w_ffn_up': nrm(ks[13], (DEPTH, D_MODEL, 2 * D_FF_2), D_MODEL ** -0.5),
        'ffn_conv_w': nrm(ks[14], (DEPTH, CONV_WIDTH, 2 * D_FF_2), CONV_WIDTH ** -0.5),
        'ffn_conv_b': nrm(ks[15], (DEPTH, 2 * D_FF_2), 0.02),
        'w_ffn_down': nrm(ks[16], (DEPTH, D_FF_2, D_MODEL), D_FF_2 ** -0.5),
        'ffn_post_g': gain(ks[17], D_MODEL),
    }

def second_block(x, meta_tokens, mix_pre_g, w_in, b_in, w_attn_o, pool_w, pool_scale, w_pool_o,
              w_out, mix_post_g, ffn_pre_g, w_ffn_up, ffn_conv_w, ffn_conv_b, w_ffn_down,
              ffn_post_g):
    B = x.shape[0]
    meta = jnp.broadcast_to(meta_tokens.astype(x.dtype)[None], (B, N_META, D_MODEL))
    r = jnp.concatenate([meta, x], axis=1)
    for l in range(DEPTH):
        h = rmsnorm(r, mix_pre_g[l])
        mix = mixer_block(h, w_in[l], b_in[l], w_attn_o[l], pool_w[l], pool_scale[l],
                          w_pool_o[l], w_out[l])
        r = r + rmsnorm(mix, mix_post_g[l])
        h = rmsnorm(r, ffn_pre_g[l])
        ff = conv_ffn(h, w_ffn_up[l], ffn_conv_w[l], ffn_conv_b[l], w_ffn_down[l])
        r = r + rmsnorm(ff, ffn_post_g[l])
    return r[:, N_META:]


def setup_inputs(seed=0):
    out = dict(first_inputs(seed))
    for name, value in second_inputs(seed + 1).items():
        if name != "x":
            out[name + "_2"] = value
    return out


def reference(
    x, c, ada_w, ada_b, mix_pre_g, mix_post_g, w_in, conv_w, conv_b, conv_ln_g, conv_ln_b,
    w_out, ffn_pre_g, ffn_post_g, w_gate, w_up, w_down, meta_tokens_2, mix_pre_g_2, w_in_2,
    b_in_2, w_attn_o_2, pool_w_2, pool_scale_2, w_pool_o_2, w_out_2, mix_post_g_2, ffn_pre_g_2,
    w_ffn_up_2, ffn_conv_w_2, ffn_conv_b_2, w_ffn_down_2, ffn_post_g_2,
):
    x = first_block(
        x, c, ada_w, ada_b, mix_pre_g, mix_post_g, w_in, conv_w, conv_b, conv_ln_g, conv_ln_b,
        w_out, ffn_pre_g, ffn_post_g, w_gate, w_up, w_down,
    )
    return second_block(
        x, meta_tokens_2, mix_pre_g_2, w_in_2, b_in_2, w_attn_o_2, pool_w_2, pool_scale_2,
        w_pool_o_2, w_out_2, mix_post_g_2, ffn_pre_g_2, w_ffn_up_2, ffn_conv_w_2, ffn_conv_b_2,
        w_ffn_down_2, ffn_post_g_2,
    )


_drawn_inputs = setup_inputs


def setup_inputs(seed=0):
    import zlib

    import numpy as np

    out = dict(_drawn_inputs(seed))
    spreads = {}
    factors = {'mix_pre_g': 7.378,
     'mix_post_g': 7.185,
     'conv_b': 4.908,
     'conv_ln_g': 7.377,
     'conv_ln_b': 8.0,
     'ffn_pre_g': 5.957,
     'ffn_post_g': 7.903,
     'mix_pre_g_2': 3.217,
     'mix_post_g_2': 11.642,
     'ffn_pre_g_2': 9.057,
     'ffn_conv_b_2': 21.383,
     'ffn_post_g_2': 65.15}
    for name, (base, spread) in spreads.items():
        noise = np.random.default_rng([zlib.crc32(name.encode()), seed]).standard_normal(out[name].shape)
        drawn = base * np.exp(spread * noise) if base else spread * noise
        out[name] = __import__('jax').numpy.asarray(drawn.astype(out[name].dtype))
    for name, factor in factors.items():
        out[name] = (out[name] * factor).astype(out[name].dtype)
    return out
```

```python
import concourse.bass as bass
from concourse import mybir
from contextlib import ExitStack, contextmanager

D = 2048
KT = D // 128
SEQ, META = 256, 16
ALL = SEQ + META
LIVE0 = META - 2
LIVE = ALL - LIVE0
HD, HEADS = 128, 8
DA = HD * HEADS
AT = DA // 128
CONV_K = 31
F = 5632
FT = F // 128
CHUNK = 512
NCHUNK = F // CHUNK
MODS = 6
SCALE = HD ** -0.5
NEG = -1e30
RING = 4
LEAD = 3
QT = LIVE // 3
QW = (128, 256, 272)
QO = (0, 128, 384)
QSUM = sum(QW)
WINDOWS = (2, 4, 8, 16)
FFN_HALVES = NCHUNK * 24
HALVES = 112 + FFN_HALVES + 48 + 2 + 16 + 2 + 32 + 64 + 32 + FFN_HALVES
U_GROUP = 8 + 12 + 16 + NCHUNK * 12 + 12
X_TOTAL = 4 * KT

SB, ST = slice(META, ALL), slice(LIVE0, ALL)


class Count:

    def __init__(self, start=0):
        self.c, self.i, self.per, self.c0 = start, None, 0, 0

    def enter(self, i, per):
        self.i, self.per, self.c0 = i, per, self.c

    def leave(self, trips):
        assert self.c - self.c0 == self.per, (self.c - self.c0, self.per)
        self.c, self.i = self.c0 + self.per * trips, None

    def at(self, mult=1, add=0):
        base = self.c * mult + add
        return base if self.i is None or not self.per else self.i * (self.per * mult) + base

    def div(self, d, mult, add):
        base = (self.c // d) * mult + add
        if self.i is None or not self.per:
            return base
        assert self.per % d == 0
        return self.i * (self.per // d * mult) + base

    def mod(self, d):
        assert self.i is None or self.per % d == 0
        return self.c % d

    def next(self, n=1, mult=1, add=0):
        self.c += n
        return self.at(mult, add)


@contextmanager
def loop(eng, trips, *counts):
    with eng.Fori(0, trips) as i:
        for c, per in counts:
            c.enter(i, per)
        yield i
    for c, _ in counts:
        c.leave(trips)


def ds(start, size=1):
    return bass.ds(start, size)


def build(nc, x, c, ada_w, ada_b, mix_pre_g, mix_post_g, w_in, conv_w, conv_b, conv_ln_g, conv_ln_b,
          w_out, ffn_pre_g, ffn_post_g, w_gate, w_up, w_down, meta_tokens_2, mix_pre_g_2, w_in_2,
          b_in_2, w_attn_o_2, pool_w_2, pool_scale_2, w_pool_o_2, w_out_2, mix_post_g_2,
          ffn_pre_g_2, w_ffn_up_2, ffn_conv_w_2, ffn_conv_b_2, w_ffn_down_2, ffn_post_g_2, out):
    f32, f32r = mybir.dt.float32, mybir.dt.float32r
    ACT, ALU, AX = mybir.ActivationFunctionType, mybir.AluOpType, mybir.AxisListType
    ctx = ExitStack()
    with ctx:
        base = (nc.sbuf_base + 31) // 32 * 32
        sizes = dict(raw=RING * 8192, hi=RING * 4096, lo=RING * 4096, xt=KT * ALL * 4,
                     hhi=KT * ALL * 4, hlo=KT * ALL * 4, r1=KT * ALL * 4, r2=3 * AT * ALL * 4,
                     r2t=10240, r3=24576)
        at, region = 0, {}
        for name, size in sizes.items():
            region[name] = at
            at += size
        ctx.enter_context(nc.sbuf_tensor("arena", [128, at + 32], mybir.dt.uint8))

        def place(name, reg, off, shape, dt=f32):
            n = 4
            for s in shape[1:]:
                n *= s
            spans = {"r2": ("r2", "r2t"), "hhi": ("hhi", "hlo")}.get(reg, (reg,))
            assert off + n <= sum(sizes[r] for r in spans), name
            return nc.alloc_sbuf_tensor_at(name, shape, dt, offset=base + region[reg] + off, align_bytes=4)

        def sb(name, shape, dt=f32):
            return ctx.enter_context(nc.sbuf_tensor(name, shape, dt))

        def sem(name):
            return ctx.enter_context(nc.semaphore(name))

        raw = place("raw", "raw", 0, [128, RING, 2, 4, 256])
        w_hi = place("w_hi", "hi", 0, [128, RING, 4, 256], f32r)
        w_lo = place("w_lo", "lo", 0, [128, RING, 4, 256], f32r)
        xt = place("xt", "xt", 0, [128, KT, ALL])
        h_hi = place("h_hi", "hhi", 0, [128, KT, ALL], f32r)
        h_lo = place("h_lo", "hlo", 0, [128, KT, ALL], f32r)
        ada_pre = place("ada_pre", "hhi", 0, [128, 4, D])
        y = place("y", "r1", 0, [128, KT, ALL])
        upad = place("upad", "r1", 0, [128, AT, CONV_K - 1 + SEQ])
        cv = place("cv", "r1", AT * (CONV_K - 1 + SEQ) * 4, [128, AT, SEQ])
        d_hi = place("d_hi", "r1", 0, [128, AT, LIVE], f32r)
        d_lo = place("d_lo", "r1", AT * LIVE * 4, [128, AT, LIVE], f32r)
        siga = place("siga", "r1", 0, [128, KT, LIVE])
        m_hi = place("m_hi", "r1", 0, [128, KT, LIVE], f32r)
        qkv = place("qkv", "r2", 0, [128, 3 * AT, ALL])
        xrow = place("xrow", "r2", 0, [128, 2, D])
        mrow = place("mrow", "r2", 16384, [META, D])
        cwrow = place("cwrow", "r2", 24576, [CONV_K, DA])
        prow = place("prow", "r2", 28672, [128, 7, 128])
        a_hi = place("a_hi", "r2", 0, [128, AT, ALL], f32r)
        a_lo = place("a_lo", "r2", AT * ALL * 4, [128, AT, ALL], f32r)
        y2 = place("y2", "r2", 0, [128, KT, ALL])
        u2 = place("u2", "r2", 3 * AT * ALL * 4, [128, AT, META + ALL])
        m_lo = place("m_lo", "r2", 2 * AT * ALL * 4, [128, KT, LIVE], f32r)
        hid = place("hid", "r2", 0, [128, 4, SEQ])
        sg = place("sg", "r2", 4096, [128, 4, SEQ])
        va = place("va", "r2", 8192, [128, 4, SEQ])
        hid_hi = place("hid_hi", "r2", 12288, [128, 4, SEQ], f32r)
        hid_lo = place("hid_lo", "r2", 16384, [128, 4, SEQ], f32r)
        outrow = place("outrow", "r2", 0, [128, 2, D])
        sigg = place("sigg", "r2t", 0, [128, 2, SEQ])
        cvb = place("cvb", "r2t", 2048, [128, SEQ])
        sil = place("sil", "r2t", 0, [128, 2, SEQ])
        q_s = place("q_s", "r2t", 0, [128, ALL])
        k_s = place("k_s", "r2t", 1088, [128, ALL])
        v_s = place("v_s", "r2t", 2176, [128, ALL])
        sm = place("sm", "r2t", 3264, [128, QSUM])
        v_t = place("v_t", "r2t", 5888, [128, 3, 128])
        p_t = place("p_t", "r2t", 7424, [128, 6 * QT])
        ada_raw = place("ada_raw", "r3", 0, [128, 2, D])
        acc = place("acc", "r3", 16384, [128, D])
        pl_hi = place("pl_hi", "r3", 0, [128, AT, LIVE], f32r)
        pl_lo = place("pl_lo", "r3", AT * LIVE * 4, [128, AT, LIVE], f32r)
        lf = [place(f"lf{n}", "r3", 16512 + n * 2112, [HEADS, 256 + ALL]) for n in range(2)]
        sc_in = place("sc_in", "r3", 16512 + 4224, [HEADS, ALL])
        gp_s = place("gp_s", "r3", 16512, [128, 2, LIVE])
        m1 = place("m1", "r3", 16512 + 2064, [128, 2, LIVE])
        mt = place("mt", "r3", 16512 + 4128, [128, 2, LIVE])
        pcol = sb("pcol", [128, 7, 128])
        cwt = sb("cwt", [128, AT, CONV_K + 1])
        ident = sb("ident", [128, 128])
        ones = sb("ones", [128, 128])
        mask = sb("mask", [128, QSUM])
        sq = sb("sq", [128, 2, ALL])
        rstd = sb("rstd", [128, ALL])
        stat = sb("stat", [128, ALL])
        mod = sb("mod", [128, MODS, KT])
        cact = sb("cact", [128, KT])
        coef = sb("coef", [128, 4, KT])
        sel = sb("sel", [HEADS, QT])
        pick = sb("pick", [HEADS, HEADS])
        win = sb("win", [128, 2, META + ALL])
        bf = sb("bf", [HEADS, 1])
        mx = sb("mx", [128, 3])
        rs = sb("rs", [128, 3])
        bank = ctx.enter_context(nc.psum_tensor("bank", [128, 8, 512], f32))
        B_S, B_N, B_P, B_V = 4, 5, 6, 7

        adab, ccol, pscale = pcol[:, 0, 0:96], pcol[:, 0, 96:112], pcol[:, 0, 112:120]
        g_mix1, g_mixp1, g_ffn1, g_ffnp1 = (pcol[:, 1, 16 * n:16 * n + 16] for n in range(4))
        lng, lnb, cb = (pcol[:, 1, 64 + 8 * n:72 + 8 * n] for n in range(3))
        g_mix2, g_mixp2, g_ffn2, g_ffnp2 = (pcol[:, 2, 16 * n:16 * n + 16] for n in range(4))
        b_qkv, b_u, b_ga, b_gp = (pcol[:, 2, a:b] for a, b in ((64, 88), (88, 96), (96, 112), (112, 128)))
        C_QKV, C_F, C_U = 0, 3 * DA, 3 * DA + HEADS
        C_GA = C_U + DA
        C_GP = C_GA + D

        raw_loaded = [sem(f"raw_loaded{n}") for n in range(2 * RING)]
        hi_ready = sem("hi_ready")
        lo_ready = sem("lo_ready")
        half_used = sem("half_used")
        bank_free = [sem(f"bank_free{n}") for n in range(4)]
        c_loaded, rows_loaded = sem("c_loaded"), sem("rows_loaded")
        consts = sem("consts")
        tr_done = sem("tr_done")
        tr_copied = sem("tr_copied")
        cact_ready = sem("cact_ready")
        pre_loaded = [sem(f"pre_loaded{n}") for n in range(4)]
        pre_used = sem("pre_used")
        ada_loaded = [sem(f"ada_loaded{n}") for n in range(2)]
        ada_used = sem("ada_used")
        acc_zero = sem("acc_zero")
        ada_sum = sem("ada_sum")
        mod_ready = sem("mod_ready")
        coef_ready = sem("coef_ready")
        sq_ready = sem("sq_ready")
        sq_used = sem("sq_used")
        stat_ready = sem("stat_ready")
        var_ready = sem("var_ready")
        rstd_ready = sem("rstd_ready")
        term_ready = sem("term_ready")
        h_hi_ready = sem("h_hi_ready")
        h_ready = sem("h_ready")
        y_scaled = sem("y_scaled")
        x_ready = sem("x_ready")
        y_zero = sem("y_zero")
        conv_step = sem("conv_step")
        mu_sum, cen_ready = sem("mu_sum"), sem("cen_ready")
        ln_term, ln_silu = sem("ln_term"), sem("ln_silu")
        mix_hi, mix_ready = sem("mix_hi"), sem("mix_ready")
        staged = sem("staged")
        s_done = sem("s_done")
        v_done = sem("v_done")
        soft = sem("soft")
        p_masked = sem("p_masked")
        v_copied, p_exp = sem("v_copied"), sem("p_exp")
        p_ready = sem("p_ready")
        pt_done, pt_copied = sem("pt_done"), sem("pt_copied")
        o_done = sem("o_done")
        o_hi, o_lo = sem("o_hi"), sem("o_lo")
        hid_ready = sem("hid_ready")
        hid_hi_ready, hid_lo_ready = sem("hid_hi_ready"), sem("hid_lo_ready")
        tap_ready = sem("tap_ready")
        tap_next = sem("tap_next")
        gelu_ready = sem("gelu_ready")
        f_step = sem("f_step")
        scan = sem("scan")
        pads = sem("pads")
        u_ready = sem("u_ready")
        win_step = sem("win_step")
        d_ready, d_hi_ready, d_lo_ready = sem("d_ready"), sem("d_hi_ready"), sem("d_lo_ready")
        pl_hi_ready, pl_lo_ready = sem("pl_hi_ready"), sem("pl_lo_ready")
        m_part = sem("m_part")
        m_ready, m_hi_ready, m_lo_ready = sem("m_ready"), sem("m_hi_ready"), sem("m_lo_ready")
        last_done, last_copied, stored = sem("last_done"), sem("last_copied"), sem("stored")
        block = ctx.enter_context(nc.Block())

        def fp(ap):
            return ap.bitcast(f32)

        @block.sync
        def _(sp):
            units = Count()

            def half(src):
                slot = units.mod(2 * RING)
                sp.wait_ge(lo_ready, units.at(1, 1))
                sp.dma_start(raw[:, slot // 2, slot % 2], src).then_inc(raw_loaded[slot], 16)
                units.next()

            def k_tiles(w, row, col, rows):
                for r in range(row, row + rows, 512):
                    half(w[r:r + 512, ds(col, 256)].rearrange("(t p) n -> p t n", p=128))

            def down_rows(w, chunk):
                for n in range(8):
                    half(w[ds(chunk, CHUNK), n * 256:n * 256 + 256].rearrange("(t p) n -> p t n", p=128))

            for src, dst in ((ada_b.rearrange("(n p) -> n p", p=128), prow[0:96, 0]),
                             (c.rearrange("(n p) -> n p", p=128), prow[96:112, 0]),
                             (pool_scale_2.rearrange("(n p) -> n p", p=128), prow[112:120, 0])):
                sp.dma_start(dst, src).then_inc(c_loaded, 16)
            pre = Count()
            for part in range(2):
                with loop(sp, 4, (pre, 4)) as i:
                    rows = [sp.snap(i * 512 + n * 128) for n in range(4)]
                    for n in range(4):
                        row = rows[n]
                        slot = pre.mod(4)
                        sp.wait_ge(pre_used, pre.at(1, 1))
                        sp.dma_start(ada_pre[:, slot], ada_w[ds(row, 128), part * D:(part + 1) * D])\
                          .then_inc(pre_loaded[slot], 16)
                        pre.next()
            with loop(sp, 4, (units, 8)) as i:
                a = sp.snap(i * 256 + 3 * DA)
                g = sp.snap(i * 256 + 3 * DA + DA)
                k_tiles(w_in, 0, g, D)
                k_tiles(w_in, 0, a, D)
            with loop(sp, 6, (units, 8)) as i:
                cols = [sp.snap(i * 512 + n * 256) for n in range(2)]
                for col in cols:
                    k_tiles(w_in, 0, col, D)
            for row in (DA, 0):
                with loop(sp, 2, (units, 8)) as i:
                    cols = [sp.snap(i * 1024 + n * 256) for n in range(4)]
                    for col in cols:
                        k_tiles(w_out, row, col, DA)

            def ffn(gate, up, up0, down):
                for n in range(2):
                    k_tiles(gate, 0, n * 256, D)
                for n in range(2):
                    k_tiles(up, 0, up0 + n * 256, D)
                with loop(sp, NCHUNK - 1, (units, 24)) as i:
                    gates = [sp.snap(i * CHUNK + CHUNK + n * 256) for n in range(2)]
                    rows = sp.snap(i * CHUNK)
                    ups = [sp.snap(i * CHUNK + up0 + CHUNK + n * 256) for n in range(2)]
                    for col in gates:
                        k_tiles(gate, 0, col, D)
                    down_rows(down, rows)
                    for col in ups:
                        k_tiles(up, 0, col, D)
                down_rows(down, (NCHUNK - 1) * CHUNK)

            ffn(w_gate, w_up, 0, w_down)
            with loop(sp, 6, (units, 8)) as i:
                cols = [sp.snap(i * 512 + n * 256) for n in range(2)]
                for col in cols:
                    k_tiles(w_in_2, 0, col, D)
            for n in range(2):
                slot = units.mod(2 * RING)
                sp.wait_ge(lo_ready, units.at(1, 1))
                sp.dma_start(raw[:, slot // 2, slot % 2].rearrange("p t n -> p (t n)").rearrange("p (t n) -> p t n", n=128),
                             w_in_2[1024 * n:1024 * n + 1024, C_F:C_F + 128].rearrange("(t p) n -> p t n", p=128))\
                  .then_inc(raw_loaded[slot], 16)
                units.next()
            for j in range(4):
                k_tiles(w_in_2, 0, C_U + j * 256, D)
            k_tiles(pool_w_2.rearrange("g c n -> (g c) n"), 0, 0, DA)
            with loop(sp, 4, (units, 8)) as i:
                cols = [sp.snap(i * 512 + n * 256 + C_GA) for n in range(2)]
                for col in cols:
                    k_tiles(w_in_2, 0, col, D)
            with loop(sp, 4, (units, 16)) as i:
                cols = [sp.snap(i * 512 + n * 256) for n in range(2)]
                gps = [sp.snap((i * 2 + n) * 256 + C_GP) for n in range(2)]
                for n in range(2):
                    k_tiles(w_in_2, 0, gps[n], D)
                    k_tiles(w_attn_o_2, 0, cols[n], DA)
                    k_tiles(w_pool_o_2, 0, cols[n], DA)
            with loop(sp, 4, (units, 8)) as i:
                cols = [sp.snap(i * 512 + n * 256) for n in range(2)]
                for col in cols:
                    k_tiles(w_out_2, 0, col, D)
            ffn(w_ffn_up_2, w_ffn_up_2, F, w_ffn_down_2)
            sp.wait_ge(last_copied, 8)
            sp.dma_start(out.rearrange("(t p) n -> p t n", p=128), outrow[:, :, :]).then_inc(stored, 16)
            sp.wait_ge(stored, 16)

        @block.gpsimd
        def _(gp):
            gp.memset(ident[:, :], 0.0).then_inc(consts, 1)
            gp.memset(ones[:, :], 1.0).then_inc(consts, 1)
            gp.wait_ge(consts, 2)
            gp.affine_select(out=ident[:, :], in_=ident[:, :], compare_op=ALU.not_equal, fill=1.0,
                             base=0, pattern=[[-1, 128]], channel_multiplier=1).then_inc(consts, 1)
            gp.memset(mask[:, :], 0.0).then_inc(consts, 1)
            gp.wait_ge(consts, 4)
            m = mask[:, 0:512].rearrange("p (j k) -> p j k", j=2)
            gp.affine_select(out=m, in_=m, compare_op=ALU.is_ge, fill=NEG, base=0,
                             pattern=[[128, 2], [-1, SEQ]], channel_multiplier=1).then_inc(consts, 1)
            ada, heads = Count(), Count()

            def ada_load(part, kt, slot, lag=2):
                off = gp.snap(kt * 128)
                gp.wait_ge(ada_used, ada.at(1, 3 - lag))
                gp.dma_start(ada_raw[:, slot], ada_w[ds(off, 128), part * D:(part + 1) * D])\
                  .then_inc(ada_loaded[slot], 16)
                ada.next()

            def stage(head, width, cols):
                gp.wait_ge(v_done, heads.next())
                for n, dst in enumerate((q_s, k_s, v_s)):
                    gp.tensor_copy(dst[:, 0:width], qkv[:, ds(head + n * AT), cols].rearrange("p a n -> p (a n)"))\
                      .then_inc(staged, 1)

            with loop(gp, 8, (ada, 2)) as i:
                for n in range(2):
                    ada_load(2, i * 2 + n, n)
            with loop(gp, 4, (ada, 2)) as i:
                for n in range(2):
                    ada_load(3, i * 2 + n, n)
            gp.wait_ge(mix_ready, AT)
            with loop(gp, 2, (ada, 4), (heads, 4)) as i:
                for n in range(4):
                    stage(i * 4 + n, SEQ, SB)
                    ada_load(3, i * 4 + (n + 8), n % 2)
            with loop(gp, 8, (ada, 2)) as i:
                for n in range(2):
                    ada_load(4, i * 2 + n, n)
            gp.wait_ge(h_ready, 2 * KT)
            gp.memset(y[:, :, SB], 0.0).then_inc(y_zero, 1)
            for n in range(6):
                ada_load(5, n, n % 2)
            with loop(gp, NCHUNK - 1, (ada, 1)) as i:
                ada_load(5, i + 6, 0, 1)
            gp.wait_ge(h_ready, 3 * KT)
            gp.memset(mask[:, :], 0.0).then_inc(consts, 1)
            gp.memset(u2[:, :, 0:META], 0.0).then_inc(pads, 1)
            gp.memset(lf[0][:, 0:256], 0.0).then_inc(pads, 1)
            gp.memset(lf[1][:, 0:256], 0.0).then_inc(pads, 1)
            gp.wait_ge(consts, 6)
            for j in range(3):
                m = mask[0:QT, QO[j]:QO[j] + QW[j]]
                gp.affine_select(out=m, in_=m, compare_op=ALU.is_ge, fill=NEG, base=LIVE0 + QT * j,
                                 pattern=[[-1, QW[j]]], channel_multiplier=1).then_inc(consts, 1)
            gp.tensor_scalar(pick[:, :], ident[0:HEADS, 0:HEADS], -1.0 / SCALE, 0.0, ALU.mult, ALU.add)\
              .then_inc(consts, 1)
            gp.wait_ge(consts, 10)
            gp.wait_ge(d_ready, AT)
            with loop(gp, 4, (heads, 2)) as i:
                for n in range(2):
                    stage(i * 2 + n, ALL, slice(0, ALL))
                    gp.tensor_copy(sel[:, :], pick[:, ds(i * 2 + n)].to_broadcast([HEADS, QT])).then_inc(staged, 1)
            gp.wait_ge(h_ready, 4 * KT)
            gp.memset(y[:, :, SB], 0.0).then_inc(y_zero, 1)

        @block.scalar
        def _(act):
            halves, done, groups = Count(), Count(RING), Count()

            def convert():
                if halves.i is None and halves.c >= HALVES:
                    return
                slot, half = halves.mod(2 * RING) // 2, halves.mod(2)
                act.wait_ge(raw_loaded[halves.mod(2 * RING)], halves.div(2 * RING, 16, 16))
                act.wait_ge(half_used, halves.at(1, 1))
                act.activation(w_hi[:, halves.mod(RING)], raw[:, slot, half], ACT.Copy).then_inc(hi_ready, 1)
                halves.next()

            def group(n=4):
                for _ in range(n):
                    convert()
                act.wait_ge(half_used, done.next(n))
                groups.next()
                return 2 * ((groups.mod(2) - 1) % 2)

            def skip(n_halves, n_groups):
                for _ in range(n_halves):
                    convert()
                done.next(n_halves)
                groups.next(n_groups)

            act.dma_start(xrow[:, :, :], x.rearrange("(t p) n -> p t n", p=128)).then_inc(rows_loaded, 16)
            for t, src, r, n in (
                    (1, mix_pre_g, 0, 16), (1, mix_post_g, 16, 16), (1, ffn_pre_g, 32, 16),
                    (1, ffn_post_g, 48, 16), (1, conv_ln_g, 64, 8), (1, conv_ln_b, 72, 8), (1, conv_b, 80, 8),
                    (2, mix_pre_g_2, 0, 16), (2, mix_post_g_2, 16, 16), (2, ffn_pre_g_2, 32, 16),
                    (2, ffn_post_g_2, 48, 16), (2, b_in_2[0:C_F], 64, 24), (2, b_in_2[C_U:C_GA], 88, 8),
                    (2, b_in_2[C_GA:C_GP], 96, 16), (2, b_in_2[C_GP:C_GP + D], 112, 16),
                    (3, ffn_conv_b_2, 0, 2 * FT), (4, ffn_conv_w_2[0], 0, 2 * FT),
                    (5, ffn_conv_w_2[1], 0, 2 * FT), (6, ffn_conv_w_2[2], 0, 2 * FT)):
                act.dma_start(prow[r:r + n, t], src.rearrange("(n p) -> n p", p=128)).then_inc(rows_loaded, 16)
            act.dma_start(mrow[:, :], meta_tokens_2).then_inc(rows_loaded, 16)
            act.dma_start(cwrow[:, :], conv_w).then_inc(rows_loaded, 16)
            act.dma_start(bf[:, :], b_in_2[C_F:C_U].rearrange("(n p) -> n p", p=1)).then_inc(rows_loaded, 16)
            seen = Count()

            def copied(out_ap, in_ap):
                act.wait_ge(tr_done, seen.next())
                act.activation(out_ap, in_ap, ACT.Copy).then_inc(tr_copied, 1)

            def quarters(b, n):
                return bank[:, b, 0:512 if n == 4 else 256].rearrange("p (a b) -> p a b", a=n)

            copied(pcol[:, 0, 0:120], bank[:, B_S, 0:120])
            act.wait_ge(tr_copied, 1)
            act.activation(cact[:, :], ccol, ACT.Silu).then_inc(cact_ready, 1)
            for n in range(8):
                t, j = n // 4, n % 4
                copied(xt[:, 4 * j:4 * j + 4, META + 128 * t:META + 128 * t + 128], quarters(B_S + (1 + n) % 4, 4))
            copied(pcol[:, 1, 0:88], bank[:, B_S + 1, 0:88])
            copied(pcol[:, 2, :], bank[:, B_S + 2, 0:128])
            copied(pcol[:, 3:7, 0:88], quarters(B_S + 3, 4)[:, :, 0:88])
            copied(xt[:, :, 0:META], quarters(B_S, KT))
            copied(cwt[:, :, 0:CONV_K], quarters(B_S + 1, AT)[:, :, 0:CONV_K])
            act.wait_ge(tr_copied, 14)
            sqs, roots, terms = Count(), Count(), Count()

            def squares(src, cols, n=KT, ready=None):
                width = cols.stop - cols.start
                for kt in range(n):
                    if ready is not None:
                        act.wait_ge(ready[0], ready[1].next())
                    if sqs.c >= 2:
                        act.wait_ge(sq_used, sqs.at(1, -1))
                    act.activation(sq[:, kt % 2, 0:width], src[:, kt, cols], ACT.Square).then_inc(sq_ready, 1)
                    sqs.next()

            def root(width):
                act.wait_ge(var_ready, roots.next())
                act.activation(rstd[:, 0:width], stat[:, 0:width], ACT.Sqrt).then_inc(rstd_ready, 1)

            def h_tiles(cols, shift=None):
                for kt in range(KT):
                    act.wait_ge(term_ready, terms.next())
                    if shift is None:
                        act.activation(h_hi[:, kt, cols], y[:, kt, cols], ACT.Copy).then_inc(h_hi_ready, 1)
                    else:
                        act.activation(h_hi[:, kt, cols], y[:, kt, cols], ACT.Identity,
                                       bias=shift[:, kt:kt + 1]).then_inc(h_hi_ready, 1)

            def y_whole():
                for b in range(4):
                    act.wait_ge(bank_free[b], groups.div(2, 1, 1))

            xs, cens = Count(), Count()
            squares(xt, SB)
            for _ in range(LEAD):
                convert()
            root(SEQ)
            act.wait_ge(mod_ready, 2)
            h_tiles(SB, mod[:, 0])
            with loop(act, 4, (halves, 8), (done, 8), (groups, 2)) as i:
                group()
                for o in range(2):
                    act.wait_ge(bank_free[2 + o], i + 1)
                    act.activation(sigg[:, o], bank[:, o, 0:SEQ], ACT.Sigmoid).then_inc(bank_free[o], 1)
                skip(4, 1)
            with loop(act, 6, (halves, 8), (done, 8), (groups, 2)) as i:
                for n in range(2):
                    b = group()
                    for o in range(2):
                        act.activation(qkv[:, ds(i * 4 + (2 * n + o)), SB], bank[:, b + o:b + o + 1, 0:SEQ],
                                       ACT.Copy).then_inc(bank_free[b + o], 1)
            squares(cv, slice(0, SEQ), AT, (cen_ready, cens))
            root(SEQ)
            for t in range(AT):
                act.wait_ge(ln_term, t + 1)
                if t >= 2:
                    act.wait_ge(mix_ready, t - 1)
                act.activation(sil[:, t % 2], cv[:, t, :], ACT.Silu, bias=lnb[:, t:t + 1]).then_inc(ln_silu, 1)
                act.wait_ge(ln_silu, t + 1)
                act.activation(h_hi[:, AT + t, SB], sil[:, t % 2], ACT.Copy).then_inc(mix_hi, 1)
            vs, masked, pts, outs = Count(1), Count(), Count(), Count()

            def exps(tiles, v_parts):
                act.wait_ge(v_done, vs.next())
                for dst, src in v_parts:
                    act.activation(dst, src, ACT.Copy).then_inc(v_copied, 1)
                act.wait_ge(p_masked, masked.next())
                for rows, o, w, j in tiles:
                    act.activation(sm[0:rows, o:o + w], sm[0:rows, o:o + w], ACT.Exp, bias=mx[0:rows, j:j + 1],
                                   accum_out=rs[0:rows, j:j + 1]).then_inc(p_exp, 1)

            def copy_pt(parts):
                act.wait_ge(pt_done, pts.next())
                for dst, src in parts:
                    act.activation(dst, src, ACT.Copy).then_inc(pt_copied, 1)

            def round_out(dst, width):
                act.wait_ge(o_done, outs.next())
                act.activation(dst, bank[:, B_P:B_P + 1, 0:width], ACT.Copy).then_inc(o_hi, 1)

            with loop(act, 2, (halves, 8), (done, 8), (groups, 4), (vs, 4), (masked, 4), (pts, 4), (outs, 4)) as i:
                for n in range(4):
                    convert()
                    exps([(128, 0, SEQ, 0), (128, SEQ, SEQ, 1)], [(v_t[:, 0:2, :], quarters(B_V, 2))])
                    convert()
                    copy_pt([(p_t[:, 0:384], bank[:, B_P, 0:384])])
                    act.wait_ge(half_used, done.next(2))
                    for o in range(2):
                        b = 2 * (n % 2) + o
                        act.activation(y[:, ds(i * 8 + (2 * n + o)), SB], bank[:, b:b + 1, 0:SEQ], ACT.Copy)\
                           .then_inc(bank_free[b], 1)
                    groups.next()
                    round_out(h_hi[:, ds(i * 4 + n), SB], SEQ)
            with loop(act, 2, (halves, 8), (done, 8), (groups, 4)) as i:
                skip(8, 4)
            y_whole()
            squares(y, SB)
            root(SEQ)
            squares(xt, SB, KT, (x_ready, xs))
            root(SEQ)
            act.wait_ge(mod_ready, 5)
            h_tiles(SB, mod[:, 3])
            taps, gelus, hids = Count(), Count(), Count()

            def gate1(i, b, t):
                for o in range(2):
                    act.activation(sg[:, t + o], bank[:, b + o, 0:SEQ], ACT.Silu).then_inc(bank_free[b + o], 1)

            def up1(i, b, t):
                for o in range(2):
                    act.wait_ge(bank_free[b + o], groups_end())
                    act.activation(hid_hi[:, t + o], hid[:, t + o], ACT.Copy).then_inc(hid_hi_ready, 1)

            def groups_end():
                groups.c -= 1
                v = groups.div(2, 1, 2)
                groups.c += 1
                return v

            def tap(dst, i, b, t, first):
                for o in range(2):
                    ch = i * 4 + (t + o + first)
                    act.activation(dst[:, t + o:t + o + 1, :], bank[:, b + o:b + o + 1, 0:SEQ], ACT.Identity,
                                   scale=pcol[:, 4, ds(ch)], bias=pcol[:, 3, ds(ch)]).then_inc(tap_ready, 1)

            def gate2(i, b, t):
                tap(sg, i, b, t, 0)
                for o in range(2):
                    act.wait_ge(bank_free[b + o], groups_end())
                    act.activation(sg[:, t + o], sg[:, t + o], ACT.Gelu_apprx_tanh).then_inc(gelu_ready, 1)

            def up2(i, b, t):
                tap(va, i, b, t, FT)
                for o in range(2):
                    act.wait_ge(hid_ready, hids.next())
                    act.activation(hid_hi[:, t + o], hid[:, t + o], ACT.Copy).then_inc(hid_hi_ready, 1)

            def ffn(gate, up, n_hids):
                def chunk(i, read):
                    for g in range(2):
                        read(i, group(), 2 * g)
                chunk(0, gate)
                chunk(0, up)
                with loop(act, NCHUNK - 1, (halves, 24), (done, 24), (groups, 12), (hids, n_hids)) as i:
                    chunk(i + 1, gate)
                    skip(8, 8)
                    chunk(i + 1, up)
                skip(8, 8)

            ffn(gate1, up1, 0)
            y_whole()
            squares(y, SB)
            root(SEQ)
            squares(xt, slice(0, ALL), KT, (x_ready, xs))
            root(ALL)
            h_tiles(slice(0, ALL))
            with loop(act, 6, (halves, 8), (done, 8), (groups, 2)) as i:
                for n in range(2):
                    b = group()
                    for o in range(2):
                        t = i * 4 + (2 * n + o)
                        act.activation(qkv[:, ds(t), :], bank[:, b + o:b + o + 1, 0:ALL], ACT.Identity,
                                       bias=b_qkv[:, ds(t)]).then_inc(bank_free[b + o], 1)
            convert()
            convert()
            act.wait_ge(half_used, done.next(2))
            act.wait_ge(mod_ready, 6)
            act.activation(lf[1][:, 256:], bank[0:HEADS, B_N, 0:ALL], ACT.Identity, bias=bf[:, :]).then_inc(f_step, 1)
            act.wait_ge(f_step, 1)
            act.activation(sc_in[:, :], lf[1][:, 256:], ACT.Abs).then_inc(f_step, 1)
            act.wait_ge(f_step, 2)
            act.activation(sc_in[:, :], sc_in[:, :], ACT.Exp, scale=-1.0).then_inc(f_step, 1)
            act.wait_ge(f_step, 3)
            act.activation(sc_in[:, :], sc_in[:, :], ACT.Ln, bias=1.0).then_inc(f_step, 1)
            for j in range(4):
                b = group()
                for o in range(2):
                    t = 2 * j + o
                    act.activation(u2[:, t, META:], bank[:, b + o, 0:ALL], ACT.Identity,
                                   bias=b_u[:, t:t + 1]).then_inc(bank_free[b + o], 1)
            for t in range(AT):
                act.wait_ge(d_ready, t + 1)
                act.activation(d_hi[:, t], sq[:, t % 2, 0:LIVE], ACT.Copy).then_inc(d_hi_ready, 1)
            for g in range(4):
                if g % 2 == 0:
                    convert()
                    act.wait_ge(half_used, done.next(1))
                groups.next()
                for o in range(2):
                    t, b = 2 * g + o, 2 * (g % 2) + o
                    act.wait_ge(d_lo_ready if t < 2 else pl_lo_ready, AT if t < 2 else t - 1)
                    act.activation(sq[:, t % 2, 0:LIVE], bank[:, b, 0:LIVE], ACT.Copy, scale=pscale[:, t:t + 1])\
                       .then_inc(bank_free[b], 1)
                    act.wait_ge(bank_free[b], groups_end())
                    act.activation(pl_hi[:, t], sq[:, t % 2, 0:LIVE], ACT.Copy).then_inc(pl_hi_ready, 1)
            with loop(act, 4, (halves, 8), (done, 8), (groups, 2), (vs, 2), (masked, 2), (pts, 2), (outs, 2)) as i:
                for n in range(2):
                    convert()
                    exps([(QT, QO[j], QW[j], j) for j in range(3)],
                         [(v_t[:, 0:2, :], quarters(B_V, 2)), (v_t[0:META, 2, :], bank[0:META, B_V, 256:384])])
                    convert()
                    convert()
                    copy_pt([(p_t[:, 0:5 * QT], bank[:, B_P, 0:5 * QT]),
                             (p_t[0:META, 5 * QT:6 * QT], bank[0:META, B_V, 384:384 + QT])])
                    convert()
                    act.wait_ge(half_used, done.next(4))
                    groups.next()
                    for o in range(2):
                        t, b = i * 4 + (2 * n + o), 2 * n + o
                        act.activation(siga[:, ds(t)], bank[:, b:b + 1, 0:LIVE], ACT.Sigmoid, bias=b_ga[:, ds(t)])\
                           .then_inc(bank_free[b], 1)
                    round_out(a_hi[:, ds(i * 2 + n), 0:LIVE], LIVE)
            ms = Count()
            with loop(act, 4, (halves, 16), (done, 16), (groups, 6), (ms, 4)) as i:
                for n in range(2):
                    b = group()
                    for o in range(2):
                        act.activation(gp_s[:, o:o + 1], bank[:, b + o:b + o + 1, 0:LIVE], ACT.Sigmoid,
                                       bias=b_gp[:, ds(i * 4 + (2 * n + o))]).then_inc(bank_free[b + o], 1)
                    skip(4, 2)
                    for o in range(2):
                        act.wait_ge(m_ready, ms.next())
                        act.activation(m_hi[:, ds(i * 4 + (2 * n + o))], mt[:, o:o + 1], ACT.Copy).then_inc(m_hi_ready, 1)
            with loop(act, 4, (halves, 8), (done, 8), (groups, 2)) as i:
                for n in range(2):
                    b = group()
                    for o in range(2):
                        act.activation(y2[:, ds(i * 4 + (2 * n + o)), ST], bank[:, b + o:b + o + 1, 0:LIVE],
                                       ACT.Copy).then_inc(bank_free[b + o], 1)
            y_whole()
            squares(y2, ST)
            root(LIVE)
            squares(xt, ST, KT, (x_ready, xs))
            root(LIVE)
            h_tiles(ST)
            ffn(gate2, up2, 4)
            y_whole()
            squares(y, SB)
            root(SEQ)
            for n in range(8):
                act.wait_ge(last_done, n + 1)
                act.activation(outrow[:, n // 4, 512 * (n % 4):512 * (n % 4) + 512], bank[:, B_S + n % 4, :], ACT.Copy)\
                   .then_inc(last_copied, 1)

        @block.vector
        def _(dve):
            halves, done, groups = Count(), Count(RING), Count()

            def convert():
                if halves.i is None and halves.c >= HALVES:
                    return
                slot, half = halves.mod(2 * RING) // 2, halves.mod(2)
                dve.wait_ge(hi_ready, halves.at(1, 1))
                dve.tensor_tensor(w_lo[:, halves.mod(RING)], raw[:, slot, half], fp(w_hi[:, halves.mod(RING)]),
                                  ALU.subtract).then_inc(lo_ready, 1)
                halves.next()

            def group(n=4):
                for _ in range(n):
                    convert()
                dve.wait_ge(half_used, done.next(n))
                groups.next()
                return 2 * ((groups.mod(2) - 1) % 2)

            def skip(n_halves, n_groups):
                for _ in range(n_halves):
                    convert()
                done.next(n_halves)
                groups.next(n_groups)

            def groups_end():
                groups.c -= 1
                v = groups.div(2, 1, 2)
                groups.c += 1
                return v

            dve.memset(mx[:, :], 0.0).then_inc(lo_ready, 2 * RING)
            dve.memset(rs[:, :], 0.0).then_inc(half_used, RING)
            dve.memset(stat[:, 0:1], 0.0).then_inc(bank_free[0], 1)
            dve.memset(stat[:, 1:2], 0.0).then_inc(bank_free[1], 1)
            dve.memset(stat[:, 2:3], 0.0).then_inc(bank_free[2], 1)
            dve.memset(stat[:, 3:4], 0.0).then_inc(bank_free[3], 1)
            dve.memset(stat[:, 4:5], 0.0).then_inc(pre_used, 4)
            dve.memset(stat[:, 5:6], 0.0).then_inc(ada_used, 2)
            dve.memset(stat[:, 6:7], 0.0).then_inc(v_done, 1)
            pre, ada = Count(), Count()
            slot_loads = [Count(), Count()]
            zeros = Count()

            def clear_acc():
                dve.memset(acc[:, :], 0.0).then_inc(acc_zero, 1)
                dve.wait_ge(acc_zero, zeros.next())

            def finish(part):
                dve.wait_ge(ada_sum, part + 1)
                dve.tensor_tensor(mod[:, part], bank[:, B_N, 496:512], adab[:, KT * part:KT * part + KT], ALU.add)\
                   .then_inc(mod_ready, 1)

            def ada_step(kt, slot):
                dve.wait_ge(ada_loaded[slot], slot_loads[slot].next(1, 16))
                dve.wait_ge(ada_used, ada.at(1, 2))
                dve.scalar_tensor_tensor(out=acc[:, :], in0=ada_raw[:, slot], scalar=cact[:, ds(kt)], in1=acc[:, :],
                                         op0=ALU.mult, op1=ALU.add).then_inc(ada_used, 1)
                ada.next()

            dve.wait_ge(cact_ready, 1)
            for part in range(2):
                clear_acc()
                with loop(dve, 4, (pre, 4)) as i:
                    for n in range(4):
                        dve.wait_ge(pre_loaded[n], pre.div(4, 16, 16))
                        dve.wait_ge(pre_used, pre.at(1, 4))
                        dve.scalar_tensor_tensor(out=acc[:, :], in0=ada_pre[:, n], scalar=cact[:, ds(i * 4 + n)],
                                                 in1=acc[:, :], op0=ALU.mult, op1=ALU.add).then_inc(pre_used, 1)
                        pre.next()
                finish(part)
            clear_acc()
            for _ in range(LEAD):
                convert()
            dve.wait_ge(mod_ready, 2)
            dve.scalar_tensor_tensor(out=coef[:, 0], in0=mod[:, 1], scalar=1.0, in1=g_mix1,
                                     op0=ALU.add, op1=ALU.mult).then_inc(coef_ready, 1)
            dve.wait_ge(coef_ready, 1)
            sums, stats, roots, terms, hs, ys, xs = (Count() for _ in range(7))

            def inverse(width, n, eps):
                dve.wait_ge(sq_used, sums.next(n // 128))
                dve.tensor_scalar(stat[:, 0:width], bank[:, B_N, 0:width], 1.0 / n, eps, ALU.mult, ALU.add)\
                   .then_inc(stat_ready, 1)
                dve.wait_ge(stat_ready, stats.next())
                dve.reciprocal(stat[:, 0:width], stat[:, 0:width]).then_inc(var_ready, 1)
                dve.wait_ge(rstd_ready, roots.next())

            def h_tiles(cols, scale, shift=None):
                width = cols.stop - cols.start
                for kt in range(KT):
                    dve.scalar_tensor_tensor(out=y[:, kt, cols], in0=xt[:, kt, cols], scalar=scale[:, kt:kt + 1],
                                             in1=rstd[:, 0:width], op0=ALU.mult, op1=ALU.mult).then_inc(term_ready, 1)
                for kt in range(KT):
                    dve.wait_ge(h_hi_ready, hs.next())
                    if shift is None:
                        dve.tensor_tensor(h_lo[:, kt, cols], y[:, kt, cols], fp(h_hi[:, kt, cols]), ALU.subtract)\
                           .then_inc(h_ready, 1)
                    else:
                        dve.scalar_tensor_tensor(out=h_lo[:, kt, cols], in0=y[:, kt, cols], scalar=shift[:, kt:kt + 1],
                                                 in1=fp(h_hi[:, kt, cols]), op0=ALU.add, op1=ALU.subtract)\
                           .then_inc(h_ready, 1)

            def residual(src, cols, scale):
                width = cols.stop - cols.start

                def add(kt):
                    dve.wait_ge(y_scaled, ys.at(1, kt + 1))
                    dve.tensor_tensor(xt[:, kt, cols], xt[:, kt, cols], src[:, kt, cols], ALU.add).then_inc(x_ready, 1)

                for kt in range(KT):
                    dve.scalar_tensor_tensor(out=src[:, kt, cols], in0=src[:, kt, cols], scalar=scale[:, kt:kt + 1],
                                             in1=rstd[:, 0:width], op0=ALU.mult, op1=ALU.mult).then_inc(y_scaled, 1)
                    if kt:
                        add(kt - 1)
                add(KT - 1)
                ys.next(KT)
                dve.wait_ge(x_ready, xs.next(KT))

            inverse(SEQ, D, 1e-6)
            h_tiles(SB, coef[:, 0], mod[:, 0])
            dve.wait_ge(h_ready, KT)
            dve.memset(upad[:, :, 0:CONV_K - 1], 0.0).then_inc(conv_step, 1)
            with loop(dve, 4, (halves, 8), (done, 8), (groups, 2), (ada, 4),
                      (slot_loads[0], 2), (slot_loads[1], 2)) as i:
                for n in range(4):
                    convert()
                    convert()
                    ada_step(i * 4 + n, n % 2)
                dve.wait_ge(half_used, done.next(8))
                groups.next(2)
                for o in range(2):
                    dve.wait_ge(bank_free[o], i + 2)
                    dve.tensor_tensor(upad[:, ds(i * 2 + o), CONV_K - 1:], bank[:, 2 + o:3 + o, 0:SEQ],
                                      sigg[:, o:o + 1], ALU.mult).then_inc(bank_free[2 + o], 1)
            finish(2)
            clear_acc()
            steps = Count(1)

            def conv_tile(t):
                def u(j):
                    return upad[:, ds(t), j:j + SEQ]

                w = lambda j: cwt[:, ds(t), j]
                dst = (cv[:, ds(t), :], cvb[:, :].rearrange("p (a n) -> p a n", a=1))
                dve.wait_ge(conv_step, steps.at())
                dve.tensor_scalar(dst[0], u(0), w(0), cb[:, ds(t)], ALU.mult, ALU.add).then_inc(conv_step, 1)
                dve.tensor_scalar(dst[1], u(1), w(1), None, ALU.mult).then_inc(conv_step, 1)
                steps.next(2)
                for j in range(2, CONV_K):
                    dve.wait_ge(conv_step, steps.at(1, -1))
                    dve.scalar_tensor_tensor(out=dst[j % 2], in0=u(j), scalar=w(j), in1=dst[j % 2],
                                             op0=ALU.mult, op1=ALU.add).then_inc(conv_step, 1)
                    steps.next()
                dve.wait_ge(conv_step, steps.at())
                dve.tensor_tensor(dst[0], dst[0], dst[1], ALU.add).then_inc(conv_step, 1)
                steps.next()

            with loop(dve, 4, (halves, 8), (done, 8), (groups, 2), (ada, 2), (steps, CONV_K + 1),
                      (slot_loads[0], 1), (slot_loads[1], 1)) as i:
                for n in range(2):
                    skip(4, 1)
                    ada_step(i * 2 + n, n)
                conv_tile(i)
            with loop(dve, 2, (halves, 8), (done, 8), (groups, 2), (steps, 2 * (CONV_K + 1))) as i:
                for n in range(2):
                    skip(4, 1)
                    conv_tile(i * 2 + (4 + n))
            dve.wait_ge(mu_sum, 1)
            dve.tensor_scalar(stat[:, 0:SEQ], bank[:, B_N, 0:SEQ], 1.0 / DA, None, ALU.mult).then_inc(stat_ready, 1)
            dve.wait_ge(stat_ready, stats.next())
            for t in range(AT):
                dve.tensor_tensor(cv[:, t, :], cv[:, t, :], stat[:, 0:SEQ], ALU.subtract).then_inc(cen_ready, 1)
            inverse(SEQ, DA, 1e-5)
            for t in range(AT):
                dve.scalar_tensor_tensor(out=cv[:, t, :], in0=cv[:, t, :], scalar=lng[:, t:t + 1], in1=rstd[:, 0:SEQ],
                                         op0=ALU.mult, op1=ALU.mult).then_inc(ln_term, 1)
            for t in range(AT):
                dve.wait_ge(mix_hi, t + 1)
                dve.tensor_tensor(h_lo[:, AT + t, SB], sil[:, t % 2], fp(h_hi[:, AT + t, SB]), ALU.subtract)\
                   .then_inc(mix_ready, 1)
            scored, soft_n, exped, outs, masked, probs = (Count() for _ in range(6))

            def softmax_max(parts, tiles, rows):
                dve.wait_ge(s_done, scored.next())
                for o, w, src in parts:
                    dve.scalar_tensor_tensor(out=sm[0:rows, o:o + w], in0=src, scalar=SCALE, in1=mask[0:rows, o:o + w],
                                             op0=ALU.mult, op1=ALU.add).then_inc(soft, 1)
                dve.wait_ge(soft, soft_n.next(len(parts)))
                for o, w, j in tiles:
                    dve.reduce_max(mx[0:rows, j:j + 1], sm[0:rows, o:o + w], AX.X).then_inc(soft, 1)
                dve.wait_ge(soft, soft_n.next(len(tiles)))
                n = len(tiles)
                dve.tensor_scalar(mx[0:rows, 0:n], mx[0:rows, 0:n], -1.0, None, ALU.mult).then_inc(p_masked, 1)

            def softmax_norm(tiles, rows):
                n = len(tiles)
                dve.wait_ge(p_exp, exped.next(n))
                dve.reciprocal(rs[0:rows, 0:n], rs[0:rows, 0:n]).then_inc(soft, 1)
                dve.wait_ge(soft, soft_n.next())
                for o, w, j in tiles:
                    dve.tensor_scalar(sm[0:rows, o:o + w], sm[0:rows, o:o + w], rs[0:rows, j:j + 1], None, ALU.mult)\
                       .then_inc(p_ready, 1)

            def out_rest(lo_ap, hi_ap, width):
                dve.wait_ge(o_hi, outs.next())
                dve.tensor_tensor(lo_ap, bank[:, B_P:B_P + 1, 0:width], fp(hi_ap), ALU.subtract).then_inc(o_lo, 1)

            t1 = [(0, SEQ, 0), (SEQ, SEQ, 1)]
            with loop(dve, 2, (halves, 8), (done, 8), (groups, 4), (ada, 4), (slot_loads[0], 2), (slot_loads[1], 2),
                      (scored, 4), (soft_n, 4 * 4), (exped, 8), (outs, 4)) as i:
                for n in range(4):
                    convert()
                    softmax_max([(0, 512, bank[:, B_S, :])], t1, 128)
                    softmax_norm(t1, 128)
                    convert()
                    ada_step(i * 4 + (n + 8), n % 2)
                    out_rest(h_lo[:, ds(i * 4 + n), SB], h_hi[:, ds(i * 4 + n), SB], SEQ)
                done.next(8)
                groups.next(4)
            finish(3)
            clear_acc()
            with loop(dve, 2, (halves, 8), (done, 8), (groups, 4), (ada, 8), (slot_loads[0], 4), (slot_loads[1], 4)) as i:
                for n in range(4):
                    b = group(2)
                    for o in range(2):
                        t = i * 8 + (2 * n + o)
                        dve.tensor_tensor(y[:, ds(t), SB], y[:, ds(t), SB], bank[:, b + o:b + o + 1, 0:SEQ], ALU.add)\
                           .then_inc(bank_free[b + o], 1)
                    for s in range(2):
                        ada_step(i * 8 + (2 * n + s), s)
            finish(4)
            clear_acc()
            dve.wait_ge(mod_ready, 5)
            dve.tensor_tensor(coef[:, 1], mod[:, 2], g_mixp1, ALU.mult).then_inc(coef_ready, 1)
            dve.scalar_tensor_tensor(out=coef[:, 2], in0=mod[:, 4], scalar=1.0, in1=g_ffn1,
                                     op0=ALU.add, op1=ALU.mult).then_inc(coef_ready, 1)
            dve.wait_ge(coef_ready, 3)
            inverse(SEQ, D, 1e-6)
            residual(y, SB, coef[:, 1])
            inverse(SEQ, D, 1e-6)
            h_tiles(SB, coef[:, 2], mod[:, 3])
            hids, taps, nexts, gelus = (Count() for _ in range(4))

            def rest(t):
                for o in range(2):
                    dve.wait_ge(hid_hi_ready, hids.next())
                    dve.tensor_tensor(hid_lo[:, t + o], hid[:, t + o], fp(hid_hi[:, t + o]), ALU.subtract)\
                       .then_inc(hid_lo_ready, 1)

            def down(i):
                for j in range(8):
                    b = group(1)
                    for o in range(2):
                        dve.tensor_tensor(y[:, 2 * j + o, SB], y[:, 2 * j + o, SB], bank[:, b + o, 0:SEQ], ALU.add)\
                           .then_inc(bank_free[b + o], 1)

            def gate1(i, t):
                skip(4, 1)

            def up1(i, t):
                b = group()
                for o in range(2):
                    dve.wait_ge(bank_free[b + o], sg_free(b))
                    dve.tensor_tensor(hid[:, t + o], bank[:, b + o, 0:SEQ], sg[:, t + o], ALU.mult)\
                       .then_inc(bank_free[b + o], 1)
                rest(t)

            def sg_free(b):
                groups.c -= 1
                v = groups.div(2, 1, 1)
                groups.c += 1
                return v

            def more_taps(dst, i, b, t, first, last_sem):
                for k in (1, 2):
                    for o in range(2):
                        if k == 1:
                            dve.wait_ge(tap_ready, taps.next())
                        else:
                            dve.wait_ge(tap_next, nexts.at(1, o + 1))
                        ch = i * 4 + (t + o + first)
                        dve.scalar_tensor_tensor(out=dst[:, t + o:t + o + 1, :], in0=bank[:, b + o:b + o + 1, k:k + SEQ],
                                                 scalar=pcol[:, 4 + k, ds(ch)], in1=dst[:, t + o:t + o + 1, :],
                                                 op0=ALU.mult, op1=ALU.add)\
                           .then_inc(tap_next if k == 1 else bank_free[b + o], 1)
                nexts.next(2)

            def gate2(i, t):
                more_taps(sg, i, group(), t, 0, None)

            def up2(i, t):
                b = group()
                more_taps(va, i, b, t, FT, None)
                for o in range(2):
                    dve.wait_ge(bank_free[b + o], groups_end())
                    dve.wait_ge(gelu_ready, gelus.next())
                    dve.tensor_tensor(hid[:, t + o], va[:, t + o], sg[:, t + o], ALU.mult).then_inc(hid_ready, 1)
                rest(t)

            def ffn(gate, up, n_taps, with_ada):
                def chunk(i, read):
                    for g in range(2):
                        read(i, 2 * g)
                chunk(0, gate)
                if with_ada:
                    for n in range(6):
                        ada_step(n, n % 2)
                chunk(0, up)
                with loop(dve, NCHUNK - 1, (halves, 24), (done, 24), (groups, 12), (hids, 4), (taps, 2 * n_taps),
                          (nexts, 2 * n_taps), (gelus, n_taps), (ada, with_ada), (slot_loads[0], with_ada)) as i:
                    chunk(i + 1, gate)
                    down(i)
                    chunk(i + 1, up)
                    if with_ada:
                        ada_step(i + 6, 0)
                if with_ada:
                    finish(5)
                    dve.wait_ge(mod_ready, 6)
                    dve.tensor_tensor(coef[:, 3], mod[:, 5], g_ffnp1, ALU.mult).then_inc(coef_ready, 1)
                    dve.wait_ge(coef_ready, 4)
                down(0)

            dve.wait_ge(y_zero, 1)
            ffn(gate1, up1, 0, 1)
            inverse(SEQ, D, 1e-6)
            residual(y, SB, coef[:, 3])
            inverse(ALL, D, 1e-6)
            h_tiles(slice(0, ALL), g_mix2)
            with loop(dve, 6, (halves, 8), (done, 8), (groups, 2)) as i:
                skip(8, 2)
            skip(2, 0)
            dve.wait_ge(f_step, 4)
            dve.wait_ge(pads, 3)
            dve.scalar_tensor_tensor(out=lf[0][:, 256:], in0=lf[1][:, 256:], scalar=0.0, in1=sc_in[:, :],
                                     op0=ALU.min, op1=ALU.subtract).then_inc(scan, 1)
            for n in range(9):
                dve.wait_ge(scan, n + 1)
                a, b, s = lf[n % 2], lf[(n + 1) % 2], 1 << n
                dve.tensor_tensor(b[:, 256:], a[:, 256:], a[:, 256 - s:256 + ALL - s], ALU.add).then_inc(scan, 1)
            skip(16, 4)
            n_win = 0
            for t in range(AT):
                w = WINDOWS[t // 2]
                last, s = u2[:, t, :], 1
                dve.wait_ge(bank_free[t % 4], 1 + (U_GROUP + t // 2) // 2 + 1)
                k = 0
                while s < w:
                    dst = win[:, k % 2, :]
                    if n_win:
                        dve.wait_ge(win_step, n_win)
                    lo = 2 * s - 1
                    dve.tensor_tensor(dst[:, lo:], last[:, lo:], last[:, lo - s:META + ALL - s], ALU.add)\
                       .then_inc(win_step, 1)
                    n_win += 1
                    last, s, k = dst, 2 * s, k + 1
                dve.wait_ge(win_step, n_win)
                if t >= 2:
                    dve.wait_ge(d_lo_ready, t - 1)
                full = slice(META + LIVE0, META + ALL)
                args = dict(op0=ALU.mult, op1=ALU.subtract)
                if LIVE0 + 1 < w:
                    dve.scalar_tensor_tensor(out=sq[:, t % 2, 0:1], in0=last[:, full.start:full.start + 1],
                                             scalar=1.0 / (LIVE0 + 1), in1=u2[:, t, full.start:full.start + 1], **args)\
                       .then_inc(win_step, 1)
                    n_win += 1
                    dve.scalar_tensor_tensor(out=sq[:, t % 2, 1:LIVE], in0=last[:, full.start + 1:full.stop],
                                             scalar=1.0 / w, in1=u2[:, t, full.start + 1:full.stop], **args)\
                       .then_inc(d_ready, 1)
                else:
                    dve.scalar_tensor_tensor(out=sq[:, t % 2, 0:LIVE], in0=last[:, full], scalar=1.0 / w,
                                             in1=u2[:, t, full], **args).then_inc(d_ready, 1)
                dve.wait_ge(d_hi_ready, t + 1)
                dve.tensor_tensor(d_lo[:, t], sq[:, t % 2, 0:LIVE], fp(d_hi[:, t]), ALU.subtract).then_inc(d_lo_ready, 1)
            for t in range(AT):
                if t % 4 == 0:
                    skip(1, 2)
                dve.wait_ge(pl_hi_ready, t + 1)
                dve.tensor_tensor(pl_lo[:, t], sq[:, t % 2, 0:LIVE], fp(pl_hi[:, t]), ALU.subtract).then_inc(pl_lo_ready, 1)
            t2 = [(QO[j], QW[j], j) for j in range(3)]
            dve.wait_ge(consts, 9)
            with loop(dve, 4, (halves, 8), (done, 8), (groups, 2), (scored, 2), (soft_n, 12), (exped, 6), (outs, 2)) as i:
                for n in range(2):
                    convert()
                    softmax_max([(0, 384, bank[0:QT, B_S, 0:384]), (384, 272, bank[0:QT, B_N, 0:272])], t2, QT)
                    softmax_norm(t2, QT)
                    convert()
                    convert()
                    convert()
                    out_rest(a_lo[:, ds(i * 2 + n), 0:LIVE], a_hi[:, ds(i * 2 + n), 0:LIVE], LIVE)
                done.next(8)
                groups.next(2)
            ms, parts = Count(), Count()
            with loop(dve, 4, (halves, 16), (done, 16), (groups, 6), (ms, 4), (parts, 4)) as i:
                for n in range(2):
                    skip(4, 1)
                    gate_free = groups_end()
                    gb = 2 * ((groups.mod(2) - 1) % 2)
                    b = group(2)
                    for o in range(2):
                        dve.tensor_tensor(m1[:, o:o + 1], bank[:, b + o:b + o + 1, 0:LIVE],
                                          siga[:, ds(i * 4 + (2 * n + o))], ALU.mult).then_inc(bank_free[b + o], 1)
                    b = group(2)
                    for o in range(2):
                        dve.wait_ge(bank_free[gb + o], gate_free)
                        dve.tensor_tensor(mt[:, o:o + 1], bank[:, b + o:b + o + 1, 0:LIVE], gp_s[:, o:o + 1], ALU.mult)\
                           .then_inc(bank_free[b + o], 1)
                    for o in range(2):
                        dve.wait_ge(bank_free[b + o], groups_end())
                        dve.tensor_tensor(mt[:, o:o + 1], mt[:, o:o + 1], m1[:, o:o + 1], ALU.add).then_inc(m_ready, 1)
                    for o in range(2):
                        dve.wait_ge(m_hi_ready, ms.next())
                        t = ds(i * 4 + (2 * n + o))
                        dve.tensor_tensor(m_lo[:, t], mt[:, o:o + 1], fp(m_hi[:, t]), ALU.subtract).then_inc(m_lo_ready, 1)
                parts.next(4)
            with loop(dve, 4, (halves, 8), (done, 8), (groups, 2)) as i:
                skip(8, 2)
            inverse(LIVE, D, 1e-6)
            residual(y2, ST, g_mixp2)
            inverse(LIVE, D, 1e-6)
            h_tiles(ST, g_ffn2)
            dve.wait_ge(y_zero, 2)
            ffn(gate2, up2, 4, 0)
            inverse(SEQ, D, 1e-6)
            residual(y, SB, g_ffnp2)

        @block.tensor
        def _(pe):
            halves, groups = Count(), Count()

            def half(x_hi, x_lo, kts, width, first, last, nk=4, tiles=2, sub=None, out_bank=None, free=True):
                slot = halves.mod(RING)
                b = 2 * groups.mod(2) if out_bank is None else out_bank
                pe.wait_ge(lo_ready, halves.at(1, 2 * RING + 1))
                if first and out_bank is None:
                    for o in range(2):
                        pe.wait_ge(bank_free[b + o], groups.div(2, 1, 1))
                for k, kt in enumerate(kts):
                    for o in range(tiles):
                        cut = (slice(k, k + 1), slice(o * 128, o * 128 + 128))
                        if tiles == 1:
                            cut = (slice(k // 2, k // 2 + 1), slice(k % 2 * 128, k % 2 * 128 + 128))
                        wh = w_hi[:, slot, cut[0], cut[1]].rearrange("p a n -> p (a n)")
                        wl = w_lo[:, slot, cut[0], cut[1]].rearrange("p a n -> p (a n)")
                        dst = bank[:, b + o, 0:width]
                        pe.matmul(dst, wh, x_hi(kt), start=first and k == 0, stop=False)
                        pe.matmul(dst, wh, x_lo(kt), start=False, stop=False)
                        mm = pe.matmul(dst, wl, x_hi(kt), start=False, stop=last and k == len(kts) - 1)
                mm.then_inc(half_used, 1)
                halves.next()
                if last and out_bank is None:
                    groups.next()

            def product(x_hi, x_lo, cols, n_kt=KT, kt0=0, ready=None):
                width = cols.stop - cols.start
                for q in range(n_kt // 4):
                    if ready is not None:
                        pe.wait_ge(ready[0], ready[1] + 4 * q + 4)
                    kts = range(kt0 + 4 * q, kt0 + 4 * q + 4)
                    half(lambda kt: x_hi[:, kt, cols], lambda kt: x_lo[:, kt, cols], kts, width,
                         q == 0, q == n_kt // 4 - 1)

            used = Count()

            def turn(pairs):
                n = used.c
                if n >= 4:
                    pe.wait_ge(tr_copied, n - 3)
                for dst, src in pairs:
                    rows = src.shape[0]
                    mm = pe.transpose(dst(bank[:, B_S + n % 4, :]), src, ident[0:rows, 0:rows])
                mm.then_inc(tr_done, 1)
                used.next()

            pe.wait_ge(consts, 3)
            pe.wait_ge(c_loaded, 48)
            turn([(lambda b: b[:, 0:120], prow[0:120, 0])])
            pe.wait_ge(rows_loaded, 16 * 23)
            for n in range(8):
                t, j = n // 4, n % 4
                turn([(lambda b, a=a: b[:, 128 * a:128 * a + 128], xrow[:, t, 512 * j + 128 * a:512 * j + 128 * a + 128])
                      for a in range(4)])
            turn([(lambda b: b[:, 0:88], prow[0:88, 1])])
            turn([(lambda b: b[:, 0:128], prow[:, 2])])
            turn([(lambda b, a=a: b[:, 128 * a:128 * a + 88], prow[0:88, 3 + a]) for a in range(4)])
            turn([(lambda b, a=a: b[:, META * a:META * a + META], mrow[:, 128 * a:128 * a + 128]) for a in range(KT)])
            turn([(lambda b, a=a: b[:, 32 * a:32 * a + CONV_K], cwrow[:, 128 * a:128 * a + 128]) for a in range(AT)])
            sqs = Count()

            def channel_sums(width, n=KT):
                for kt in range(n):
                    pe.wait_ge(sq_ready, sqs.next())
                    pe.matmul(bank[:, B_N, 0:width], ones[:, :], sq[:, kt % 2, 0:width],
                              start=kt == 0, stop=kt == n - 1).then_inc(sq_used, 1)

            def ada_total(part):
                for j in range(KT):
                    mm = pe.matmul(bank[:, B_N, 496 + j:497 + j], acc[:, 128 * j:128 * j + 128], ones[:, 0:1],
                                   start=True, stop=True)
                mm.then_inc(ada_sum, 1)

            pe.wait_ge(tr_copied, 14)
            channel_sums(SEQ)
            for part in range(2):
                pe.wait_ge(pre_used, 4 + 16 * (part + 1))
                ada_total(part)
            with loop(pe, 4, (halves, 8), (groups, 2)):
                for n in range(2):
                    product(h_hi, h_lo, SB, ready=(h_ready, 0))
            pe.wait_ge(ada_used, 2 + 16)
            ada_total(2)
            with loop(pe, 6, (halves, 8), (groups, 2)):
                for n in range(2):
                    product(h_hi, h_lo, SB)
            pe.wait_ge(conv_step, 1 + AT * (CONV_K + 1))
            pe.wait_ge(mod_ready, 3)
            for t in range(AT):
                mm = pe.matmul(bank[:, B_N, 0:SEQ], ones[:, :], cv[:, t, :], start=t == 0, stop=t == AT - 1)
            mm.then_inc(mu_sum, 1)
            channel_sums(SEQ, AT)
            staged_n, copied_n, probs_n, ptc, heads = Count(), Count(), Count(), Count(), Count()

            def scores(per_head, tiles, v_parts):
                pe.wait_ge(staged, staged_n.next(per_head))
                for n, mats in enumerate(tiles):
                    for m, (dst, lhs, rhs) in enumerate(mats):
                        mm = pe.matmul(dst, lhs, rhs, start=m == 0, stop=m == len(mats) - 1)
                mm.then_inc(s_done, 1)
                for dst, src in v_parts:
                    mm = pe.transpose(dst, src, ident[:, :])
                mm.then_inc(v_done, 1)

            def turn_p(n_tiles, parts):
                pe.wait_ge(p_ready, probs_n.next(n_tiles))
                for dst, src in parts:
                    rows = src.shape[0]
                    mm = pe.transpose(dst, src, ident[0:rows, 0:rows])
                mm.then_inc(pt_done, 1)

            def weigh(n_pt, n_v, parts):
                pe.wait_ge(pt_copied, ptc.next(n_pt))
                pe.wait_ge(v_copied, copied_n.next(n_v))
                for m, (dst, v, p) in enumerate(parts):
                    mm = pe.matmul(dst, v, p, start=m == 0, stop=m == len(parts) - 1)
                mm.then_inc(o_done, 1)

            B = lambda b, lo, hi, rows=128: bank[0:rows, b, lo:hi]
            pe.wait_ge(mix_ready, AT)
            with loop(pe, 2, (halves, 8), (groups, 4), (staged_n, 12), (copied_n, 4), (probs_n, 8), (ptc, 4), (heads, 4)) as i:
                for n in range(4):
                    scores(3, [[(B(B_S, 256 * j, 256 * j + 256), q_s[:, 128 * j:128 * j + 128], k_s[:, 0:SEQ])]
                               for j in range(2)],
                           [(B(B_V, 128 * t, 128 * t + 128), v_s[:, 128 * t:128 * t + 128]) for t in range(2)])
                    for q in range(2):
                        kts = range(AT + 4 * q, AT + 4 * q + 4)
                        half(lambda kt: h_hi[:, kt, SB], lambda kt: h_lo[:, kt, SB], kts, SEQ, q == 0, q == 1)
                        if q == 0:
                            turn_p(2, [(B(B_P, 0, 128), sm[:, 0:128]), (B(B_P, 128, 256), sm[:, 256:384]),
                                       (B(B_P, 256, 384), sm[:, 384:512])])
                    weigh(1, 1, [(B(B_P, 0, 256), v_t[:, 0, :], p_t[:, 0:256]),
                                 (B(B_P, 128, 256), v_t[:, 1, :], p_t[:, 256:384])])
                    heads.next()
            pe.wait_ge(ada_used, 2 + 32)
            ada_total(3)
            pe.wait_ge(o_lo, HEADS)
            with loop(pe, 2, (halves, 8), (groups, 4)) as i:
                for n in range(4):
                    product(h_hi, h_lo, SB, AT)
            pe.wait_ge(ada_used, 2 + 48)
            pe.wait_ge(mod_ready, 4)
            ada_total(4)
            pe.wait_ge(mod_ready, 5)
            channel_sums(SEQ)
            channel_sums(SEQ)
            downs = Count()

            def ffn(cols, h_base, with_ada):
                def chunk(ready=None):
                    for g in range(2):
                        product(h_hi, h_lo, cols, ready=ready)

                def down():
                    pe.wait_ge(hid_lo_ready, downs.next(4))
                    for j in range(8):
                        half(lambda kt: hid_hi[:, kt], lambda kt: hid_lo[:, kt], range(4), SEQ, True, True)

                chunk((h_ready, h_base))
                chunk()
                with loop(pe, NCHUNK - 1, (halves, 24), (groups, 12), (downs, 4)):
                    chunk()
                    down()
                    chunk()
                if with_ada:
                    pe.wait_ge(ada_used, 2 + 64)
                    ada_total(5)
                down()

            ffn(SB, KT, True)
            pe.wait_ge(mod_ready, 6)
            channel_sums(SEQ)
            every = slice(0, ALL)
            channel_sums(ALL)
            with loop(pe, 6, (halves, 8), (groups, 2)):
                for n in range(2):
                    product(h_hi, h_lo, every, ready=(h_ready, 2 * KT))
            for q in range(2):
                half(lambda kt: h_hi[:, kt, :], lambda kt: h_lo[:, kt, :], range(8 * q, 8 * q + 8), ALL,
                     q == 0, q == 1, tiles=1, out_bank=B_N)
            for j in range(4):
                product(h_hi, h_lo, every)
            for h in range(2):
                slot = halves.mod(RING)
                pe.wait_ge(lo_ready, halves.at(1, 2 * RING + 1))
                pe.wait_ge(d_lo_ready, 4 * h + 4)
                for g in range(2):
                    b = 2 * groups.mod(2)
                    for o in range(2):
                        pe.wait_ge(bank_free[b + o], groups.div(2, 1, 1))
                        for k in range(2):
                            wh = w_hi[:, slot, 2 * g + k, o * 128:o * 128 + 128]
                            wl = w_lo[:, slot, 2 * g + k, o * 128:o * 128 + 128]
                            t = 4 * h + 2 * g + k
                            dst = bank[:, b + o, 0:LIVE]
                            pe.matmul(dst, wh, d_hi[:, t], start=k == 0, stop=False)
                            pe.matmul(dst, wh, d_lo[:, t], start=False, stop=False)
                            mm = pe.matmul(dst, wl, d_hi[:, t], start=False, stop=k == 1)
                    groups.next()
                mm.then_inc(half_used, 1)
                halves.next()
            pe.wait_ge(scan, 10)
            csum = lf[1]
            with loop(pe, 4, (halves, 8), (groups, 2), (staged_n, 8), (copied_n, 4), (probs_n, 6), (ptc, 4)) as i:
                for n in range(2):
                    dst = (B(B_S, 0, 128, QT), B(B_S, 128, 384, QT), B(B_N, 0, 272, QT))
                    scores(4, [[(dst[j], q_s[:, LIVE0 + QT * j:LIVE0 + QT * j + QT], k_s[:, 0:QW[j]]),
                                (dst[j], sel[:, :], csum[:, 256:256 + QW[j]])] for j in range(3)],
                           [(B(B_V, 128 * t, 128 * t + 128, min(128, ALL - 128 * t)),
                             v_s[:, 128 * t:min(128 * t + 128, ALL)]) for t in range(3)])
                    for q in range(4):
                        kts = range(4 * q, 4 * q + 4)
                        half(lambda kt: h_hi[:, kt, ST], lambda kt: h_lo[:, kt, ST], kts, LIVE, q == 0, q == 3)
                        if q == 1:
                            P = lambda j, k, w=128: sm[0:QT, QO[j] + 128 * k:QO[j] + 128 * k + w]
                            turn_p(3, [(B(B_P, 0, QT), P(0, 0)), (B(B_P, QT, 2 * QT), P(1, 0)),
                                       (B(B_P, 2 * QT, 3 * QT), P(2, 0)), (B(B_P, 3 * QT, 4 * QT), P(1, 1)),
                                       (B(B_P, 4 * QT, 5 * QT), P(2, 1)), (B(B_V, 384, 384 + QT, META), P(2, 2, META))])
                    weigh(2, 2, [(B(B_P, 0, LIVE), v_t[:, 0, :], p_t[:, 0:3 * QT]),
                                 (B(B_P, QT, LIVE), v_t[:, 1, :], p_t[:, 3 * QT:5 * QT]),
                                 (B(B_P, 2 * QT, LIVE), v_t[0:META, 2, :], p_t[0:META, 5 * QT:6 * QT])])
            pe.wait_ge(o_lo, 2 * HEADS)
            pe.wait_ge(pl_lo_ready, AT)
            narrow = slice(0, LIVE)
            with loop(pe, 4, (halves, 16), (groups, 6)):
                for n in range(2):
                    product(h_hi, h_lo, ST)
                    product(a_hi, a_lo, narrow, AT)
                    product(pl_hi, pl_lo, narrow, AT)
            pe.wait_ge(m_lo_ready, KT)
            with loop(pe, 4, (halves, 8), (groups, 2)):
                for n in range(2):
                    product(m_hi, m_lo, narrow)
            channel_sums(LIVE)
            channel_sums(LIVE)
            ffn(ST, 3 * KT, False)
            channel_sums(SEQ)
            for n in range(8):
                t, j = n // 4, n % 4
                pe.wait_ge(x_ready, X_TOTAL)
                if n >= 4:
                    pe.wait_ge(last_copied, n - 3)
                for a in range(4):
                    mm = pe.transpose(bank[:, B_S + n % 4, 128 * a:128 * a + 128],
                                      xt[:, 4 * j + a, META + 128 * t:META + 128 * t + 128], ident[:, :])
                mm.then_inc(last_done, 1)


_INS = ['x', 'c', 'ada_w', 'ada_b', 'mix_pre_g', 'mix_post_g', 'w_in', 'conv_w', 'conv_b', 'conv_ln_g',
        'conv_ln_b', 'w_out', 'ffn_pre_g', 'ffn_post_g', 'w_gate', 'w_up', 'w_down', 'meta_tokens_2',
        'mix_pre_g_2', 'w_in_2', 'b_in_2', 'w_attn_o_2', 'pool_w_2', 'pool_scale_2', 'w_pool_o_2', 'w_out_2',
        'mix_post_g_2', 'ffn_pre_g_2', 'w_ffn_up_2', 'ffn_conv_w_2', 'ffn_conv_b_2', 'w_ffn_down_2',
        'ffn_post_g_2']


def kernel(**inputs):
    import numpy as _np
    import concourse.bacc as _bacc
    from concourse.bass_utils import run_bass_kernel_spmd as _run

    nc = _bacc.Bacc("TRN2", target_bir_lowering=False, num_devices=1)
    arrays, args = {}, []
    for name in _INS:
        a = _np.ascontiguousarray(inputs[name])
        if a.shape[0] == 1:
            a = a.reshape(a.shape[1:])
        arrays[f"in_{name}"] = a
        args.append(nc.dram_tensor(f"in_{name}", a.shape, mybir.dt.float32, kind="ExternalInput").ap())
    args.append(nc.dram_tensor("out", (SEQ, D), mybir.dt.float32, kind="ExternalOutput").ap())
    build(nc, *args)
    r = _run(nc, [arrays], core_ids=[0])
    return r.results[0]["out"].reshape(1, SEQ, D)
```

```python
import concourse.bass as bass
from concourse import mybir
from contextlib import ExitStack, contextmanager

D = 2048
KT = D // 128
SEQ, META = 256, 16
ALL = SEQ + META
LIVE0 = META - 2
LIVE = ALL - LIVE0
HD, HEADS = 128, 8
DA = HD * HEADS
AT = DA // 128
CONV_K = 31
F = 5632
FT = F // 128
CHUNK = 512
NCHUNK = F // CHUNK
MODS = 6
SCALE = HD ** -0.5
NEG = -1e30
RING = 4
LEAD = 3
QT = LIVE // 3
QW = (128, 256, 272)
QO = (0, 128, 384)
QSUM = sum(QW)
WINDOWS = (2, 4, 8, 16)
FFN_HALVES = NCHUNK * 24
HALVES = 112 + FFN_HALVES + 2 + 64 + 96 + 2 + 32 + FFN_HALVES
X_TOTAL = 4 * KT

ADA_SLOT = [a % 2 if a < 4 * KT - (NCHUNK - 1) else 0 for a in range(4 * KT)]

SB, ST = slice(META, ALL), slice(LIVE0, ALL)


class Count:

    def __init__(self, start=0):
        self.c, self.i, self.per, self.c0 = start, None, 0, 0

    def enter(self, i, per):
        self.i, self.per, self.c0 = i, per, self.c

    def leave(self, trips):
        assert self.c - self.c0 == self.per, (self.c - self.c0, self.per)
        self.c, self.i = self.c0 + self.per * trips, None

    def at(self, mult=1, add=0):
        base = self.c * mult + add
        return base if self.i is None or not self.per else self.i * (self.per * mult) + base

    def div(self, d, mult, add):
        base = (self.c // d) * mult + add
        if self.i is None or not self.per:
            return base
        assert self.per % d == 0
        return self.i * (self.per // d * mult) + base

    def mod(self, d):
        assert self.i is None or self.per % d == 0
        return self.c % d

    def next(self, n=1, mult=1, add=0):
        self.c += n
        return self.at(mult, add)


class Banks:

    def __init__(self):
        self.had, self.pair, self.read = [Count(), Count()], 0, None

    def bank(self):
        return 2 * self.pair

    def free(self):
        return self.had[self.pair].at(1, 1)

    def close(self):
        b, self.read = self.bank(), self.had[self.pair].at(1, 2)
        self.had[self.pair].next()
        self.pair ^= 1
        return b


@contextmanager
def loop(eng, trips, *counts):
    flat = []
    for c, per in counts:
        if isinstance(c, Banks):
            flat += [(c.had[0], (per + 1) // 2), (c.had[1], per // 2)]
        else:
            flat.append((c, per))
    counts = flat
    with eng.Fori(0, trips) as i:
        for c, per in counts:
            c.enter(i, per)
        yield i
    for c, _ in counts:
        c.leave(trips)


def ds(start, size=1):
    return bass.ds(start, size)


def build(nc, x, c, ada_w, ada_b, mix_pre_g, mix_post_g, w_in, conv_w, conv_b, conv_ln_g, conv_ln_b,
          w_out, ffn_pre_g, ffn_post_g, w_gate, w_up, w_down, meta_tokens_2, mix_pre_g_2, w_in_2,
          b_in_2, w_attn_o_2, pool_w_2, pool_scale_2, w_pool_o_2, w_out_2, mix_post_g_2,
          ffn_pre_g_2, w_ffn_up_2, ffn_conv_w_2, ffn_conv_b_2, w_ffn_down_2, ffn_post_g_2, out):
    f32, f32r = mybir.dt.float32, mybir.dt.float32r
    ACT, ALU, AX = mybir.ActivationFunctionType, mybir.AluOpType, mybir.AxisListType
    ctx = ExitStack()
    with ctx:
        base = (nc.sbuf_base + 31) // 32 * 32
        sizes = dict(raw=RING * 4096, hi=RING * 4096, lo=RING * 4096, xt=KT * ALL * 4,
                     hhi=KT * ALL * 4, hlo=KT * ALL * 4, r1=KT * ALL * 4, r2=41472, r3=25600)
        at, region = 0, {}
        for name, size in sizes.items():
            region[name] = at
            at += size
        ctx.enter_context(nc.sbuf_tensor("arena", [128, at + 32], mybir.dt.uint8))

        def place(name, reg, off, shape, dt=f32):
            n = 4
            for s in shape[1:]:
                n *= s
            spans = {"hhi": ("hhi", "hlo")}.get(reg, (reg,))
            assert off + n <= sum(sizes[r] for r in spans), name
            return nc.alloc_sbuf_tensor_at(name, shape, dt, offset=base + region[reg] + off, align_bytes=4)

        def sb(name, shape, dt=f32):
            return ctx.enter_context(nc.sbuf_tensor(name, shape, dt))

        def sem(name):
            return ctx.enter_context(nc.semaphore(name))

        raw = place("raw", "raw", 0, [128, RING, 4, 256])
        w_hi = place("w_hi", "hi", 0, [128, RING, 4, 256], f32r)
        w_lo = place("w_lo", "lo", 0, [128, RING, 4, 256], f32r)
        xt = place("xt", "xt", 0, [128, KT, ALL])
        h_hi = place("h_hi", "hhi", 0, [128, KT, ALL], f32r)
        h_lo = place("h_lo", "hlo", 0, [128, KT, ALL], f32r)
        ada_pre = place("ada_pre", "hhi", 0, [128, 4, D])
        y = place("y", "r1", 0, [128, KT, ALL])
        upad = place("upad", "r1", 0, [128, AT, CONV_K - 1 + SEQ])
        cv = place("cv", "r1", AT * (CONV_K - 1 + SEQ) * 4, [128, AT, SEQ])
        y1 = place("y1", "hhi", 0, [128, KT, ALL])
        c_hi = place("c_hi", "hlo", 0, [128, AT, ALL], f32r)
        c_lo = place("c_lo", "hlo", AT * ALL * 4, [128, AT, ALL], f32r)
        m_hi = place("m_hi", "r1", 0, [128, KT, LIVE], f32r)
        u2 = place("u2", "r1", 0, [128, AT, META + ALL])
        xrow = place("xrow", "r2", 0, [128, 2, D])
        mrow = place("mrow", "r2", 16384, [META, D])
        cwrow = place("cwrow", "r2", 24576, [CONV_K, DA])
        prow = place("prow", "r2", 28672, [128, 7, 128])
        a_hi = place("a_hi", "r2", 0, [128, AT, ALL], f32r)
        a_lo = place("a_lo", "r2", AT * ALL * 4, [128, AT, ALL], f32r)
        y2 = place("y2", "r2", 0, [128, KT, ALL])
        m_lo = place("m_lo", "r2", 2 * AT * ALL * 4, [128, KT, LIVE], f32r)
        hid = place("hid", "r2", 0, [128, 4, SEQ])
        sg = place("sg", "r2", 4096, [128, 4, SEQ])
        va = place("va", "r2", 8192, [128, 4, SEQ])
        hid_hi = place("hid_hi", "r2", 12288, [128, 4, SEQ], f32r)
        hid_lo = place("hid_lo", "r2", 16384, [128, 4, SEQ], f32r)
        outrow = place("outrow", "r2", 0, [128, 2, D])
        qkv = place("qkv", "r2", 17408, [128, 3, 2, ALL])
        sm = place("sm", "r2", 23936, [128, QSUM])
        v_t = place("v_t", "r2", 26560, [128, 3, 128])
        p_t = place("p_t", "r2", 28096, [128, 6 * QT])
        acc_b = place("acc_b", "r2", 30208, [128, D])
        sigg = place("sigg", "r2", 38400, [128, 2, SEQ])
        cvb = place("cvb", "r2", 40448, [128, SEQ])
        ada_raw = place("ada_raw", "r3", 0, [128, 2, D])
        acc = place("acc", "r3", 16384, [128, D])
        pl_hi = place("pl_hi", "r3", 0, [128, AT, LIVE], f32r)
        pl_lo = place("pl_lo", "r3", AT * LIVE * 4, [128, AT, LIVE], f32r)
        d_hi, d_lo = pl_hi, pl_lo
        lf = [place(f"lf{n}", "r3", 16512 + n * 2112, [HEADS, 256 + ALL]) for n in range(2)]
        sc_in = place("sc_in", "r3", 16512 + 4224, [HEADS, ALL])
        rel = place("rel", "r3", 16512 + 5312, [HEADS, 3, ALL])
        ga_s = place("ga_s", "r3", 16512, [128, 2, LIVE])
        gp_s = place("gp_s", "r3", 16512 + 2064, [128, 2, LIVE])
        pcol = sb("pcol", [128, 7, 128])
        cwt = sb("cwt", [128, AT, CONV_K + 1])
        ident = sb("ident", [128, 128])
        ones = sb("ones", [128, 128])
        mask = sb("mask", [128, QSUM])
        sq = sb("sq", [128, 2, ALL])
        rstd = sb("rstd", [128, ALL])
        stat = sb("stat", [128, ALL])
        mod = sb("mod", [128, MODS, KT])
        cact = sb("cact", [128, 4, KT])
        coef = sb("coef", [128, 4, KT])
        sel = sb("sel", [HEADS, 2, QT])
        pick = sb("pick", [HEADS, HEADS])
        win = sb("win", [128, 2, META + ALL])
        bf = sb("bf", [HEADS, 1])
        mx = sb("mx", [128, 3])
        rs = sb("rs", [128, 3])
        bank = ctx.enter_context(nc.psum_tensor("bank", [128, 8, 512], f32))
        B_S, B_N, B_P, B_V = 4, 5, 6, 7

        adab, ccol, pscale = pcol[:, 0, 0:96], pcol[:, 0, 96:112], pcol[:, 0, 112:120]
        g_mix1, g_mixp1, g_ffn1, g_ffnp1 = (pcol[:, 1, 16 * n:16 * n + 16] for n in range(4))
        lng, lnb, cb = (pcol[:, 1, 64 + 8 * n:72 + 8 * n] for n in range(3))
        g_mix2, g_mixp2, g_ffn2, g_ffnp2 = (pcol[:, 2, 16 * n:16 * n + 16] for n in range(4))
        b_qkv, b_u, b_ga, b_gp = (pcol[:, 2, a:b] for a, b in ((64, 88), (88, 96), (96, 112), (112, 128)))
        C_QKV, C_F, C_U = 0, 3 * DA, 3 * DA + HEADS
        C_GA = C_U + DA
        C_GP = C_GA + D

        raw_loaded = [sem(f"raw_loaded{n}") for n in range(RING)]
        hi_ready = sem("hi_ready")
        lo_ready = sem("lo_ready")
        half_used = sem("half_used")
        bank_free = [sem(f"bank_free{n}") for n in range(4)]
        c_loaded, rows_loaded = sem("c_loaded"), sem("rows_loaded")
        consts = sem("consts")
        tr_done = sem("tr_done")
        tr_copied = sem("tr_copied")
        cact_ready = sem("cact_ready")
        pre_loaded = [sem(f"pre_loaded{n}") for n in range(4)]
        pre_used = sem("pre_used")
        ada_loaded = [sem(f"ada_loaded{n}") for n in range(2)]
        ada_scaled = sem("ada_scaled")
        ada_used = sem("ada_used")
        acc_zero = sem("acc_zero")
        ada_sum = sem("ada_sum")
        mod_ready = sem("mod_ready")
        coef_ready = sem("coef_ready")
        sq_ready = sem("sq_ready")
        sq_used = sem("sq_used")
        stat_ready = sem("stat_ready")
        var_ready = sem("var_ready")
        rstd_ready = sem("rstd_ready")
        term_ready = sem("term_ready")
        h_hi_ready = sem("h_hi_ready")
        h_ready = sem("h_ready")
        y_scaled = sem("y_scaled")
        x_ready = sem("x_ready")
        y_zero = sem("y_zero")
        conv_step = sem("conv_step")
        mu_sum, cen_ready = sem("mu_sum"), sem("cen_ready")
        ln_term, ln_silu = sem("ln_term"), sem("ln_silu")
        mix_hi, mix_ready = sem("mix_hi"), sem("mix_ready")
        sel_ready = sem("sel_ready")
        s_done = sem("s_done")
        v_done = sem("v_done")
        soft = sem("soft")
        p_masked = sem("p_masked")
        v_copied, p_exp = sem("v_copied"), sem("p_exp")
        p_ready = sem("p_ready")
        pt_done, pt_copied = sem("pt_done"), sem("pt_copied")
        o_done = sem("o_done")
        o_hi, o_lo = sem("o_hi"), sem("o_lo")
        hid_ready = sem("hid_ready")
        hid_hi_ready, hid_lo_ready = sem("hid_hi_ready"), sem("hid_lo_ready")
        tap_ready = sem("tap_ready")
        tap_next = sem("tap_next")
        gelu_ready = sem("gelu_ready")
        f_step = sem("f_step")
        scan = sem("scan")
        pads = sem("pads")
        rel_ready = sem("rel_ready")
        win_step = sem("win_step")
        d_ready, d_hi_ready, d_lo_ready = sem("d_ready"), sem("d_hi_ready"), sem("d_lo_ready")
        pl_hi_ready, pl_lo_ready = sem("pl_hi_ready"), sem("pl_lo_ready")
        m_part = sem("m_part")
        m_ready, m_hi_ready, m_lo_ready = sem("m_ready"), sem("m_hi_ready"), sem("m_lo_ready")
        last_done, last_copied, stored = sem("last_done"), sem("last_copied"), sem("stored")
        block = ctx.enter_context(nc.Block())

        def fp(ap):
            return ap.bitcast(f32)

        @block.sync
        def _(sp):
            halves = Count()

            def half(src):
                slot = halves.mod(RING)
                sp.wait_ge(lo_ready, halves.at(1, 1))
                sp.dma_start(raw[:, slot], src).then_inc(raw_loaded[slot], 16)
                halves.next()

            def k_tiles(w, row, col, rows):
                for r in range(row, row + rows, 512):
                    half(w[r:r + 512, ds(col, 256)].rearrange("(t p) n -> p t n", p=128))

            def down_rows(w, chunk):
                for n in range(8):
                    half(w[ds(chunk, CHUNK), n * 256:n * 256 + 256].rearrange("(t p) n -> p t n", p=128))

            for src, dst in ((ada_b.rearrange("(n p) -> n p", p=128), prow[0:96, 0]),
                             (c.rearrange("(n p) -> n p", p=128), prow[96:112, 0]),
                             (pool_scale_2.rearrange("(n p) -> n p", p=128), prow[112:120, 0])):
                sp.dma_start(dst, src).then_inc(c_loaded, 16)
            pre = Count()
            for part in (1, 0):
                with loop(sp, 4, (pre, 4)) as i:
                    rows = [sp.snap(i * 512 + n * 128) for n in range(4)]
                    for n in range(4):
                        row = rows[n]
                        slot = pre.mod(4)
                        sp.wait_ge(pre_used, pre.at(1, 1))
                        sp.dma_start(ada_pre[:, slot], ada_w[ds(row, 128), part * D:(part + 1) * D])\
                          .then_inc(pre_loaded[slot], 16)
                        pre.next()
            with loop(sp, 4, (halves, 8)) as i:
                a = sp.snap(i * 256 + 3 * DA)
                g = sp.snap(i * 256 + 3 * DA + DA)
                k_tiles(w_in, 0, g, D)
                k_tiles(w_in, 0, a, D)
            with loop(sp, 4, (halves, 12)) as i:
                cols = [sp.snap(i * 256 + n * DA) for n in range(3)]
                for col in cols:
                    k_tiles(w_in, 0, col, D)
            for row in (0, 512):
                for n in range(8):
                    k_tiles(w_out, row, n * 256, 512)
            for n in range(8):
                k_tiles(w_out, DA, n * 256, DA)

            def ffn(gate, up, up0, down):
                for n in range(2):
                    k_tiles(gate, 0, n * 256, D)
                for n in range(2):
                    k_tiles(up, 0, up0 + n * 256, D)
                with loop(sp, NCHUNK - 1, (halves, 24)) as i:
                    gates = [sp.snap(i * CHUNK + CHUNK + n * 256) for n in range(2)]
                    rows = sp.snap(i * CHUNK)
                    ups = [sp.snap(i * CHUNK + up0 + CHUNK + n * 256) for n in range(2)]
                    for col in gates:
                        k_tiles(gate, 0, col, D)
                    down_rows(down, rows)
                    for col in ups:
                        k_tiles(up, 0, col, D)
                down_rows(down, (NCHUNK - 1) * CHUNK)

            ffn(w_gate, w_up, 0, w_down)
            for n in range(2):
                slot = halves.mod(RING)
                sp.wait_ge(lo_ready, halves.at(1, 1))
                sp.dma_start(raw[:, slot].rearrange("p t n -> p (t n)").rearrange("p (t n) -> p t n", n=128),
                             w_in_2[1024 * n:1024 * n + 1024, C_F:C_F + 128].rearrange("(t p) n -> p t n", p=128))\
                  .then_inc(raw_loaded[slot], 16)
                halves.next()
            with loop(sp, 4, (halves, 16)) as i:
                cols = [sp.snap(i * 256 + off) for off in (0, DA, 2 * DA, C_U)]
                for col in cols:
                    k_tiles(w_in_2, 0, col, D)
            k_tiles(w_in_2, 0, C_GA, D)
            k_tiles(w_in_2, 0, C_GP, D)
            k_tiles(w_attn_o_2, 0, 0, DA)
            k_tiles(pool_w_2.rearrange("g c n -> (g c) n"), 0, 0, DA)
            with loop(sp, 7, (halves, 12)) as i:
                this = sp.snap(i * 256)
                ga = sp.snap((i + 1) * 256 + C_GA)
                gp = sp.snap((i + 1) * 256 + C_GP)
                nxt = sp.snap(i * 256 + 256)
                k_tiles(w_pool_o_2, 0, this, DA)
                k_tiles(w_in_2, 0, ga, D)
                k_tiles(w_in_2, 0, gp, D)
                k_tiles(w_attn_o_2, 0, nxt, DA)
            k_tiles(w_pool_o_2, 0, 7 * 256, DA)
            with loop(sp, 4, (halves, 8)) as i:
                cols = [sp.snap(i * 512 + n * 256) for n in range(2)]
                for col in cols:
                    k_tiles(w_out_2, 0, col, D)
            ffn(w_ffn_up_2, w_ffn_up_2, F, w_ffn_down_2)
            sp.wait_ge(last_copied, 8)
            sp.dma_start(out.rearrange("(t p) n -> p t n", p=128), outrow[:, :, :]).then_inc(stored, 16)
            sp.wait_ge(stored, 16)

        @block.gpsimd
        def _(gp):
            gp.memset(ident[:, :], 0.0).then_inc(consts, 1)
            gp.memset(ones[:, :], 1.0).then_inc(consts, 1)
            gp.wait_ge(consts, 2)
            gp.affine_select(out=ident[:, :], in_=ident[:, :], compare_op=ALU.not_equal, fill=1.0,
                             base=0, pattern=[[-1, 128]], channel_multiplier=1).then_inc(consts, 1)
            gp.memset(mask[:, :], 0.0).then_inc(consts, 1)
            gp.wait_ge(consts, 4)
            m = mask[:, 0:512].rearrange("p (j k) -> p j k", j=2)
            gp.affine_select(out=m, in_=m, compare_op=ALU.is_ge, fill=NEG, base=0,
                             pattern=[[128, 2], [-1, SEQ]], channel_multiplier=1).then_inc(consts, 1)
            def ada_load(a):
                slot = ADA_SLOT[a]
                before = [b for b in range(a) if ADA_SLOT[b] == slot]
                part, kt = 2 + a // KT, a % KT
                if before:
                    gp.wait_ge(ada_used, before[-1] + 1)
                gp.dma_start(ada_raw[:, slot], ada_w[128 * kt:128 * kt + 128, part * D:(part + 1) * D])\
                  .then_inc(ada_loaded[slot], 16)

            gp.wait_ge(ada_sum, 2)
            ada_load(0)
            ada_load(1)
            for a in range(4 * KT):
                part = 2 + a // KT
                dst = acc_b if part == 3 else acc
                if a % KT == 0:
                    if part == 4:
                        gp.wait_ge(ada_sum, 3)
                    if part == 5:
                        gp.wait_ge(h_ready, 2 * KT)
                        gp.memset(y[:, :, SB], 0.0).then_inc(y_zero, 1)
                        gp.wait_ge(ada_sum, 5)
                    gp.memset(dst[:, :], 0.0).then_inc(acc_zero, 1)
                    gp.wait_ge(acc_zero, part + 1)
                gp.wait_ge(ada_scaled, a + 1)
                if a % KT:
                    gp.wait_ge(ada_used, a)
                gp.tensor_tensor(dst[:, :], dst[:, :], ada_raw[:, ADA_SLOT[a]], ALU.add).then_inc(ada_used, 1)
                for b in range(2, 4 * KT):
                    if a == max(x for x in range(b) if ADA_SLOT[x] == ADA_SLOT[b]):
                        ada_load(b)
            gp.wait_ge(h_ready, 3 * KT)
            gp.memset(mask[:, :], 0.0).then_inc(consts, 1)
            gp.memset(u2[:, :, 0:META], 0.0).then_inc(pads, 1)
            gp.memset(lf[0][:, 0:256], 0.0).then_inc(pads, 1)
            gp.memset(lf[1][:, 0:256], 0.0).then_inc(pads, 1)
            gp.wait_ge(consts, 6)
            for j in range(3):
                m = mask[0:QT, QO[j]:QO[j] + QW[j]]
                gp.affine_select(out=m, in_=m, compare_op=ALU.is_ge, fill=NEG, base=LIVE0 + QT * j,
                                 pattern=[[-1, QW[j]]], channel_multiplier=1).then_inc(consts, 1)
            gp.tensor_scalar(pick[:, :], ident[0:HEADS, 0:HEADS], -1.0 / SCALE, 0.0, ALU.mult, ALU.add)\
              .then_inc(consts, 1)
            gp.wait_ge(consts, 10)
            with loop(gp, 4) as i:
                gp.wait_ge(s_done, i * 2 + HEADS)
                for o in range(2):
                    gp.tensor_copy(sel[:, o, :], pick[:, ds(i * 2 + o)].to_broadcast([HEADS, QT]))\
                      .then_inc(sel_ready, 1)
            gp.wait_ge(h_ready, 4 * KT)
            gp.memset(y[:, :, SB], 0.0).then_inc(y_zero, 1)

        @block.scalar
        def _(act):
            halves, done, banks = Count(), Count(RING), Banks()

            def convert():
                if halves.i is None and halves.c >= HALVES:
                    return
                slot = halves.mod(RING)
                act.wait_ge(raw_loaded[slot], halves.div(RING, 16, 16))
                act.wait_ge(half_used, halves.at(1, 1))
                act.activation(w_hi[:, slot], raw[:, slot], ACT.Copy).then_inc(hi_ready, 1)
                halves.next()

            def group(n=4):
                for _ in range(n):
                    convert()
                act.wait_ge(half_used, done.next(n))
                return banks.close()

            def skip(n_halves, n_groups):
                for _ in range(n_halves):
                    convert()
                done.next(n_halves)
                for _ in range(n_groups):
                    banks.close()

            act.dma_start(xrow[:, :, :], x.rearrange("(t p) n -> p t n", p=128)).then_inc(rows_loaded, 16)
            for t, src, r, n in (
                    (1, mix_pre_g, 0, 16), (1, mix_post_g, 16, 16), (1, ffn_pre_g, 32, 16),
                    (1, ffn_post_g, 48, 16), (1, conv_ln_g, 64, 8), (1, conv_ln_b, 72, 8), (1, conv_b, 80, 8),
                    (2, mix_pre_g_2, 0, 16), (2, mix_post_g_2, 16, 16), (2, ffn_pre_g_2, 32, 16),
                    (2, ffn_post_g_2, 48, 16), (2, b_in_2[0:C_F], 64, 24), (2, b_in_2[C_U:C_GA], 88, 8),
                    (2, b_in_2[C_GA:C_GP], 96, 16), (2, b_in_2[C_GP:C_GP + D], 112, 16),
                    (3, ffn_conv_b_2, 0, 2 * FT), (4, ffn_conv_w_2[0], 0, 2 * FT),
                    (5, ffn_conv_w_2[1], 0, 2 * FT), (6, ffn_conv_w_2[2], 0, 2 * FT)):
                act.dma_start(prow[r:r + n, t], src.rearrange("(n p) -> n p", p=128)).then_inc(rows_loaded, 16)
            act.dma_start(mrow[:, :], meta_tokens_2).then_inc(rows_loaded, 16)
            act.dma_start(cwrow[:, :], conv_w).then_inc(rows_loaded, 16)
            act.dma_start(bf[:, :], b_in_2[C_F:C_U].rearrange("(n p) -> n p", p=1)).then_inc(rows_loaded, 16)
            seen = Count()

            def copied(out_ap, in_ap):
                act.wait_ge(tr_done, seen.next())
                act.activation(out_ap, in_ap, ACT.Copy).then_inc(tr_copied, 1)

            def quarters(b, n):
                return bank[:, b, 0:512 if n == 4 else 256].rearrange("p (a b) -> p a b", a=n)

            copied(pcol[:, 0, 0:120], bank[:, B_S, 0:120])
            act.wait_ge(tr_copied, 1)
            for n in range(4):
                act.activation(cact[:, n], ccol, ACT.Silu).then_inc(cact_ready, 1)
            for n in range(8):
                t, j = n // 4, n % 4
                copied(xt[:, 4 * j:4 * j + 4, META + 128 * t:META + 128 * t + 128], quarters(B_S + (1 + n) % 4, 4))
            copied(pcol[:, 1, 0:88], bank[:, B_S + 1, 0:88])
            copied(pcol[:, 2, :], bank[:, B_S + 2, 0:128])
            copied(pcol[:, 3:7, 0:88], quarters(B_S + 3, 4)[:, :, 0:88])
            copied(xt[:, :, 0:META], quarters(B_S, KT))
            copied(cwt[:, :, 0:CONV_K], quarters(B_S + 1, AT)[:, :, 0:CONV_K])
            act.wait_ge(tr_copied, 14)
            sqs, roots, terms = Count(), Count(), Count()

            def square(src, cols, kt):
                if sqs.c >= 2:
                    act.wait_ge(sq_used, sqs.at(1, -1))
                act.activation(sq[:, kt % 2, 0:cols.stop - cols.start], src[:, kt, cols], ACT.Square)\
                   .then_inc(sq_ready, 1)
                sqs.next()

            def squares(src, cols, n=KT, ready=None):
                for kt in range(n):
                    if ready is not None:
                        act.wait_ge(ready[0], ready[1].next())
                    square(src, cols, kt)

            def squares_of_sums(src, cols, first, n_halves):
                for o in range(2):
                    act.wait_ge(bank_free[first + o], banks.read)
                    square(src, cols, n_halves + o)

            def root(width):
                act.wait_ge(var_ready, roots.next())
                act.activation(rstd[:, 0:width], stat[:, 0:width], ACT.Sqrt).then_inc(rstd_ready, 1)

            def h_tile(kt, cols, shift=None):
                act.wait_ge(term_ready, terms.next())
                if shift is None:
                    act.activation(h_hi[:, kt, cols], y[:, kt, cols], ACT.Copy).then_inc(h_hi_ready, 1)
                else:
                    act.activation(h_hi[:, kt, cols], y[:, kt, cols], ACT.Identity,
                                   bias=shift[:, kt:kt + 1]).then_inc(h_hi_ready, 1)

            def h_tiles(cols, shift=None):
                for kt in range(KT):
                    h_tile(kt, cols, shift)

            xs, cens = Count(), Count()
            squares(xt, SB)
            root(SEQ)
            act.wait_ge(mod_ready, 2)
            for kt in range(KT):
                h_tile(kt, SB, mod[:, 0])
                if kt % 4 == 3 and kt < 4 * LEAD:
                    convert()
            slot_loads = [Count(), Count()]
            c_rows = cact[:, :, :].rearrange("p a n -> p (a n)")
            act.wait_ge(cact_ready, 4)

            def ada_row(a, slot):
                act.wait_ge(ada_loaded[slot], slot_loads[slot].next(1, 16))
                act.activation(ada_raw[:, slot], ada_raw[:, slot], ACT.Copy, scale=c_rows[:, ds(a)])\
                   .then_inc(ada_scaled, 1)

            with loop(act, 4, (halves, 8), (done, 8), (banks, 2), (slot_loads[0], 2), (slot_loads[1], 2)) as i:
                for n in range(8):
                    convert()
                    if n % 2:
                        ada_row(i * 4 + n // 2, n // 2 % 2)
                    if n == 4:
                        act.wait_ge(half_used, done.next(4))
                        b = banks.close()
                        for o in range(2):
                            act.wait_ge(bank_free[2 + o], banks.free())
                            act.activation(sigg[:, o], bank[:, b + o, 0:SEQ], ACT.Sigmoid).then_inc(bank_free[b + o], 1)
                done.next(4)
                banks.close()
            vs, masked, pts, outs = Count(), Count(), Count(), Count()

            def exps(tiles, v_parts):
                act.wait_ge(v_done, vs.next())
                for dst, src in v_parts:
                    act.activation(dst, src, ACT.Copy).then_inc(v_copied, 1)
                act.wait_ge(p_masked, masked.next())
                for rows, o, w, j in tiles:
                    act.activation(sm[0:rows, o:o + w], sm[0:rows, o:o + w], ACT.Exp, bias=mx[0:rows, j:j + 1],
                                   accum_out=rs[0:rows, j:j + 1]).then_inc(p_exp, 1)

            def copy_pt(parts):
                act.wait_ge(pt_done, pts.next())
                for dst, src in parts:
                    act.activation(dst, src, ACT.Copy).then_inc(pt_copied, 1)

            def round_out(head, width):
                act.wait_ge(o_done, outs.next())
                act.activation(a_hi[:, ds(head), 0:width], bank[:, B_P:B_P + 1, 0:width], ACT.Copy).then_inc(o_hi, 1)

            def attend(n, pair, exp_tiles, v_parts, pt_parts, width):
                if n == 1:
                    exps(exp_tiles, v_parts)
                if n == 4:
                    copy_pt(pt_parts)
                if n == 5:
                    round_out(pair * 2, width)
                    act.wait_ge(v_done, vs.at(1, 1))
                    exps(exp_tiles, v_parts)
                if n == 8:
                    copy_pt(pt_parts)
                if n == 9:
                    round_out(pair * 2 + 1, width)

            attend1 = lambda n, pair: attend(n, pair, [(128, 0, SEQ, 0), (128, SEQ, SEQ, 1)],
                                             [(v_t[:, 0:2, :], quarters(B_V, 2))],
                                             [(p_t[:, 0:384], bank[:, B_P, 0:384])], SEQ)

            def heads1(body, pair):
                banks.pair = 0
                for n in range(12):
                    convert()
                    if n % 2:
                        ada_row(body * 6 + (KT + n // 2), n // 2 % 2)
                    if pair is not None:
                        attend1(n, pair)
                    if n in (5, 8, 11):
                        act.wait_ge(half_used, done.next(4))
                        b = banks.close()
                        for o in range(2):
                            act.activation(qkv[:, n // 4 + n // 11 - 1, o, SB], bank[:, b + o, 0:SEQ], ACT.Copy)\
                               .then_inc(bank_free[b + o], 1)

            heads1(0, None)
            with loop(act, 3, (halves, 12), (done, 12), (banks, 3), (vs, 2), (masked, 2), (pts, 2), (outs, 2),
                      (slot_loads[0], 3), (slot_loads[1], 3)) as i:
                heads1(i + 1, i)
            for n in range(16):
                convert()
                if n % 2:
                    ada_row(KT + 24 + n // 2, n // 2 % 2)
                if n <= 8:
                    attend1(n, 3)
                if n == 8:
                    attend1(9, 3)
                if 1 <= n <= 8:
                    act.wait_ge(half_used, done.next(1))
                    b = banks.close()
                    for o in range(2):
                        act.activation(y1[:, 2 * n - 2 + o, SB], bank[:, b + o, 0:SEQ], ACT.Copy)\
                           .then_inc(bank_free[b + o], 1)
                if n == 10:
                    squares(cv, slice(0, SEQ), AT, (cen_ready, cens))
                if n == 12:
                    root(SEQ)
                    for t in range(AT):
                        act.wait_ge(ln_term, t + 1)
                        act.activation(cv[:, t, :], cv[:, t, :], ACT.Silu, bias=lnb[:, t:t + 1]).then_inc(ln_silu, 1)
                        act.wait_ge(ln_silu, t + 1)
                        act.activation(c_hi[:, t, SB], cv[:, t, :], ACT.Copy).then_inc(mix_hi, 1)
            done.next(8)
            for _ in range(8):
                banks.close()
            for j in range(8):
                convert()
                convert()
                if j:
                    squares_of_sums(y1, SB, b, 2 * j - 2)
                done.next(2)
                b = banks.close()
            squares_of_sums(y1, SB, b, 14)
            root(SEQ)
            squares(xt, SB, KT, (x_ready, xs))
            root(SEQ)
            act.wait_ge(mod_ready, 5)
            h_tiles(SB, mod[:, 3])
            taps, gelus, hids = Count(), Count(), Count()

            def gate1(i, b, t):
                for o in range(2):
                    act.activation(sg[:, t + o], bank[:, b + o, 0:SEQ], ACT.Silu).then_inc(bank_free[b + o], 1)

            def up1(i, b, t):
                for o in range(2):
                    act.wait_ge(bank_free[b + o], banks.read)
                    act.activation(hid_hi[:, t + o], hid[:, t + o], ACT.Copy).then_inc(hid_hi_ready, 1)

            def tap(dst, i, b, t, first):
                for o in range(2):
                    ch = i * 4 + (t + o + first)
                    act.activation(dst[:, t + o:t + o + 1, :], bank[:, b + o:b + o + 1, 0:SEQ], ACT.Identity,
                                   scale=pcol[:, 4, ds(ch)], bias=pcol[:, 3, ds(ch)]).then_inc(tap_ready, 1)

            def gate2(i, b, t):
                tap(sg, i, b, t, 0)
                for o in range(2):
                    act.wait_ge(bank_free[b + o], banks.read)
                    act.activation(sg[:, t + o], sg[:, t + o], ACT.Gelu_apprx_tanh).then_inc(gelu_ready, 1)

            def up2(i, b, t):
                tap(va, i, b, t, FT)
                for o in range(2):
                    act.wait_ge(hid_ready, hids.next())
                    act.activation(hid_hi[:, t + o], hid[:, t + o], ACT.Copy).then_inc(hid_hi_ready, 1)

            def ffn(gate, up, n_hids, with_ada):
                def chunk(i, read):
                    for g in range(2):
                        read(i, group(), 2 * g)

                first = (gate, 0), (gate, 2), (up, 0), (up, 2)
                a = 3 * KT
                for read, t in first:
                    read(0, group(), t)
                    for n in range(with_ada * (2 - t // 2)):
                        ada_row(a, ADA_SLOT[a])
                        a += 1
                with loop(act, NCHUNK - 1, (halves, 24), (done, 24), (banks, 12), (hids, n_hids),
                          (slot_loads[0], with_ada)) as i:
                    chunk(i + 1, gate)
                    skip(8, 8)
                    chunk(i + 1, up)
                    if with_ada:
                        ada_row(i + a, 0)
                for j in range(8):
                    convert()
                    if j:
                        squares_of_sums(y, SB, b, 2 * j - 2)
                    done.next(1)
                    b = banks.close()
                squares_of_sums(y, SB, b, 14)
                root(SEQ)

            ffn(gate1, up1, 0, 1)
            squares(xt, slice(0, ALL), KT, (x_ready, xs))
            root(ALL)
            h_tiles(slice(0, ALL))
            convert()
            convert()
            act.wait_ge(half_used, done.next(2))
            act.wait_ge(mod_ready, 6)
            act.activation(lf[1][:, 256:], bank[0:HEADS, B_N, 0:ALL], ACT.Identity, bias=bf[:, :]).then_inc(f_step, 1)
            act.wait_ge(f_step, 1)
            act.activation(sc_in[:, :], lf[1][:, 256:], ACT.Abs).then_inc(f_step, 1)
            act.wait_ge(f_step, 2)
            act.activation(sc_in[:, :], sc_in[:, :], ACT.Exp, scale=-1.0).then_inc(f_step, 1)
            act.wait_ge(f_step, 3)
            act.activation(sc_in[:, :], sc_in[:, :], ACT.Ln, bias=1.0).then_inc(f_step, 1)
            every = slice(0, ALL)
            attend2 = lambda n, pair: attend(
                n, pair, [(QT, QO[j], QW[j], j) for j in range(3)],
                [(v_t[:, 0:2, :], quarters(B_V, 2)), (v_t[0:META, 2, :], bank[0:META, B_V, 256:384])],
                [(p_t[:, 0:5 * QT], bank[:, B_P, 0:5 * QT]),
                 (p_t[0:META, 5 * QT:6 * QT], bank[0:META, B_V, 384:384 + QT])], LIVE)

            def heads2(body, pair):
                for n in range(16):
                    convert()
                    if pair is not None:
                        attend2(n, pair)
                    if n in (5, 8, 12, 15):
                        act.wait_ge(half_used, done.next(4))
                        b = banks.close()
                        for o in range(2):
                            if n < 15:
                                act.activation(qkv[:, n // 4 - 1, o:o + 1, every], bank[:, b + o:b + o + 1, 0:ALL],
                                               ACT.Identity, bias=b_qkv[:, ds(body * 2 + (AT * (n // 4 - 1) + o))])\
                                   .then_inc(bank_free[b + o], 1)
                            else:
                                act.activation(u2[:, ds(body * 2 + o), META:], bank[:, b + o:b + o + 1, 0:ALL],
                                               ACT.Identity, bias=b_u[:, ds(body * 2 + o)])\
                                   .then_inc(bank_free[b + o], 1)

            heads2(0, None)
            with loop(act, 3, (halves, 16), (done, 16), (banks, 4), (vs, 2), (masked, 2), (pts, 2), (outs, 2)) as i:
                heads2(i + 1, i)
            ms = Count()

            def gate(dst, bias, tile):
                b = banks.close()
                for o in range(2):
                    act.activation(dst[:, o:o + 1], bank[:, b + o:b + o + 1, 0:LIVE], ACT.Sigmoid,
                                   bias=bias[:, ds(tile + o)]).then_inc(bank_free[b + o], 1)

            for n in range(10):
                convert()
                if n <= 8:
                    attend2(n, 3)
                if n == 8:
                    attend2(9, 3)
                if 1 <= n <= 8:
                    act.wait_ge(d_ready, n)
                    act.activation(d_hi[:, n - 1], sq[:, (n - 1) % 2, 0:LIVE], ACT.Copy).then_inc(d_hi_ready, 1)
                if n in (4, 8):
                    act.wait_ge(half_used, done.next(4))
                    gate(ga_s if n == 4 else gp_s, b_ga if n == 4 else b_gp, 0)
            done.next(2)
            banks.close()
            for g in range(4):
                if g % 2 == 0:
                    convert()
                    act.wait_ge(half_used, done.next(1))
                b = banks.close()
                for o in range(2):
                    t = 2 * g + o
                    act.wait_ge(d_lo_ready if t < 2 else pl_lo_ready, AT if t < 2 else t - 1)
                    act.activation(sq[:, t % 2, 0:LIVE], bank[:, b + o, 0:LIVE], ACT.Copy, scale=pscale[:, t:t + 1])\
                       .then_inc(bank_free[b + o], 1)
                    act.wait_ge(bank_free[b + o], banks.read)
                    act.activation(pl_hi[:, t], sq[:, t % 2, 0:LIVE], ACT.Copy).then_inc(pl_hi_ready, 1)

            def mix(body):
                skip(2, 1)
                for o in range(2):
                    act.wait_ge(m_ready, ms.next())
                    act.activation(m_hi[:, ds(body * 2 + o)], gp_s[:, o:o + 1], ACT.Copy).then_inc(m_hi_ready, 1)

            with loop(act, 7, (halves, 12), (done, 12), (banks, 4), (ms, 2)) as i:
                mix(i)
                for n in range(2):
                    for _ in range(4):
                        convert()
                    act.wait_ge(half_used, done.next(4))
                    if n == 1:
                        act.wait_ge(m_lo_ready, ms.at())
                    gate(gp_s if n else ga_s, b_gp if n else b_ga, i * 2 + 2)
                skip(2, 1)
            mix(7)

            def out_tiles(b, tile):
                for o in range(2):
                    act.activation(y2[:, ds(tile + o), ST], bank[:, b + o:b + o + 1, 0:LIVE], ACT.Copy)\
                       .then_inc(bank_free[b + o], 1)

            with loop(act, 3, (halves, 8), (done, 8), (banks, 2)) as i:
                for n in range(2):
                    out_tiles(group(), i * 4 + 2 * n)
            for n in range(8):
                convert()
                if n == 4:
                    act.wait_ge(half_used, done.next(4))
                    out_tiles(banks.close(), 12)
                if n < 6:
                    for o in range(2):
                        if n == 0:
                            act.wait_ge(bank_free[2 * banks.pair + 2 * 0 + o], banks.free())
                        square(y2, ST, 2 * n + o)
            act.wait_ge(half_used, done.next(4))
            out_tiles(banks.close(), 14)
            for kt in range(12, KT):
                for b in range(4):
                    act.wait_ge(bank_free[b], banks.had[b // 2].at(1, 1))
                square(y2, ST, kt)
            root(LIVE)
            squares(xt, ST, KT, (x_ready, xs))
            root(LIVE)
            h_tiles(ST)
            ffn(gate2, up2, 4, 0)
            for n in range(8):
                act.wait_ge(last_done, n + 1)
                act.activation(outrow[:, n // 4, 512 * (n % 4):512 * (n % 4) + 512], bank[:, B_S + n % 4, :], ACT.Copy)\
                   .then_inc(last_copied, 1)

        @block.vector
        def _(dve):
            halves, done, banks = Count(), Count(RING), Banks()

            def convert():
                if halves.i is None and halves.c >= HALVES:
                    return
                slot = halves.mod(RING)
                dve.wait_ge(hi_ready, halves.at(1, 1))
                dve.tensor_tensor(w_lo[:, slot], raw[:, slot], fp(w_hi[:, slot]), ALU.subtract).then_inc(lo_ready, 1)
                halves.next()

            def group(n=4):
                for _ in range(n):
                    convert()
                dve.wait_ge(half_used, done.next(n))
                return banks.close()

            def skip(n_halves, n_groups):
                for _ in range(n_halves):
                    convert()
                done.next(n_halves)
                for _ in range(n_groups):
                    banks.close()

            dve.memset(mx[:, :], 0.0).then_inc(lo_ready, RING)
            dve.memset(rs[:, :], 0.0).then_inc(half_used, RING)
            dve.memset(stat[:, 0:1], 0.0).then_inc(bank_free[0], 1)
            dve.memset(stat[:, 1:2], 0.0).then_inc(bank_free[1], 1)
            dve.memset(stat[:, 2:3], 0.0).then_inc(bank_free[2], 1)
            dve.memset(stat[:, 3:4], 0.0).then_inc(bank_free[3], 1)
            dve.memset(stat[:, 4:5], 0.0).then_inc(pre_used, 4)
            pre, zeros, parts_done = Count(), Count(), Count()

            def clear_acc():
                dve.memset(acc[:, :], 0.0).then_inc(acc_zero, 1)
                dve.wait_ge(acc_zero, zeros.next())

            def finish(part):
                dve.wait_ge(ada_sum, parts_done.next())
                dve.tensor_tensor(mod[:, part], bank[:, B_N, 496:512], adab[:, KT * part:KT * part + KT], ALU.add)\
                   .then_inc(mod_ready, 1)

            def mod_part(part):
                with loop(dve, 4, (pre, 4)) as i:
                    for n in range(4):
                        dve.wait_ge(pre_loaded[n], pre.div(4, 16, 16))
                        dve.wait_ge(pre_used, pre.at(1, 4))
                        dve.scalar_tensor_tensor(out=acc[:, :], in0=ada_pre[:, n], scalar=cact[:, 0, ds(i * 4 + n)],
                                                 in1=acc[:, :], op0=ALU.mult, op1=ALU.add).then_inc(pre_used, 1)
                        pre.next()

            sums, stats, roots, hs, ys, xs = (Count() for _ in range(6))

            def inverse(width, n, eps):
                dve.wait_ge(sq_used, sums.next(n // 128))
                dve.tensor_scalar(stat[:, 0:width], bank[:, B_N, 0:width], 1.0 / n, eps, ALU.mult, ALU.add)\
                   .then_inc(stat_ready, 1)
                dve.wait_ge(stat_ready, stats.next())
                dve.reciprocal(stat[:, 0:width], stat[:, 0:width]).then_inc(var_ready, 1)
                dve.wait_ge(rstd_ready, roots.next())

            def term(kt, cols, scale):
                dve.scalar_tensor_tensor(out=y[:, kt, cols], in0=xt[:, kt, cols], scalar=scale[:, kt:kt + 1],
                                         in1=rstd[:, 0:cols.stop - cols.start], op0=ALU.mult, op1=ALU.mult)\
                   .then_inc(term_ready, 1)

            def h_rest(kt, cols, shift=None):
                dve.wait_ge(h_hi_ready, hs.next())
                if shift is None:
                    dve.tensor_tensor(h_lo[:, kt, cols], y[:, kt, cols], fp(h_hi[:, kt, cols]), ALU.subtract)\
                       .then_inc(h_ready, 1)
                else:
                    dve.scalar_tensor_tensor(out=h_lo[:, kt, cols], in0=y[:, kt, cols], scalar=shift[:, kt:kt + 1],
                                             in1=fp(h_hi[:, kt, cols]), op0=ALU.add, op1=ALU.subtract)\
                       .then_inc(h_ready, 1)

            def h_tiles(cols, scale, shift=None):
                for kt in range(4):
                    term(kt, cols, scale)
                for kt in range(KT):
                    if kt + 4 < KT:
                        term(kt + 4, cols, scale)
                    h_rest(kt, cols, shift)

            def residual(src, cols, scale):
                width = cols.stop - cols.start

                def add(kt):
                    dve.wait_ge(y_scaled, ys.at(1, kt + 1))
                    dve.tensor_tensor(xt[:, kt, cols], xt[:, kt, cols], src[:, kt, cols], ALU.add).then_inc(x_ready, 1)

                for kt in range(KT):
                    dve.scalar_tensor_tensor(out=src[:, kt, cols], in0=src[:, kt, cols], scalar=scale[:, kt:kt + 1],
                                             in1=rstd[:, 0:width], op0=ALU.mult, op1=ALU.mult).then_inc(y_scaled, 1)
                    if kt:
                        add(kt - 1)
                add(KT - 1)
                ys.next(KT)
                dve.wait_ge(x_ready, xs.next(KT))

            dve.wait_ge(cact_ready, 4)
            clear_acc()
            mod_part(1)
            finish(1)
            clear_acc()
            dve.wait_ge(mod_ready, 1)
            dve.scalar_tensor_tensor(out=coef[:, 0], in0=mod[:, 1], scalar=1.0, in1=g_mix1,
                                     op0=ALU.add, op1=ALU.mult).then_inc(coef_ready, 1)
            dve.wait_ge(coef_ready, 1)
            inverse(SEQ, D, 1e-6)
            for kt in range(KT):
                term(kt, SB, coef[:, 0])
            mod_part(0)
            finish(0)
            dve.wait_ge(mod_ready, 2)
            for kt in range(KT):
                h_rest(kt, SB, mod[:, 0])
                if kt % 4 == 3 and kt < 4 * LEAD:
                    convert()
            dve.wait_ge(h_ready, KT)
            dve.memset(upad[:, :, 0:CONV_K - 1], 0.0).then_inc(conv_step, 1)
            steps = Count(1)

            def conv(t, n):
                def u(j):
                    return upad[:, ds(t), j:j + SEQ]

                w = lambda j: cwt[:, ds(t), j]
                dst = (cv[:, ds(t), :], cvb[:, :].rearrange("p (a n) -> p a n", a=1))
                for j in range(4 * n, 4 * n + 4):
                    if j in (0, 1, CONV_K):
                        dve.wait_ge(conv_step, steps.at())
                    else:
                        dve.wait_ge(conv_step, steps.at(1, -1))
                    if j == 0:
                        op = dve.tensor_scalar(dst[0], u(0), w(0), cb[:, ds(t)], ALU.mult, ALU.add)
                    elif j == 1:
                        op = dve.tensor_scalar(dst[1], u(1), w(1), None, ALU.mult)
                    elif j < CONV_K:
                        op = dve.scalar_tensor_tensor(out=dst[j % 2], in0=u(j), scalar=w(j), in1=dst[j % 2],
                                                      op0=ALU.mult, op1=ALU.add)
                    else:
                        op = dve.tensor_tensor(dst[0], dst[0], dst[1], ALU.add)
                    op.then_inc(conv_step, 1)
                    steps.next()

            def gated(body, tile):
                if tile is not None:
                    for o in range(2):
                        dve.wait_ge(bank_free[2 + o], banks.had[1].at(1, 1))
                for n in range(8):
                    convert()
                    if tile is not None:
                        conv(tile, n)
                dve.wait_ge(half_used, done.next(8))
                g = banks.close()
                g_read = banks.read
                a = banks.close()
                for o in range(2):
                    dve.wait_ge(bank_free[g + o], g_read)
                    dve.tensor_tensor(upad[:, ds(body * 2 + o), CONV_K - 1:], bank[:, a + o:a + o + 1, 0:SEQ],
                                      sigg[:, o:o + 1], ALU.mult).then_inc(bank_free[a + o], 1)

            gated(0, None)
            with loop(dve, 3, (halves, 8), (done, 8), (banks, 2), (steps, CONV_K + 1)) as i:
                gated(i + 1, i)
            finish(2)
            for o in range(2):
                dve.wait_ge(bank_free[2 + o], banks.had[1].at(1, 1))
            scored, soft_n, exped, outs = (Count() for _ in range(4))

            def softmax_max(parts, tiles, rows):
                dve.wait_ge(s_done, scored.next())
                for o, w, src in parts:
                    dve.scalar_tensor_tensor(out=sm[0:rows, o:o + w], in0=src, scalar=SCALE, in1=mask[0:rows, o:o + w],
                                             op0=ALU.mult, op1=ALU.add).then_inc(soft, 1)
                dve.wait_ge(soft, soft_n.next(len(parts)))
                for o, w, j in tiles:
                    dve.reduce_max(mx[0:rows, j:j + 1], sm[0:rows, o:o + w], AX.X).then_inc(soft, 1)
                dve.wait_ge(soft, soft_n.next(len(tiles)))
                n = len(tiles)
                dve.tensor_scalar(mx[0:rows, 0:n], mx[0:rows, 0:n], -1.0, None, ALU.mult).then_inc(p_masked, 1)

            def softmax_norm(tiles, rows):
                n = len(tiles)
                dve.wait_ge(p_exp, exped.next(n))
                dve.reciprocal(rs[0:rows, 0:n], rs[0:rows, 0:n]).then_inc(soft, 1)
                dve.wait_ge(soft, soft_n.next())
                for o, w, j in tiles:
                    dve.tensor_scalar(sm[0:rows, o:o + w], sm[0:rows, o:o + w], rs[0:rows, j:j + 1], None, ALU.mult)\
                       .then_inc(p_ready, 1)

            def out_rest(head, width):
                dve.wait_ge(o_hi, outs.next())
                dve.tensor_tensor(a_lo[:, ds(head), 0:width], bank[:, B_P:B_P + 1, 0:width],
                                  fp(a_hi[:, ds(head), 0:width]), ALU.subtract).then_inc(o_lo, 1)

            def attend(n, pair, parts, tiles, rows, width):
                if n in (5, 9):
                    out_rest(pair * 2 + n // 9, width)
                if n in (1, 5):
                    softmax_max(parts, tiles, rows)
                if n in (2, 7):
                    softmax_norm(tiles, rows)

            attend1 = lambda n, pair: attend(n, pair, [(0, 512, bank[:, B_S, :])], [(0, SEQ, 0), (SEQ, SEQ, 1)],
                                             128, SEQ)

            def heads1(pair, tile):
                banks.pair = 0
                for n in range(12):
                    convert()
                    if pair is not None:
                        attend1(n, pair)
                    if n < 8:
                        conv(tile, n)
                done.next(12)
                for _ in range(3):
                    banks.close()

            heads1(None, 3)
            with loop(dve, 3, (halves, 12), (done, 12), (banks, 3), (steps, CONV_K + 1), (scored, 2), (soft_n, 8),
                      (exped, 4), (outs, 2)) as i:
                heads1(i, i + 4)

            def add_group(dst, first):
                b = banks.close()
                for o in range(2):
                    dve.tensor_tensor(dst[:, first + o, SB], dst[:, first + o, SB], bank[:, b + o, 0:SEQ], ALU.add)\
                       .then_inc(bank_free[b + o], 1)

            for n in range(16):
                convert()
                if n <= 8:
                    attend1(n, 3)
                if n == 8:
                    attend1(9, 3)
                if n < 8:
                    conv(AT - 1, n)
                if n == 7:
                    finish(3)
                if n == 8:
                    done.next(8)
                    for _ in range(8):
                        banks.close()
                if n >= 9:
                    dve.wait_ge(half_used, done.next())
                    add_group(y1, 2 * (n - 9))
                if n == 10:
                    dve.wait_ge(mu_sum, 1)
                    dve.tensor_scalar(stat[:, 0:SEQ], bank[:, B_N, 0:SEQ], 1.0 / DA, None, ALU.mult).then_inc(stat_ready, 1)
                    dve.wait_ge(stat_ready, stats.next())
                    for t in range(AT):
                        dve.tensor_tensor(cv[:, t, :], cv[:, t, :], stat[:, 0:SEQ], ALU.subtract).then_inc(cen_ready, 1)
                if n == 12:
                    inverse(SEQ, DA, 1e-5)
                    for t in range(AT):
                        dve.scalar_tensor_tensor(out=cv[:, t, :], in0=cv[:, t, :], scalar=lng[:, t:t + 1],
                                                 in1=rstd[:, 0:SEQ], op0=ALU.mult, op1=ALU.mult).then_inc(ln_term, 1)
                if n == 13:
                    for t in range(AT):
                        dve.wait_ge(mix_hi, t + 1)
                        dve.tensor_tensor(c_lo[:, t, SB], cv[:, t, :], fp(c_hi[:, t, SB]), ALU.subtract)\
                           .then_inc(mix_ready, 1)
            dve.wait_ge(half_used, done.next())
            add_group(y1, 14)
            finish(4)
            for j in range(8):
                convert()
                convert()
                dve.wait_ge(half_used, done.next(2))
                add_group(y1, 2 * j)
            dve.wait_ge(mod_ready, 5)
            dve.tensor_tensor(coef[:, 1], mod[:, 2], g_mixp1, ALU.mult).then_inc(coef_ready, 1)
            dve.scalar_tensor_tensor(out=coef[:, 2], in0=mod[:, 4], scalar=1.0, in1=g_ffn1,
                                     op0=ALU.add, op1=ALU.mult).then_inc(coef_ready, 1)
            dve.wait_ge(coef_ready, 3)
            inverse(SEQ, D, 1e-6)
            residual(y1, SB, coef[:, 1])
            inverse(SEQ, D, 1e-6)
            h_tiles(SB, coef[:, 2], mod[:, 3])
            hids, taps, nexts, gelus = (Count() for _ in range(4))

            def rest(t):
                for o in range(2):
                    dve.wait_ge(hid_hi_ready, hids.next())
                    dve.tensor_tensor(hid_lo[:, t + o], hid[:, t + o], fp(hid_hi[:, t + o]), ALU.subtract)\
                       .then_inc(hid_lo_ready, 1)

            def down():
                for j in range(8):
                    convert()
                    dve.wait_ge(half_used, done.next())
                    add_group(y, 2 * j)

            def gate1(i, t):
                skip(4, 1)

            def up1(i, t):
                sg_read = banks.free()
                b = group()
                for o in range(2):
                    dve.wait_ge(bank_free[b + o], sg_read)
                    dve.tensor_tensor(hid[:, t + o], bank[:, b + o, 0:SEQ], sg[:, t + o], ALU.mult)\
                       .then_inc(bank_free[b + o], 1)
                rest(t)

            def more_taps(dst, i, b, t, first):
                for k in (1, 2):
                    for o in range(2):
                        if k == 1:
                            dve.wait_ge(tap_ready, taps.next())
                        else:
                            dve.wait_ge(tap_next, nexts.at(1, o + 1))
                        ch = i * 4 + (t + o + first)
                        dve.scalar_tensor_tensor(out=dst[:, t + o:t + o + 1, :], in0=bank[:, b + o:b + o + 1, k:k + SEQ],
                                                 scalar=pcol[:, 4 + k, ds(ch)], in1=dst[:, t + o:t + o + 1, :],
                                                 op0=ALU.mult, op1=ALU.add)\
                           .then_inc(tap_next if k == 1 else bank_free[b + o], 1)
                nexts.next(2)

            def gate2(i, t):
                more_taps(sg, i, group(), t, 0)

            def up2(i, t):
                b = group()
                more_taps(va, i, b, t, FT)
                for o in range(2):
                    dve.wait_ge(bank_free[b + o], banks.read)
                    dve.wait_ge(gelu_ready, gelus.next())
                    dve.tensor_tensor(hid[:, t + o], va[:, t + o], sg[:, t + o], ALU.mult).then_inc(hid_ready, 1)
                rest(t)

            def ffn(gate, up, n_taps, with_ada):
                def chunk(i, read):
                    for g in range(2):
                        read(i, 2 * g)
                chunk(0, gate)
                chunk(0, up)
                with loop(dve, NCHUNK - 1, (halves, 24), (done, 24), (banks, 12), (hids, 4), (taps, 2 * n_taps),
                          (nexts, 2 * n_taps), (gelus, n_taps)) as i:
                    chunk(i + 1, gate)
                    down()
                    chunk(i + 1, up)
                if with_ada:
                    finish(5)
                    dve.wait_ge(mod_ready, 6)
                    dve.tensor_tensor(coef[:, 3], mod[:, 5], g_ffnp1, ALU.mult).then_inc(coef_ready, 1)
                    dve.wait_ge(coef_ready, 4)
                down()

            dve.wait_ge(y_zero, 1)
            ffn(gate1, up1, 0, 1)
            inverse(SEQ, D, 1e-6)
            residual(y, SB, coef[:, 3])
            inverse(ALL, D, 1e-6)
            h_tiles(slice(0, ALL), g_mix2)
            skip(2, 0)
            dve.wait_ge(f_step, 4)
            dve.wait_ge(pads, 3)
            dve.scalar_tensor_tensor(out=lf[0][:, 256:], in0=lf[1][:, 256:], scalar=0.0, in1=sc_in[:, :],
                                     op0=ALU.min, op1=ALU.subtract).then_inc(scan, 1)
            for n in range(9):
                dve.wait_ge(scan, n + 1)
                a, b, s = lf[n % 2], lf[(n + 1) % 2], 1 << n
                dve.tensor_tensor(b[:, 256:], a[:, 256:], a[:, 256 - s:256 + ALL - s], ALU.add).then_inc(scan, 1)
            for j in range(3):
                ref = 256 + LIVE0 + QT * (j + 1) - 1
                dve.wait_ge(scan, 10)
                dve.tensor_scalar(rel[:, j, :], lf[1][:, 256:], lf[1][:, ref:ref + 1], None, ALU.subtract)\
                   .then_inc(rel_ready, 1)
            attend2 = lambda n, pair: attend(
                n, pair, [(0, 384, bank[0:QT, B_S, 0:384]), (384, 272, bank[0:QT, B_N, 0:272])],
                [(QO[j], QW[j], j) for j in range(3)], QT, LIVE)
            skip(16, 4)
            dve.wait_ge(consts, 9)
            with loop(dve, 3, (halves, 16), (done, 16), (banks, 4), (scored, 2), (soft_n, 12), (exped, 6), (outs, 2)) as i:
                for n in range(16):
                    convert()
                    attend2(n, i)
                done.next(16)
                for _ in range(4):
                    banks.close()
            n_win = 0
            u_read = [banks.had[b // 2].at(1, 1) for b in range(4)]

            def window(t):
                nonlocal n_win
                w = WINDOWS[t // 2]
                last, s = u2[:, t, :], 1
                if t == 0:
                    for b in range(4):
                        dve.wait_ge(bank_free[b], u_read[b])
                k = 0
                while s < w:
                    dst = win[:, k % 2, :]
                    if n_win:
                        dve.wait_ge(win_step, n_win)
                    lo = 2 * s - 1
                    dve.tensor_tensor(dst[:, lo:], last[:, lo:], last[:, lo - s:META + ALL - s], ALU.add)\
                       .then_inc(win_step, 1)
                    n_win += 1
                    last, s, k = dst, 2 * s, k + 1
                dve.wait_ge(win_step, n_win)
                if t >= 2:
                    dve.wait_ge(d_lo_ready, t - 1)
                full = slice(META + LIVE0, META + ALL)
                args = dict(op0=ALU.mult, op1=ALU.subtract)
                if LIVE0 + 1 < w:
                    dve.scalar_tensor_tensor(out=sq[:, t % 2, 0:1], in0=last[:, full.start:full.start + 1],
                                             scalar=1.0 / (LIVE0 + 1), in1=u2[:, t, full.start:full.start + 1], **args)\
                       .then_inc(win_step, 1)
                    n_win += 1
                    dve.scalar_tensor_tensor(out=sq[:, t % 2, 1:LIVE], in0=last[:, full.start + 1:full.stop],
                                             scalar=1.0 / w, in1=u2[:, t, full.start + 1:full.stop], **args)\
                       .then_inc(d_ready, 1)
                else:
                    dve.scalar_tensor_tensor(out=sq[:, t % 2, 0:LIVE], in0=last[:, full], scalar=1.0 / w,
                                             in1=u2[:, t, full], **args).then_inc(d_ready, 1)

            def attn_part():
                b = banks.close()
                for o in range(2):
                    dve.tensor_tensor(ga_s[:, o:o + 1], bank[:, b + o:b + o + 1, 0:LIVE], ga_s[:, o:o + 1], ALU.mult)\
                       .then_inc(bank_free[b + o], 1)
                return b, banks.read

            for n in range(10):
                convert()
                if n <= 8:
                    attend2(n, 3)
                if n == 8:
                    attend2(9, 3)
                if 1 <= n <= 8:
                    dve.wait_ge(d_hi_ready, n)
                    dve.tensor_tensor(d_lo[:, n - 1], sq[:, (n - 1) % 2, 0:LIVE], fp(d_hi[:, n - 1]), ALU.subtract)\
                       .then_inc(d_lo_ready, 1)
                if n < 8:
                    window(n)

            def gates_done():
                for _ in range(2):
                    b = banks.close()
                    for o in range(2):
                        dve.wait_ge(bank_free[b + o], banks.read)

            done.next(8)
            gates_done()
            dve.wait_ge(half_used, done.next(2))
            attn = attn_part()
            for t in range(AT):
                if t % 4 == 0:
                    skip(1, 2)
                dve.wait_ge(pl_hi_ready, t + 1)
                dve.tensor_tensor(pl_lo[:, t], sq[:, t % 2, 0:LIVE], fp(pl_hi[:, t]), ALU.subtract).then_inc(pl_lo_ready, 1)
            ms, pools = Count(), Count()

            def mix(body, attn):
                b = group(2)
                for o in range(2):
                    dve.tensor_tensor(gp_s[:, o:o + 1], bank[:, b + o:b + o + 1, 0:LIVE], gp_s[:, o:o + 1], ALU.mult)\
                       .then_inc(bank_free[b + o], 1)
                for o in range(2):
                    dve.wait_ge(bank_free[b + o], banks.read)
                    dve.tensor_tensor(gp_s[:, o:o + 1], gp_s[:, o:o + 1], ga_s[:, o:o + 1], ALU.add).then_inc(m_ready, 1)
                for o in range(2):
                    dve.wait_ge(m_hi_ready, ms.next())
                    t = ds(body * 2 + o)
                    dve.tensor_tensor(m_lo[:, t], gp_s[:, o:o + 1], fp(m_hi[:, t]), ALU.subtract).then_inc(m_lo_ready, 1)

            with loop(dve, 7, (halves, 12), (done, 12), (banks, 4), (ms, 2)) as i:
                mix(i, attn)
                for _ in range(8):
                    convert()
                done.next(8)
                gates_done()
                convert()
                convert()
                dve.wait_ge(half_used, done.next(2))
                attn_part()
            mix(7, attn)
            with loop(dve, 4, (halves, 8), (done, 8), (banks, 2)) as i:
                skip(8, 2)
            inverse(LIVE, D, 1e-6)
            residual(y2, ST, g_mixp2)
            inverse(LIVE, D, 1e-6)
            h_tiles(ST, g_ffn2)
            dve.wait_ge(y_zero, 2)
            ffn(gate2, up2, 4, 0)
            inverse(SEQ, D, 1e-6)
            residual(y, SB, g_ffnp2)

        @block.tensor
        def _(pe):
            halves, banks = Count(), Banks()

            def half(x_hi, x_lo, kts, width, first, last, fixed=None):
                slot = halves.mod(RING)
                b = banks.bank() if fixed is None else fixed
                pe.wait_ge(lo_ready, halves.at(1, RING + 1))
                if first and fixed is None:
                    for o in range(2):
                        pe.wait_ge(bank_free[b + o], banks.free())
                for k, kt in enumerate(kts):
                    for o in range(2 if fixed is None else 1):
                        tile = (k, o) if fixed is None else (k // 2, k % 2)
                        wh = w_hi[:, slot, tile[0], tile[1] * 128:tile[1] * 128 + 128]
                        wl = w_lo[:, slot, tile[0], tile[1] * 128:tile[1] * 128 + 128]
                        dst = bank[:, b + o, 0:width]
                        pe.matmul(dst, wh, x_hi(kt), start=first and k == 0, stop=False)
                        pe.matmul(dst, wh, x_lo(kt), start=False, stop=False)
                        mm = pe.matmul(dst, wl, x_hi(kt), start=False, stop=last and k == len(kts) - 1)
                mm.then_inc(half_used, 1)
                halves.next()
                if last and fixed is None:
                    banks.close()

            def product(x_hi, x_lo, cols, n_kt=KT, kt0=0, ready=None):
                for q in range(n_kt // 4):
                    quarter(q, x_hi, x_lo, cols, n_kt, kt0, ready)

            def quarter(q, x_hi, x_lo, cols, n_kt=KT, kt0=0, ready=None):
                if ready is not None:
                    pe.wait_ge(ready[0], ready[1] + 4 * q + 4)
                half(lambda kt: x_hi[:, kt, cols], lambda kt: x_lo[:, kt, cols],
                     range(kt0 + 4 * q, kt0 + 4 * q + 4), cols.stop - cols.start, q == 0, q == n_kt // 4 - 1)

            used = Count()

            def turn(pairs):
                n = used.c
                if n >= 4:
                    pe.wait_ge(tr_copied, n - 3)
                for dst, src in pairs:
                    rows = src.shape[0]
                    mm = pe.transpose(dst(bank[:, B_S + n % 4, :]), src, ident[0:rows, 0:rows])
                mm.then_inc(tr_done, 1)
                used.next()

            pe.wait_ge(consts, 3)
            pe.wait_ge(c_loaded, 48)
            turn([(lambda b: b[:, 0:120], prow[0:120, 0])])
            pe.wait_ge(rows_loaded, 16 * 23)
            for n in range(8):
                t, j = n // 4, n % 4
                turn([(lambda b, a=a: b[:, 128 * a:128 * a + 128], xrow[:, t, 512 * j + 128 * a:512 * j + 128 * a + 128])
                      for a in range(4)])
            turn([(lambda b: b[:, 0:88], prow[0:88, 1])])
            turn([(lambda b: b[:, 0:128], prow[:, 2])])
            turn([(lambda b, a=a: b[:, 128 * a:128 * a + 88], prow[0:88, 3 + a]) for a in range(4)])
            turn([(lambda b, a=a: b[:, META * a:META * a + META], mrow[:, 128 * a:128 * a + 128]) for a in range(KT)])
            turn([(lambda b, a=a: b[:, 32 * a:32 * a + CONV_K], cwrow[:, 128 * a:128 * a + 128]) for a in range(AT)])
            sqs = Count()

            def channel_sum(kt, width, n=KT):
                pe.wait_ge(sq_ready, sqs.next())
                pe.matmul(bank[:, B_N, 0:width], ones[:, :], sq[:, kt % 2, 0:width],
                          start=kt == 0, stop=kt == n - 1).then_inc(sq_used, 1)

            def channel_sums(width, n=KT):
                for kt in range(n):
                    channel_sum(kt, width, n)

            def ada_total(acc):
                for j in range(KT):
                    mm = pe.matmul(bank[:, B_N, 496 + j:497 + j], acc[:, 128 * j:128 * j + 128], ones[:, 0:1],
                                   start=True, stop=True)
                mm.then_inc(ada_sum, 1)

            pe.wait_ge(tr_copied, 14)
            channel_sums(SEQ)
            for n in range(2):
                pe.wait_ge(pre_used, 4 + 16 * (n + 1))
                if n:
                    pe.wait_ge(mod_ready, n)
                ada_total(acc)
            with loop(pe, 4, (halves, 8), (banks, 2)):
                for n in range(2):
                    product(h_hi, h_lo, SB, ready=(h_ready, 0))
            pe.wait_ge(ada_used, 16)
            ada_total(acc)
            probs_n, ptc, vtc, sels = Count(), Count(), Count(), Count()

            def scores(tiles, v_parts):
                for n, mats in enumerate(tiles):
                    for m, (dst, lhs, rhs) in enumerate(mats):
                        mm = pe.matmul(dst, lhs, rhs, start=m == 0, stop=m == len(mats) - 1)
                mm.then_inc(s_done, 1)
                for dst, src in v_parts:
                    mm = pe.transpose(dst, src, ident[:, :])
                mm.then_inc(v_done, 1)

            def turn_p(n_tiles, parts):
                pe.wait_ge(p_ready, probs_n.next(n_tiles))
                for dst, src in parts:
                    rows = src.shape[0]
                    mm = pe.transpose(dst, src, ident[0:rows, 0:rows])
                mm.then_inc(pt_done, 1)

            def weigh(n_pt, n_v, parts):
                pe.wait_ge(pt_copied, ptc.next(n_pt))
                pe.wait_ge(v_copied, vtc.next(n_v))
                for m, (dst, v, p) in enumerate(parts):
                    mm = pe.matmul(dst, v, p, start=m == 0, stop=m == len(parts) - 1)
                mm.then_inc(o_done, 1)

            B = lambda b, lo, hi, rows=128: bank[0:rows, b, lo:hi]

            def attend1(n, v_ready):
                q, k, v = (lambda o, j=j: qkv[:, j, o, SB] for j in range(3))

                def head(o):
                    scores([[(B(B_S, 256 * j, 256 * j + 256), q(o)[:, 128 * j:128 * j + 128], k(o))] for j in range(2)],
                           [(B(B_V, 128 * t, 128 * t + 128), v(o)[:, 128 * t:128 * t + 128]) for t in range(2)])

                if n == 1:
                    for o in range(2):
                        pe.wait_ge(bank_free[o], v_ready)
                    head(0)
                if n in (4, 8):
                    turn_p(2, [(B(B_P, 0, 128), sm[:, 0:128]), (B(B_P, 128, 256), sm[:, 256:384]),
                               (B(B_P, 256, 384), sm[:, 384:512])])
                if n in (5, 9):
                    weigh(1, 1, [(B(B_P, 0, 256), v_t[:, 0, :], p_t[:, 0:256]),
                                 (B(B_P, 128, 256), v_t[:, 1, :], p_t[:, 256:384])])
                if n == 5:
                    head(1)

            def heads1(attended):
                banks.pair = 0
                v_ready = banks.had[0].at(1, 1)
                for n in range(12):
                    if attended:
                        attend1(n, v_ready)
                    quarter(n % 4, h_hi, h_lo, SB)

            heads1(False)
            with loop(pe, 3, (halves, 12), (banks, 3), (probs_n, 4), (ptc, 2), (vtc, 2)):
                heads1(True)
            pe.wait_ge(ada_used, 32)
            pe.wait_ge(mod_ready, 3)
            ada_total(acc_b)
            v_ready = banks.had[0].at(1, 1)
            for n in range(16):
                if n <= 8:
                    attend1(n, v_ready)
                if n == 8:
                    pe.wait_ge(conv_step, 1 + AT * (CONV_K + 1))
                    pe.wait_ge(mod_ready, 4)
                    for t in range(AT):
                        mm = pe.matmul(bank[:, B_N, 0:SEQ], ones[:, :], cv[:, t, :], start=t == 0, stop=t == AT - 1)
                    mm.then_inc(mu_sum, 1)
                    attend1(9, v_ready)
                    pe.wait_ge(o_lo, HEADS)
                if n == 11:
                    channel_sums(SEQ, AT)
                if n == 0:
                    pe.wait_ge(o_lo, HEADS // 2)
                half(lambda kt: a_hi[:, kt, 0:SEQ], lambda kt: a_lo[:, kt, 0:SEQ],
                     range(n // 8 * 4, n // 8 * 4 + 4), SEQ, True, True)
            pe.wait_ge(ada_used, 48)
            pe.wait_ge(ln_term, 1)
            ada_total(acc)
            for j in range(8):
                for q in range(2):
                    quarter(q, c_hi, c_lo, SB, AT, ready=(mix_ready, 0))
                    if q == 0 and j:
                        for o in range(2):
                            if j == 1 and o == 0:
                                pe.wait_ge(mod_ready, 5)
                            channel_sum(2 * j - 2 + o, SEQ)
            channel_sum(14, SEQ)
            channel_sum(15, SEQ)
            channel_sums(SEQ)
            downs = Count()

            def ffn(cols, h_base, with_ada):
                def chunk(ready=None):
                    for g in range(2):
                        product(h_hi, h_lo, cols, ready=ready)

                def down():
                    pe.wait_ge(hid_lo_ready, downs.next(4))
                    for j in range(8):
                        half(lambda kt: hid_hi[:, kt], lambda kt: hid_lo[:, kt], range(4), SEQ, True, True)

                chunk((h_ready, h_base))
                chunk()
                with loop(pe, NCHUNK - 1, (halves, 24), (banks, 12), (downs, 4)):
                    chunk()
                    down()
                    chunk()
                if with_ada:
                    pe.wait_ge(ada_used, 64)
                    ada_total(acc)
                    pe.wait_ge(mod_ready, 6)
                pe.wait_ge(hid_lo_ready, downs.next(4))
                for j in range(8):
                    half(lambda kt: hid_hi[:, kt], lambda kt: hid_lo[:, kt], range(4), SEQ, True, True)
                    if j:
                        for o in range(2):
                            channel_sum(2 * j - 2 + o, SEQ)
                channel_sum(14, SEQ)
                channel_sum(15, SEQ)

            ffn(SB, KT, True)
            every, narrow = slice(0, ALL), slice(0, LIVE)
            channel_sums(ALL)
            for q in range(2):
                pe.wait_ge(h_ready, 2 * KT + 8 * q + 8)
                half(lambda kt: h_hi[:, kt, :], lambda kt: h_lo[:, kt, :], range(8 * q, 8 * q + 8), ALL,
                     q == 0, q == 1, fixed=B_N)

            def attend2(n, v_ready):
                def head(o):
                    pe.wait_ge(sel_ready, sels.next())
                    q, k, v = (qkv[:, j, o, :] for j in range(3))
                    dst = (B(B_S, 0, 128, QT), B(B_S, 128, 384, QT), B(B_N, 0, 272, QT))
                    scores([[(dst[j], q[:, LIVE0 + QT * j:LIVE0 + QT * j + QT], k[:, 0:QW[j]]),
                             (dst[j], sel[:, o, :], rel[:, j, 0:QW[j]])] for j in range(3)],
                           [(B(B_V, 128 * t, 128 * t + 128, min(128, ALL - 128 * t)),
                             v[:, 128 * t:min(128 * t + 128, ALL)]) for t in range(3)])

                if n == 1:
                    for b in range(4):
                        pe.wait_ge(bank_free[b], v_ready[b // 2])
                    head(0)
                if n in (4, 8):
                    P = lambda j, k, w=128: sm[0:QT, QO[j] + 128 * k:QO[j] + 128 * k + w]
                    turn_p(3, [(B(B_P, 0, QT), P(0, 0)), (B(B_P, QT, 2 * QT), P(1, 0)),
                               (B(B_P, 2 * QT, 3 * QT), P(2, 0)), (B(B_P, 3 * QT, 4 * QT), P(1, 1)),
                               (B(B_P, 4 * QT, 5 * QT), P(2, 1)), (B(B_V, 384, 384 + QT, META), P(2, 2, META))])
                if n in (5, 9):
                    weigh(2, 2, [(B(B_P, 0, LIVE), v_t[:, 0, :], p_t[:, 0:3 * QT]),
                                 (B(B_P, QT, LIVE), v_t[:, 1, :], p_t[:, 3 * QT:5 * QT]),
                                 (B(B_P, 2 * QT, LIVE), v_t[0:META, 2, :], p_t[0:META, 5 * QT:6 * QT])])
                if n == 5:
                    head(1)

            for n in range(16):
                quarter(n % 4, h_hi, h_lo, every)
            pe.wait_ge(rel_ready, 3)
            with loop(pe, 3, (halves, 16), (banks, 4), (sels, 2), (probs_n, 6), (ptc, 4), (vtc, 4)):
                v_ready = [banks.had[n].at(1, 1) for n in range(2)]
                for n in range(16):
                    attend2(n, v_ready)
                    quarter(n % 4, h_hi, h_lo, every)
            v_ready = [banks.had[n].at(1, 1) for n in range(2)]
            for n in range(10):
                attend2(n, v_ready)
                if n < 8:
                    quarter(n % 4, h_hi, h_lo, ST)
            pe.wait_ge(o_lo, 2 * HEADS)
            product(a_hi, a_lo, narrow, AT)
            for h in range(2):
                slot = halves.mod(RING)
                pe.wait_ge(lo_ready, halves.at(1, RING + 1))
                pe.wait_ge(d_lo_ready, 4 * h + 4)
                for g in range(2):
                    b = banks.bank()
                    for o in range(2):
                        pe.wait_ge(bank_free[b + o], banks.free())
                        for k in range(2):
                            wh = w_hi[:, slot, 2 * g + k, o * 128:o * 128 + 128]
                            wl = w_lo[:, slot, 2 * g + k, o * 128:o * 128 + 128]
                            t = 4 * h + 2 * g + k
                            dst = bank[:, b + o, 0:LIVE]
                            pe.matmul(dst, wh, d_hi[:, t], start=k == 0, stop=False)
                            pe.matmul(dst, wh, d_lo[:, t], start=False, stop=False)
                            mm = pe.matmul(dst, wl, d_hi[:, t], start=False, stop=k == 1)
                    banks.close()
                mm.then_inc(half_used, 1)
                halves.next()
            with loop(pe, 7, (halves, 12), (banks, 4)):
                product(pl_hi, pl_lo, narrow, AT, ready=(pl_lo_ready, 0))
                product(h_hi, h_lo, ST)
                product(h_hi, h_lo, ST)
                product(a_hi, a_lo, narrow, AT)
            product(pl_hi, pl_lo, narrow, AT)
            pe.wait_ge(m_lo_ready, KT)
            with loop(pe, 3, (halves, 8), (banks, 2)):
                for n in range(2):
                    product(m_hi, m_lo, narrow)
            for n in range(8):
                quarter(n % 4, m_hi, m_lo, narrow)
                if n < 6:
                    for o in range(2):
                        channel_sum(2 * n + o, LIVE)
            for kt in range(12, KT):
                channel_sum(kt, LIVE)
            channel_sums(LIVE)
            ffn(ST, 3 * KT, False)
            for n in range(8):
                t, j = n // 4, n % 4
                pe.wait_ge(x_ready, X_TOTAL)
                if n >= 4:
                    pe.wait_ge(last_copied, n - 3)
                for a in range(4):
                    mm = pe.transpose(bank[:, B_S + n % 4, 128 * a:128 * a + 128],
                                      xt[:, 4 * j + a, META + 128 * t:META + 128 * t + 128], ident[:, :])
                mm.then_inc(last_done, 1)


_INS = ['x', 'c', 'ada_w', 'ada_b', 'mix_pre_g', 'mix_post_g', 'w_in', 'conv_w', 'conv_b', 'conv_ln_g',
        'conv_ln_b', 'w_out', 'ffn_pre_g', 'ffn_post_g', 'w_gate', 'w_up', 'w_down', 'meta_tokens_2',
        'mix_pre_g_2', 'w_in_2', 'b_in_2', 'w_attn_o_2', 'pool_w_2', 'pool_scale_2', 'w_pool_o_2', 'w_out_2',
        'mix_post_g_2', 'ffn_pre_g_2', 'w_ffn_up_2', 'ffn_conv_w_2', 'ffn_conv_b_2', 'w_ffn_down_2',
        'ffn_post_g_2']


def kernel(**inputs):
    import numpy as _np
    import concourse.bacc as _bacc
    from concourse.bass_utils import run_bass_kernel_spmd as _run

    nc = _bacc.Bacc("TRN2", target_bir_lowering=False, num_devices=1)
    arrays, args = {}, []
    for name in _INS:
        a = _np.ascontiguousarray(inputs[name])
        if a.shape[0] == 1:
            a = a.reshape(a.shape[1:])
        arrays[f"in_{name}"] = a
        args.append(nc.dram_tensor(f"in_{name}", a.shape, mybir.dt.float32, kind="ExternalInput").ap())
    args.append(nc.dram_tensor("out", (SEQ, D), mybir.dt.float32, kind="ExternalOutput").ap())
    build(nc, *args)
    r = _run(nc, [arrays], core_ids=[0])
    return r.results[0]["out"].reshape(1, SEQ, D)
```

```python
import concourse.bass as bass
from concourse import mybir
from contextlib import ExitStack, contextmanager

D = 2048
KT = D // 128
SEQ, META = 256, 16
ALL = SEQ + META
LIVE0 = META - 2
LIVE = ALL - LIVE0
HD, HEADS = 128, 8
DA = HD * HEADS
AT = DA // 128
CONV_K = 31
F = 5632
FT = F // 128
CHUNK = 512
NCHUNK = F // CHUNK
MODS = 6
SCALE = HD ** -0.5
NEG = -1e30
RING = 4
LEAD = 3
QT = LIVE // 3
QW = (128, 256, 272)
QO = (0, 128, 384)
QSUM = sum(QW)
WINDOWS = (2, 4, 8, 16)
FFN_HALVES = NCHUNK * 24
HALVES = 112 + FFN_HALVES + 2 + 64 + 96 + 2 + 32 + FFN_HALVES
POOL_X = [kt % 3 != 2 and kt < KT - 1 for kt in range(KT)]

ADA_ROW = [(2, a) for a in range(KT)] + [(3 + r // 3, 3 * b + r % 3) for b in range(4) for r in range(6)] \
    + [(3 + r // 4, 12 + r % 4) for r in range(8)] + [(5, a) for a in range(KT)]
ADA_RING = 4
ADA_SLOT = [a % 4 for a in range(KT)] + [r % 3 for r in range(24)] + [r % 4 for r in range(8)] \
    + [a % 4 if a < KT - (NCHUNK - 1) else 0 for a in range(KT)]
ADA_TAIL = (0, 1, 3, 4, 6, 7, 9, 10)
DVE_COL = 1664

SB, ST = slice(META, ALL), slice(LIVE0, ALL)


class Count:

    def __init__(self, start=0):
        self.c, self.i, self.per, self.c0 = start, None, 0, 0

    def enter(self, i, per):
        self.i, self.per, self.c0 = i, per, self.c

    def leave(self, trips):
        assert self.c - self.c0 == self.per, (self.c - self.c0, self.per)
        self.c, self.i = self.c0 + self.per * trips, None

    def at(self, mult=1, add=0):
        base = self.c * mult + add
        return base if self.i is None or not self.per else self.i * (self.per * mult) + base

    def div(self, d, mult, add):
        base = (self.c // d) * mult + add
        if self.i is None or not self.per:
            return base
        assert self.per % d == 0
        return self.i * (self.per // d * mult) + base

    def mod(self, d):
        assert self.i is None or self.per % d == 0
        return self.c % d

    def next(self, n=1, mult=1, add=0):
        self.c += n
        return self.at(mult, add)


class Banks:

    def __init__(self):
        self.had, self.pair, self.read = [Count(), Count()], 0, None

    def bank(self):
        return 2 * self.pair

    def free(self):
        return self.had[self.pair].at(1, 1)

    def close(self):
        b, self.read = self.bank(), self.had[self.pair].at(1, 2)
        self.had[self.pair].next()
        self.pair ^= 1
        return b


def wait_x(eng, kt, n, x_ready, x_added):
    if POOL_X[kt]:
        eng.wait_ge(x_added, n * sum(POOL_X) + sum(POOL_X[:kt + 1]))
    else:
        eng.wait_ge(x_ready, n * (KT - sum(POOL_X)) + kt + 1 - sum(POOL_X[:kt + 1]))


@contextmanager
def loop(eng, trips, *counts):
    flat = []
    for c, per in counts:
        if isinstance(c, Banks):
            flat += [(c.had[0], (per + 1) // 2), (c.had[1], per // 2)]
        else:
            flat.append((c, per))
    counts = flat
    with eng.Fori(0, trips) as i:
        for c, per in counts:
            c.enter(i, per)
        yield i
    for c, _ in counts:
        c.leave(trips)


def ds(start, size=1):
    return bass.ds(start, size)


def build(nc, x, c, ada_w, ada_b, mix_pre_g, mix_post_g, w_in, conv_w, conv_b, conv_ln_g, conv_ln_b,
          w_out, ffn_pre_g, ffn_post_g, w_gate, w_up, w_down, meta_tokens_2, mix_pre_g_2, w_in_2,
          b_in_2, w_attn_o_2, pool_w_2, pool_scale_2, w_pool_o_2, w_out_2, mix_post_g_2,
          ffn_pre_g_2, w_ffn_up_2, ffn_conv_w_2, ffn_conv_b_2, w_ffn_down_2, ffn_post_g_2, out):
    f32, f32r = mybir.dt.float32, mybir.dt.float32r
    ACT, ALU, AX = mybir.ActivationFunctionType, mybir.AluOpType, mybir.AxisListType
    ctx = ExitStack()
    with ctx:
        base = (nc.sbuf_base + 31) // 32 * 32
        sizes = dict(raw=RING * 4096, hi=RING * 4096, lo=RING * 4096, xt=KT * ALL * 4,
                     hhi=KT * ALL * 4, hlo=KT * ALL * 4, r1=KT * ALL * 4, r2=38400, r3=40960)
        at, region = 0, {}
        for name, size in sizes.items():
            region[name] = at
            at += size
        ctx.enter_context(nc.sbuf_tensor("arena", [128, at + 32], mybir.dt.uint8))

        def place(name, reg, off, shape, dt=f32):
            n = 4
            for s in shape[1:]:
                n *= s
            spans = {"hhi": ("hhi", "hlo")}.get(reg, (reg,))
            assert off + n <= sum(sizes[r] for r in spans), name
            return nc.alloc_sbuf_tensor_at(name, shape, dt, offset=base + region[reg] + off, align_bytes=4)

        def sb(name, shape, dt=f32):
            return ctx.enter_context(nc.sbuf_tensor(name, shape, dt))

        def sem(name):
            return ctx.enter_context(nc.semaphore(name))

        raw = place("raw", "raw", 0, [128, RING, 4, 256])
        w_hi = place("w_hi", "hi", 0, [128, RING, 4, 256], f32r)
        w_lo = place("w_lo", "lo", 0, [128, RING, 4, 256], f32r)
        xt = place("xt", "xt", 0, [128, KT, ALL])
        h_hi = place("h_hi", "hhi", 0, [128, KT, ALL], f32r)
        h_lo = place("h_lo", "hlo", 0, [128, KT, ALL], f32r)
        ada_pre = place("ada_pre", "hhi", 0, [128, 4, D])
        y = place("y", "r1", 0, [128, KT, ALL])
        upad = place("upad", "r1", 0, [128, AT, CONV_K - 1 + SEQ])
        cv = place("cv", "r1", AT * (CONV_K - 1 + SEQ) * 4, [128, AT, SEQ])
        y1 = place("y1", "hhi", 0, [128, KT, ALL])
        c_hi = place("c_hi", "hlo", 0, [128, AT, ALL], f32r)
        c_lo = place("c_lo", "hlo", AT * ALL * 4, [128, AT, ALL], f32r)
        m_hi = place("m_hi", "r1", 0, [128, KT, LIVE], f32r)
        u2 = place("u2", "r1", 0, [128, AT, META + ALL])
        xrow = place("xrow", "r2", 0, [128, 2, D])
        mrow = place("mrow", "r2", 16384, [META, D])
        cwrow = place("cwrow", "r2", 24576, [CONV_K, DA])
        prow = place("prow", "r2", 28672, [128, 7, 128])
        a1_hi = place("a1_hi", "r2", 0, [128, AT, SEQ], f32r)
        a1_lo = place("a1_lo", "r2", 8192, [128, AT, SEQ], f32r)
        qkv1 = place("qkv1", "r2", 16384, [128, 3, 2, SEQ])
        sm1 = place("sm1", "r2", 22528, [128, 2 * SEQ])
        v_t1 = place("v_t1", "r2", 24576, [128, 2, 128])
        p_t1 = place("p_t1", "r2", 25600, [128, 384])
        acc_b = place("acc_b", "r2", 27136, [128, D])
        sigg = place("sigg", "r2", 35328, [128, 2, SEQ])
        cvb = place("cvb", "r2", 37376, [128, SEQ])
        a_hi = place("a_hi", "r2", 0, [128, AT, ALL], f32r)
        a_lo = place("a_lo", "r2", AT * ALL * 4, [128, AT, ALL], f32r)
        y2 = place("y2", "r2", 0, [128, KT, ALL])
        m_lo = place("m_lo", "r2", 2 * AT * ALL * 4, [128, KT, LIVE], f32r)
        hid = place("hid", "r2", 0, [128, 4, SEQ])
        sg = place("sg", "r2", 4096, [128, 4, SEQ])
        va = place("va", "r2", 8192, [128, 4, SEQ])
        hid_hi = place("hid_hi", "r2", 12288, [128, 4, SEQ], f32r)
        hid_lo = place("hid_lo", "r2", 16384, [128, 4, SEQ], f32r)
        outrow = place("outrow", "r2", 0, [128, 2, D])
        qkv = place("qkv", "r2", 17408, [128, 3, 2, ALL])
        sm = place("sm", "r2", 23936, [128, QSUM])
        v_t = place("v_t", "r2", 26560, [128, 3, 128])
        p_t = place("p_t", "r2", 28096, [128, 6 * QT])
        win = place("win", "r2", 34048, [128, 2, META + ALL])
        ada_raw = place("ada_raw", "r3", 0, [128, ADA_RING, D])
        acc = place("acc", "r3", ADA_RING * 8192, [128, D])
        pl_hi = place("pl_hi", "r3", 0, [128, AT, LIVE], f32r)
        pl_lo = place("pl_lo", "r3", AT * LIVE * 4, [128, AT, LIVE], f32r)
        d_hi, d_lo = pl_hi, pl_lo
        lf = [place(f"lf{n}", "r3", 16512 + n * 2112, [HEADS, 256 + ALL]) for n in range(2)]
        sc_in = place("sc_in", "r3", 16512 + 4224, [HEADS, ALL])
        rel = place("rel", "r3", 16512 + 5312, [HEADS, 3, ALL])
        ga_s = place("ga_s", "r3", 16512, [128, 2, LIVE])
        gp_s = place("gp_s", "r3", 16512 + 2064, [128, 2, LIVE])
        pcol = sb("pcol", [128, 7, 128])
        cwt = sb("cwt", [128, AT, CONV_K + 1])
        ident = sb("ident", [128, 128])
        ones = sb("ones", [128, 128])
        eps = sb("eps", [128, 2])
        mask = sb("mask", [128, QSUM])
        sq = sb("sq", [128, 2, ALL])
        rstd = sb("rstd", [128, ALL])
        stat = sb("stat", [128, ALL])
        mod = sb("mod", [128, MODS, KT])
        cact = sb("cact", [128, KT])
        coef = sb("coef", [128, 4, KT])
        sel = sb("sel", [HEADS, 2, QT])
        pick = sb("pick", [HEADS, HEADS])
        bf = sb("bf", [HEADS, 1])
        mx = sb("mx", [128, 3])
        rs = sb("rs", [128, 3])
        bank = ctx.enter_context(nc.psum_tensor("bank", [128, 8, 512], f32))
        B_S, B_N, B_P, B_V = 4, 5, 6, 7

        adab, ccol, pscale = pcol[:, 0, 0:96], pcol[:, 0, 96:112], pcol[:, 0, 112:120]
        g_mix1, g_mixp1, g_ffn1, g_ffnp1 = (pcol[:, 1, 16 * n:16 * n + 16] for n in range(4))
        lng, lnb, cb = (pcol[:, 1, 64 + 8 * n:72 + 8 * n] for n in range(3))
        g_mix2, g_mixp2, g_ffn2, g_ffnp2 = (pcol[:, 2, 16 * n:16 * n + 16] for n in range(4))
        b_qkv, b_u, b_ga, b_gp = (pcol[:, 2, a:b] for a, b in ((64, 88), (88, 96), (96, 112), (112, 128)))
        C_F, C_U = 3 * DA, 3 * DA + HEADS
        C_GA = C_U + DA
        C_GP = C_GA + D

        raw_loaded = [sem(f"raw_loaded{n}") for n in range(RING)]
        hi_ready = sem("hi_ready")
        lo_ready = sem("lo_ready")
        half_used = sem("half_used")
        bank_free = [sem(f"bank_free{n}") for n in range(4)]
        c_loaded, rows_loaded = sem("c_loaded"), sem("rows_loaded")
        consts = sem("consts")
        tr_done = sem("tr_done")
        tr_copied = sem("tr_copied")
        cact_ready = sem("cact_ready")
        pre_loaded = [sem(f"pre_loaded{n}") for n in range(4)]
        pre_used = sem("pre_used")
        ada_loaded = [sem(f"ada_loaded{n}") for n in range(ADA_RING)]
        ada_scaled = sem("ada_scaled")
        ada_used = sem("ada_used")
        ada_rest = sem("ada_rest")
        rest_zero = sem("rest_zero")
        acc_zero = sem("acc_zero")
        ada_sum = sem("ada_sum")
        mod_ready = sem("mod_ready")
        coef_ready = sem("coef_ready")
        sq_ready = sem("sq_ready")
        sq_used = sem("sq_used")
        sum_ready = sem("sum_ready")
        stat_ready = sem("stat_ready")
        root_ready = sem("root_ready")
        rstd_ready = sem("rstd_ready")
        term_ready = sem("term_ready")
        h_hi_ready = sem("h_hi_ready")
        h_ready = sem("h_ready")
        y_scaled = sem("y_scaled")
        x_ready = sem("x_ready")
        x_added = sem("x_added")
        y_zero = sem("y_zero")
        conv_step = sem("conv_step")
        mu_sum, cen_ready = sem("mu_sum"), sem("cen_ready")
        ln_term, ln_silu = sem("ln_term"), sem("ln_silu")
        mix_hi, mix_ready = sem("mix_hi"), sem("mix_ready")
        sel_ready = sem("sel_ready")
        s_done = sem("s_done")
        v_done = sem("v_done")
        soft = sem("soft")
        p_masked = sem("p_masked")
        v_copied, p_exp = sem("v_copied"), sem("p_exp")
        p_ready = sem("p_ready")
        pt_done, pt_copied = sem("pt_done"), sem("pt_copied")
        o_done = sem("o_done")
        o_hi, o_lo = sem("o_hi"), sem("o_lo")
        hid_ready = sem("hid_ready")
        hid_hi_ready, hid_lo_ready = sem("hid_hi_ready"), sem("hid_lo_ready")
        tap_ready = sem("tap_ready")
        tap_next = sem("tap_next")
        gelu_ready = sem("gelu_ready")
        f_step = sem("f_step")
        scan = sem("scan")
        pads = sem("pads")
        rel_ready = sem("rel_ready")
        win_step = sem("win_step")
        d_ready, d_hi_ready, d_lo_ready = sem("d_ready"), sem("d_hi_ready"), sem("d_lo_ready")
        pl_hi_ready, pl_lo_ready = sem("pl_hi_ready"), sem("pl_lo_ready")
        m_ready, m_hi_ready, m_lo_ready = sem("m_ready"), sem("m_hi_ready"), sem("m_lo_ready")
        last_done, last_copied, stored = sem("last_done"), sem("last_copied"), sem("stored")
        block = ctx.enter_context(nc.Block())

        def fp(ap):
            return ap.bitcast(f32)

        @block.sync
        def _(sp):
            halves = Count()

            def half(src):
                slot = halves.mod(RING)
                sp.wait_ge(lo_ready, halves.at(1, 1))
                sp.dma_start(raw[:, slot], src).then_inc(raw_loaded[slot], 16)
                halves.next()

            def k_tiles(w, row, col, rows):
                for r in range(row, row + rows, 512):
                    half(w[r:r + 512, ds(col, 256)].rearrange("(t p) n -> p t n", p=128))

            def down_rows(w, chunk):
                for n in range(8):
                    half(w[ds(chunk, CHUNK), n * 256:n * 256 + 256].rearrange("(t p) n -> p t n", p=128))

            for src, dst in ((ada_b.rearrange("(n p) -> n p", p=128), prow[0:96, 0]),
                             (c.rearrange("(n p) -> n p", p=128), prow[96:112, 0]),
                             (pool_scale_2.rearrange("(n p) -> n p", p=128), prow[112:120, 0])):
                sp.dma_start(dst, src).then_inc(c_loaded, 16)
            pre = Count()
            for part in (1, 0):
                with loop(sp, 4, (pre, 4)) as i:
                    rows = [sp.snap(i * 512 + n * 128) for n in range(4)]
                    for n in range(4):
                        slot = pre.mod(4)
                        sp.wait_ge(pre_used, pre.at(1, 1))
                        sp.dma_start(ada_pre[:, slot], ada_w[ds(rows[n], 128), part * D:(part + 1) * D])\
                          .then_inc(pre_loaded[slot], 16)
                        pre.next()
            with loop(sp, 4, (halves, 8)) as i:
                a = sp.snap(i * 256 + 3 * DA)
                g = sp.snap(i * 256 + 3 * DA + DA)
                k_tiles(w_in, 0, g, D)
                k_tiles(w_in, 0, a, D)
            with loop(sp, 4, (halves, 12)) as i:
                cols = [sp.snap(i * 256 + n * DA) for n in range(3)]
                for col in cols:
                    k_tiles(w_in, 0, col, D)
            for row in (0, 512):
                for n in range(8):
                    k_tiles(w_out, row, n * 256, 512)
            for n in range(8):
                k_tiles(w_out, DA, n * 256, DA)

            def ffn(gate, up, up0, down):
                for n in range(2):
                    k_tiles(gate, 0, n * 256, D)
                for n in range(2):
                    k_tiles(up, 0, up0 + n * 256, D)
                with loop(sp, NCHUNK - 1, (halves, 24)) as i:
                    gates = [sp.snap(i * CHUNK + CHUNK + n * 256) for n in range(2)]
                    rows = sp.snap(i * CHUNK)
                    ups = [sp.snap(i * CHUNK + up0 + CHUNK + n * 256) for n in range(2)]
                    for col in gates:
                        k_tiles(gate, 0, col, D)
                    down_rows(down, rows)
                    for col in ups:
                        k_tiles(up, 0, col, D)
                down_rows(down, (NCHUNK - 1) * CHUNK)

            ffn(w_gate, w_up, 0, w_down)
            k_tiles(w_in_2, 0, 0, D)
            k_tiles(w_in_2, 0, DA, D)
            for n in range(2):
                slot = halves.mod(RING)
                sp.wait_ge(lo_ready, halves.at(1, 1))
                sp.dma_start(raw[:, slot].rearrange("p t n -> p (t n)").rearrange("p (t n) -> p t n", n=128),
                             w_in_2[1024 * n:1024 * n + 1024, C_F:C_F + 128].rearrange("(t p) n -> p t n", p=128))\
                  .then_inc(raw_loaded[slot], 16)
                halves.next()
            k_tiles(w_in_2, 0, 2 * DA, D)
            k_tiles(w_in_2, 0, C_U, D)
            with loop(sp, 3, (halves, 16)) as i:
                cols = [sp.snap((i + 1) * 256 + off) for off in (0, DA, 2 * DA, C_U)]
                for col in cols:
                    k_tiles(w_in_2, 0, col, D)
            k_tiles(w_in_2, 0, C_GA, D)
            k_tiles(w_in_2, 0, C_GP, D)
            k_tiles(w_attn_o_2, 0, 0, DA)
            k_tiles(pool_w_2.rearrange("g c n -> (g c) n"), 0, 0, DA)
            with loop(sp, 7, (halves, 12)) as i:
                this = sp.snap(i * 256)
                ga = sp.snap((i + 1) * 256 + C_GA)
                gp = sp.snap((i + 1) * 256 + C_GP)
                nxt = sp.snap(i * 256 + 256)
                k_tiles(w_pool_o_2, 0, this, DA)
                k_tiles(w_in_2, 0, ga, D)
                k_tiles(w_in_2, 0, gp, D)
                k_tiles(w_attn_o_2, 0, nxt, DA)
            k_tiles(w_pool_o_2, 0, 7 * 256, DA)
            with loop(sp, 4, (halves, 8)) as i:
                cols = [sp.snap(i * 512 + n * 256) for n in range(2)]
                for col in cols:
                    k_tiles(w_out_2, 0, col, D)
            ffn(w_ffn_up_2, w_ffn_up_2, F, w_ffn_down_2)
            for j in range(4):
                sp.wait_ge(last_copied, 2 * j + 2)
                sp.dma_start(out[:, 512 * j:512 * j + 512].rearrange("(t p) n -> p t n", p=128),
                             outrow[:, :, 512 * j:512 * j + 512]).then_inc(stored, 16)
            sp.wait_ge(stored, 64)

        @block.gpsimd
        def _(gp):
            gp.memset(ident[:, :], 0.0).then_inc(consts, 1)
            gp.memset(ones[:, :], 1.0).then_inc(consts, 1)
            gp.memset(eps[:, 0:1], 1e-6).then_inc(consts, 1)
            gp.memset(eps[:, 1:2], 1e-5).then_inc(consts, 1)
            gp.wait_ge(consts, 4)
            gp.affine_select(out=ident[:, :], in_=ident[:, :], compare_op=ALU.not_equal, fill=1.0,
                             base=0, pattern=[[-1, 128]], channel_multiplier=1).then_inc(consts, 1)
            gp.memset(mask[:, :], 0.0).then_inc(consts, 1)
            gp.wait_ge(consts, 6)
            m = mask[:, 0:512].rearrange("p (j k) -> p j k", j=2)
            gp.affine_select(out=m, in_=m, compare_op=ALU.is_ge, fill=NEG, base=0,
                             pattern=[[128, 2], [-1, SEQ]], channel_multiplier=1).then_inc(consts, 1)

            def ada_load(a):
                slot, (part, kt) = ADA_SLOT[a], ADA_ROW[a]
                before = [b for b in range(a) if ADA_SLOT[b] == slot]
                if before:
                    gp.wait_ge(ada_used, before[-1] + 1)
                    gp.wait_ge(ada_rest, min(before[-1] + 1, 3 * KT))
                gp.dma_start(ada_raw[:, slot], ada_w[128 * kt:128 * kt + 128, part * D:(part + 1) * D])\
                  .then_inc(ada_loaded[slot], 16)

            def residual(src, cols, n):
                for kt in range(KT):
                    if POOL_X[kt]:
                        gp.wait_ge(y_scaled, n * KT + kt + 1)
                        gp.tensor_tensor(xt[:, kt, cols], xt[:, kt, cols], src[:, kt, cols], ALU.add).then_inc(x_added, 1)

            def sum_squares(before, width):
                for kt in range(KT):
                    gp.wait_ge(sq_ready, before + kt + 1)
                    if kt == 0:
                        gp.tensor_copy(rstd[:, 0:width], sq[:, 0, 0:width]).then_inc(sq_used, 1)
                    else:
                        gp.wait_ge(sq_used, before + kt)
                        gp.tensor_tensor(rstd[:, 0:width], rstd[:, 0:width], sq[:, kt % 2, 0:width], ALU.add)\
                          .then_inc(sq_used, 1)

            gp.wait_ge(ada_sum, 2)
            for a in range(ADA_RING):
                ada_load(a)
            for a in range(4 * KT):
                part, kt = ADA_ROW[a]
                cols = slice(0, DVE_COL if part < 5 else D)
                dst = acc_b if part == 3 else acc
                if kt == 0:
                    if part == 4:
                        gp.wait_ge(ada_sum, 3)
                    if part == 5:
                        sum_squares(KT + AT, SEQ)
                        residual(y1, SB, 0)
                        gp.wait_ge(h_ready, 2 * KT)
                        gp.memset(y[:, :, SB], 0.0).then_inc(y_zero, 1)
                        gp.wait_ge(ada_sum, 5)
                    gp.memset(dst[:, cols], 0.0).then_inc(acc_zero, 1)
                    gp.wait_ge(acc_zero, part + 1)
                gp.wait_ge(ada_scaled, a + 1)
                if a:
                    gp.wait_ge(ada_used, a)
                gp.tensor_tensor(dst[:, cols], dst[:, cols], ada_raw[:, ADA_SLOT[a], cols], ALU.add).then_inc(ada_used, 1)
                for b in range(ADA_RING, 4 * KT):
                    if a == max(x for x in range(b) if ADA_SLOT[x] == ADA_SLOT[b]):
                        ada_load(b)
            sum_squares(3 * KT + AT, SEQ)
            residual(y, SB, 1)
            gp.wait_ge(h_ready, 3 * KT)
            gp.memset(mask[:, :], 0.0).then_inc(consts, 1)
            gp.memset(u2[:, :, 0:META], 0.0).then_inc(pads, 1)
            gp.memset(lf[0][:, 0:256], 0.0).then_inc(pads, 1)
            gp.memset(lf[1][:, 0:256], 0.0).then_inc(pads, 1)
            gp.wait_ge(consts, 8)
            for j in range(3):
                m = mask[0:QT, QO[j]:QO[j] + QW[j]]
                gp.affine_select(out=m, in_=m, compare_op=ALU.is_ge, fill=NEG, base=LIVE0 + QT * j,
                                 pattern=[[-1, QW[j]]], channel_multiplier=1).then_inc(consts, 1)
            gp.tensor_scalar(pick[:, :], ident[0:HEADS, 0:HEADS], -1.0 / SCALE, 0.0, ALU.mult, ALU.add)\
              .then_inc(consts, 1)
            gp.wait_ge(consts, 12)
            with loop(gp, 4) as i:
                gp.wait_ge(s_done, i * 2 + HEADS)
                for o in range(2):
                    gp.tensor_copy(sel[:, o, :], pick[:, ds(i * 2 + o)].to_broadcast([HEADS, QT]))\
                      .then_inc(sel_ready, 1)
            sum_squares(5 * KT + AT, LIVE)
            residual(y2, ST, 2)
            gp.wait_ge(h_ready, 4 * KT)
            gp.memset(y[:, :, SB], 0.0).then_inc(y_zero, 1)
            sum_squares(7 * KT + AT, SEQ)
            residual(y, SB, 3)

        @block.scalar
        def _(act):
            halves, done, banks = Count(), Count(RING), Banks()

            def convert():
                if halves.i is None and halves.c >= HALVES:
                    return
                slot = halves.mod(RING)
                act.wait_ge(raw_loaded[slot], halves.div(RING, 16, 16))
                act.wait_ge(half_used, halves.at(1, 1))
                act.activation(w_hi[:, slot], raw[:, slot], ACT.Copy).then_inc(hi_ready, 1)
                halves.next()

            def group(n=4):
                for _ in range(n):
                    convert()
                act.wait_ge(half_used, done.next(n))
                return banks.close()

            def skip(n_halves, n_groups):
                for _ in range(n_halves):
                    convert()
                done.next(n_halves)
                for _ in range(n_groups):
                    banks.close()

            act.dma_start(xrow[:, :, :], x.rearrange("(t p) n -> p t n", p=128)).then_inc(rows_loaded, 16)
            for t, src, r, n in (
                    (1, mix_pre_g, 0, 16), (1, mix_post_g, 16, 16), (1, ffn_pre_g, 32, 16),
                    (1, ffn_post_g, 48, 16), (1, conv_ln_g, 64, 8), (1, conv_ln_b, 72, 8), (1, conv_b, 80, 8),
                    (2, mix_pre_g_2, 0, 16), (2, mix_post_g_2, 16, 16), (2, ffn_pre_g_2, 32, 16),
                    (2, ffn_post_g_2, 48, 16), (2, b_in_2[0:C_F], 64, 24), (2, b_in_2[C_U:C_GA], 88, 8),
                    (2, b_in_2[C_GA:C_GP], 96, 16), (2, b_in_2[C_GP:C_GP + D], 112, 16),
                    (3, ffn_conv_b_2, 0, 2 * FT), (4, ffn_conv_w_2[0], 0, 2 * FT),
                    (5, ffn_conv_w_2[1], 0, 2 * FT), (6, ffn_conv_w_2[2], 0, 2 * FT)):
                act.dma_start(prow[r:r + n, t], src.rearrange("(n p) -> n p", p=128)).then_inc(rows_loaded, 16)
            act.dma_start(mrow[:, :], meta_tokens_2).then_inc(rows_loaded, 16)
            act.dma_start(cwrow[:, :], conv_w).then_inc(rows_loaded, 16)
            act.dma_start(bf[:, :], b_in_2[C_F:C_U].rearrange("(n p) -> n p", p=1)).then_inc(rows_loaded, 16)
            seen = Count()

            def copied(out_ap, in_ap):
                act.wait_ge(tr_done, seen.next())
                act.activation(out_ap, in_ap, ACT.Copy).then_inc(tr_copied, 1)

            def quarters(b, n):
                return bank[:, b, 0:512 if n == 4 else 256].rearrange("p (a b) -> p a b", a=n)

            copied(pcol[:, 0, 0:120], bank[:, B_S, 0:120])
            act.wait_ge(tr_copied, 1)
            act.activation(cact[:, :], ccol, ACT.Silu).then_inc(cact_ready, 1)
            for n in range(8):
                t, j = n // 4, n % 4
                copied(xt[:, 4 * j:4 * j + 4, META + 128 * t:META + 128 * t + 128], quarters(B_S + (1 + n) % 4, 4))
            copied(pcol[:, 1, 0:88], bank[:, B_S + 1, 0:88])
            copied(pcol[:, 2, :], bank[:, B_S + 2, 0:128])
            copied(pcol[:, 3:7, 0:88], quarters(B_S + 3, 4)[:, :, 0:88])
            copied(xt[:, :, 0:META], quarters(B_S, KT))
            copied(cwt[:, :, 0:CONV_K], quarters(B_S + 1, AT)[:, :, 0:CONV_K])
            act.wait_ge(tr_copied, 14)
            sqs, terms = Count(), Count()

            def square(src, cols, kt):
                if sqs.c >= 2:
                    act.wait_ge(sq_used, sqs.at(1, -1))
                act.activation(sq[:, kt % 2, 0:cols.stop - cols.start], src[:, kt, cols], ACT.Square)\
                   .then_inc(sq_ready, 1)
                sqs.next()

            def squares(src, cols, n=KT, ready=None, update=None):
                for kt in range(n):
                    if ready is not None:
                        act.wait_ge(ready[0], ready[1].next())
                    if update is not None:
                        wait_x(act, kt, update, x_ready, x_added)
                    square(src, cols, kt)

            def squares_of_sums(src, cols, first, n_halves):
                for o in range(2):
                    act.wait_ge(bank_free[first + o], banks.read)
                    square(src, cols, n_halves + o)

            def root(width, n=D, summed=None):
                if summed is None:
                    act.wait_ge(sq_used, sqs.at())
                else:
                    act.wait_ge(sum_ready, summed)
                act.activation(stat[:, 0:width], bank[:, B_N, 0:width], ACT.Sqrt, scale=1.0 / n,
                               bias=eps[:, 0:1] if n == D else eps[:, 1:2]).then_inc(root_ready, 1)

            def h_tile(kt, cols, shift=None):
                act.wait_ge(term_ready, terms.next())
                if shift is None:
                    act.activation(h_hi[:, kt, cols], y[:, kt, cols], ACT.Copy).then_inc(h_hi_ready, 1)
                else:
                    act.activation(h_hi[:, kt, cols], y[:, kt, cols], ACT.Identity,
                                   bias=shift[:, kt:kt + 1]).then_inc(h_hi_ready, 1)

            def h_tiles(cols, shift=None):
                for kt in range(KT):
                    h_tile(kt, cols, shift)

            cens = Count()
            squares(xt, SB)
            act.wait_ge(consts, 5)
            root(SEQ)
            act.wait_ge(mod_ready, 2)
            for kt in range(KT):
                h_tile(kt, SB, mod[:, 0])
                if kt % 4 == 3 and kt < 4 * LEAD:
                    convert()
            slot_loads = [Count() for _ in range(ADA_RING)]
            act.wait_ge(cact_ready, 1)

            def ada_row(kt, slot):
                act.wait_ge(ada_loaded[slot], slot_loads[slot].next(1, 16))
                act.activation(ada_raw[:, slot], ada_raw[:, slot], ACT.Copy, scale=cact[:, ds(kt)])\
                   .then_inc(ada_scaled, 1)

            with loop(act, 4, (halves, 8), (done, 8), (banks, 2), *((c, 1) for c in slot_loads)) as i:
                for n in range(8):
                    convert()
                    if n % 2:
                        ada_row(i * 4 + n // 2, n // 2)
                    if n == 4:
                        act.wait_ge(half_used, done.next(4))
                        b = banks.close()
                        for o in range(2):
                            act.wait_ge(bank_free[2 + o], banks.free())
                            act.activation(sigg[:, o], bank[:, b + o, 0:SEQ], ACT.Sigmoid).then_inc(bank_free[b + o], 1)
                done.next(4)
                banks.close()
            vs, masked, pts, outs = Count(), Count(), Count(), Count()

            def exps(sm, tiles, v_parts):
                act.wait_ge(v_done, vs.next())
                for dst, src in v_parts:
                    act.activation(dst, src, ACT.Copy).then_inc(v_copied, 1)
                act.wait_ge(p_masked, masked.next())
                for rows, o, w, j in tiles:
                    act.activation(sm[0:rows, o:o + w], sm[0:rows, o:o + w], ACT.Exp, bias=mx[0:rows, j:j + 1],
                                   accum_out=rs[0:rows, j:j + 1]).then_inc(p_exp, 1)

            def copy_pt(parts):
                act.wait_ge(pt_done, pts.next())
                for dst, src in parts:
                    act.activation(dst, src, ACT.Copy).then_inc(pt_copied, 1)

            def round_out(a_hi, head, width):
                act.wait_ge(o_done, outs.next())
                act.activation(a_hi[:, ds(head), 0:width], bank[:, B_P:B_P + 1, 0:width], ACT.Copy).then_inc(o_hi, 1)

            def attend(n, pair, sm, exp_tiles, v_parts, pt_parts, a_hi, width):
                if n == 4:
                    copy_pt(pt_parts)
                if n == 5:
                    round_out(a_hi, pair * 2, width)
                    act.wait_ge(v_done, vs.at(1, 1))
                if n in (2, 6):
                    exps(sm, exp_tiles, v_parts)
                if n == 8:
                    copy_pt(pt_parts)
                if n == 9:
                    round_out(a_hi, pair * 2 + 1, width)

            attend1 = lambda n, pair: attend(n, pair, sm1, [(128, 0, SEQ, 0), (128, SEQ, SEQ, 1)],
                                             [(v_t1[:, :, :], quarters(B_V, 2))],
                                             [(p_t1[:, :], bank[:, B_P, 0:384])], a1_hi, SEQ)

            def heads1(body, pair):
                banks.pair = 0
                for n in range(12):
                    convert()
                    if pair is not None:
                        attend1(n, pair)
                    if n in (5, 8, 11):
                        act.wait_ge(half_used, done.next(4))
                        b = banks.close()
                        for o in range(2):
                            act.activation(qkv1[:, n // 4 + n // 11 - 1, o], bank[:, b + o, 0:SEQ], ACT.Copy)\
                               .then_inc(bank_free[b + o], 1)
                    if n % 2 == 0:
                        k = n // 2
                        ada_row(body * 3 + k if k < 3 else (body + 1) * 3 + (k - 6), k % 3)

            heads1(0, None)
            with loop(act, 3, (halves, 12), (done, 12), (banks, 3), (vs, 2), (masked, 2), (pts, 2), (outs, 2),
                      *((c, 2) for c in slot_loads[:3])) as i:
                heads1(i + 1, i)
            for n in range(16):
                convert()
                if n <= 8:
                    attend1(n, 3)
                if n == 8:
                    attend1(9, 3)
                if 1 <= n <= 8:
                    act.wait_ge(half_used, done.next(1))
                    b = banks.close()
                    for o in range(2):
                        act.activation(y1[:, 2 * n - 2 + o, SB], bank[:, b + o, 0:SEQ], ACT.Copy)\
                           .then_inc(bank_free[b + o], 1)
                if n in ADA_TAIL:
                    k = ADA_TAIL.index(n)
                    ada_row(12 + k % 4, k % 4)
                if n == 9:
                    squares(cv, slice(0, SEQ), AT, (cen_ready, cens))
                if n == 11:
                    root(SEQ, DA)
                    for t in range(AT):
                        act.wait_ge(ln_term, t + 1)
                        act.activation(cv[:, t, :], cv[:, t, :], ACT.Silu, bias=lnb[:, t:t + 1]).then_inc(ln_silu, 1)
                        act.wait_ge(ln_silu, t + 1)
                        act.activation(c_hi[:, t, SB], cv[:, t, :], ACT.Copy).then_inc(mix_hi, 1)
            done.next(8)
            for _ in range(8):
                banks.close()
            for j in range(8):
                convert()
                convert()
                if j:
                    squares_of_sums(y1, SB, b, 2 * j - 2)
                done.next(2)
                b = banks.close()
            squares_of_sums(y1, SB, b, 14)
            root(SEQ, summed=1)
            squares(xt, SB, update=0)
            root(SEQ)
            act.wait_ge(mod_ready, 5)
            h_tiles(SB, mod[:, 3])
            taps, gelus, hids = Count(), Count(), Count()

            def gate1(i, b, t):
                for o in range(2):
                    act.activation(sg[:, t + o], bank[:, b + o, 0:SEQ], ACT.Silu).then_inc(bank_free[b + o], 1)

            def up1(i, b, t):
                for o in range(2):
                    act.wait_ge(bank_free[b + o], banks.read)
                    act.activation(hid_hi[:, t + o], hid[:, t + o], ACT.Copy).then_inc(hid_hi_ready, 1)

            def tap(dst, i, b, t, first):
                for o in range(2):
                    ch = i * 4 + (t + o + first)
                    act.activation(dst[:, t + o:t + o + 1, :], bank[:, b + o:b + o + 1, 0:SEQ], ACT.Identity,
                                   scale=pcol[:, 4, ds(ch)], bias=pcol[:, 3, ds(ch)]).then_inc(tap_ready, 1)

            def gate2(i, b, t):
                tap(sg, i, b, t, 0)
                for o in range(2):
                    act.wait_ge(bank_free[b + o], banks.read)
                    act.activation(sg[:, t + o], sg[:, t + o], ACT.Gelu_apprx_tanh).then_inc(gelu_ready, 1)

            def up2(i, b, t):
                tap(va, i, b, t, FT)
                for o in range(2):
                    act.wait_ge(hid_ready, hids.next())
                    act.activation(hid_hi[:, t + o], hid[:, t + o], ACT.Copy).then_inc(hid_hi_ready, 1)

            def ffn(gate, up, n_hids, with_ada, n_sum):
                def chunk(i, read):
                    for g in range(2):
                        read(i, group(), 2 * g)

                first = (gate, 0), (gate, 2), (up, 0), (up, 2)
                a = 0
                for read, t in first:
                    read(0, group(), t)
                    for n in range(with_ada * (2 - t // 2)):
                        ada_row(a, ADA_SLOT[3 * KT + a])
                        a += 1
                with loop(act, NCHUNK - 1, (halves, 24), (done, 24), (banks, 12), (hids, n_hids),
                          (slot_loads[0], with_ada)) as i:
                    chunk(i + 1, gate)
                    skip(8, 8)
                    if with_ada:
                        ada_row(i + a, 0)
                    chunk(i + 1, up)
                for j in range(8):
                    convert()
                    if j:
                        squares_of_sums(y, SB, b, 2 * j - 2)
                    done.next(1)
                    b = banks.close()
                squares_of_sums(y, SB, b, 14)
                root(SEQ, summed=n_sum)

            ffn(gate1, up1, 0, 1, 2)
            squares(xt, slice(0, ALL), update=1)
            root(ALL)
            h_tiles(slice(0, ALL))
            def forget_gates(step):
                if step == 0:
                    act.wait_ge(half_used, done.next(2))
                    act.wait_ge(mod_ready, 6)
                    act.activation(lf[1][:, 256:], bank[0:HEADS, B_N, 0:ALL], ACT.Identity, bias=bf[:, :])\
                       .then_inc(f_step, 1)
                else:
                    act.wait_ge(f_step, step)
                if step == 1:
                    act.activation(sc_in[:, :], lf[1][:, 256:], ACT.Abs).then_inc(f_step, 1)
                if step == 2:
                    act.activation(sc_in[:, :], sc_in[:, :], ACT.Exp, scale=-1.0).then_inc(f_step, 1)
                if step == 3:
                    act.activation(sc_in[:, :], sc_in[:, :], ACT.Ln, bias=1.0).then_inc(f_step, 1)

            every = slice(0, ALL)
            attend2 = lambda n, pair: attend(
                n, pair, sm, [(QT, QO[j], QW[j], j) for j in range(3)],
                [(v_t[:, 0:2, :], quarters(B_V, 2)), (v_t[0:META, 2, :], bank[0:META, B_V, 256:384])],
                [(p_t[:, 0:5 * QT], bank[:, B_P, 0:5 * QT]),
                 (p_t[0:META, 5 * QT:6 * QT], bank[0:META, B_V, 384:384 + QT])], a_hi, LIVE)

            def heads2(body, pair):
                for n in range(16):
                    if n == 8 and pair is None:
                        convert()
                        convert()
                    convert()
                    if pair is not None:
                        attend2(n, pair)
                    if n in (5, 8, 12, 15):
                        act.wait_ge(half_used, done.next(4))
                        b = banks.close()
                        for o in range(2):
                            if n < 15:
                                act.activation(qkv[:, n // 4 - 1, o:o + 1, every], bank[:, b + o:b + o + 1, 0:ALL],
                                               ACT.Identity, bias=b_qkv[:, ds(body * 2 + (AT * (n // 4 - 1) + o))])\
                                   .then_inc(bank_free[b + o], 1)
                            else:
                                act.activation(u2[:, ds(body * 2 + o), META:], bank[:, b + o:b + o + 1, 0:ALL],
                                               ACT.Identity, bias=b_u[:, ds(body * 2 + o)])\
                                   .then_inc(bank_free[b + o], 1)
                    if 8 <= n < 12 and pair is None:
                        forget_gates(n - 8)

            heads2(0, None)
            with loop(act, 3, (halves, 16), (done, 16), (banks, 4), (vs, 2), (masked, 2), (pts, 2), (outs, 2)) as i:
                heads2(i + 1, i)
            ms = Count()

            def gate(dst, bias, tile):
                b = banks.close()
                for o in range(2):
                    act.activation(dst[:, o:o + 1], bank[:, b + o:b + o + 1, 0:LIVE], ACT.Sigmoid,
                                   bias=bias[:, ds(tile + o)]).then_inc(bank_free[b + o], 1)

            for n in range(10):
                convert()
                if n <= 8:
                    attend2(n, 3)
                if n == 8:
                    attend2(9, 3)
                if 1 <= n <= 8:
                    act.wait_ge(d_ready, n)
                    act.activation(d_hi[:, n - 1], sq[:, (n - 1) % 2, 0:LIVE], ACT.Copy).then_inc(d_hi_ready, 1)
                if n in (4, 8):
                    act.wait_ge(half_used, done.next(4))
                    gate(ga_s if n == 4 else gp_s, b_ga if n == 4 else b_gp, 0)
            done.next(2)
            banks.close()
            for g in range(4):
                if g % 2 == 0:
                    convert()
                    act.wait_ge(half_used, done.next(1))
                b = banks.close()
                for o in range(2):
                    t = 2 * g + o
                    act.wait_ge(d_lo_ready if t < 2 else pl_lo_ready, AT if t < 2 else t - 1)
                    act.activation(sq[:, t % 2, 0:LIVE], bank[:, b + o, 0:LIVE], ACT.Copy, scale=pscale[:, t:t + 1])\
                       .then_inc(bank_free[b + o], 1)
                    act.wait_ge(bank_free[b + o], banks.read)
                    act.activation(pl_hi[:, t], sq[:, t % 2, 0:LIVE], ACT.Copy).then_inc(pl_hi_ready, 1)

            def mix(body):
                skip(2, 1)
                for o in range(2):
                    act.wait_ge(m_ready, ms.next())
                    act.activation(m_hi[:, ds(body * 2 + o)], gp_s[:, o:o + 1], ACT.Copy).then_inc(m_hi_ready, 1)

            with loop(act, 7, (halves, 12), (done, 12), (banks, 4), (ms, 2)) as i:
                mix(i)
                for n in range(2):
                    for _ in range(4):
                        convert()
                    act.wait_ge(half_used, done.next(4))
                    if n == 1:
                        act.wait_ge(m_lo_ready, ms.at())
                    gate(gp_s if n else ga_s, b_gp if n else b_ga, i * 2 + 2)
                skip(2, 1)
            mix(7)

            def out_tiles(b, tile):
                for o in range(2):
                    act.activation(y2[:, ds(tile + o), ST], bank[:, b + o:b + o + 1, 0:LIVE], ACT.Copy)\
                       .then_inc(bank_free[b + o], 1)

            with loop(act, 3, (halves, 8), (done, 8), (banks, 2)) as i:
                for n in range(2):
                    out_tiles(group(), i * 4 + 2 * n)
            for b in range(4):
                act.wait_ge(bank_free[b], banks.had[b // 2].at(1, 1))
            for n in range(8):
                convert()
                if n == 4:
                    act.wait_ge(half_used, done.next(4))
                    b = banks.close()
                    out_tiles(b, 12)
                if n < 6:
                    for o in range(2):
                        square(y2, ST, 2 * n + o)
                if n == 6:
                    squares_of_sums(y2, ST, b, 12)
            act.wait_ge(half_used, done.next(4))
            b = banks.close()
            out_tiles(b, 14)
            squares_of_sums(y2, ST, b, 14)
            root(LIVE, summed=3)
            squares(xt, ST, update=2)
            root(LIVE)
            h_tiles(ST)
            ffn(gate2, up2, 4, 0, 4)
            for n in range(8):
                act.wait_ge(last_done, n + 1)
                act.activation(outrow[:, n % 2, 512 * (n // 2):512 * (n // 2) + 512], bank[:, B_S + n % 4, :], ACT.Copy)\
                   .then_inc(last_copied, 1)

        @block.vector
        def _(dve):
            halves, done, banks = Count(), Count(RING), Banks()

            def convert():
                if halves.i is None and halves.c >= HALVES:
                    return
                slot = halves.mod(RING)
                dve.wait_ge(hi_ready, halves.at(1, 1))
                dve.tensor_tensor(w_lo[:, slot], raw[:, slot], fp(w_hi[:, slot]), ALU.subtract).then_inc(lo_ready, 1)
                halves.next()

            def group(n=4):
                for _ in range(n):
                    convert()
                dve.wait_ge(half_used, done.next(n))
                return banks.close()

            def skip(n_halves, n_groups):
                for _ in range(n_halves):
                    convert()
                done.next(n_halves)
                for _ in range(n_groups):
                    banks.close()

            dve.memset(mx[:, :], 0.0).then_inc(lo_ready, RING)
            dve.memset(rs[:, :], 0.0).then_inc(half_used, RING)
            dve.memset(rstd[:, 0:1], 0.0).then_inc(bank_free[0], 1)
            dve.memset(rstd[:, 1:2], 0.0).then_inc(bank_free[1], 1)
            dve.memset(rstd[:, 2:3], 0.0).then_inc(bank_free[2], 1)
            dve.memset(rstd[:, 3:4], 0.0).then_inc(bank_free[3], 1)
            dve.memset(rstd[:, 4:5], 0.0).then_inc(pre_used, 4)
            pre, zeros, parts_done = Count(), Count(), Count()

            def clear(dst):
                dve.memset(dst[:, :], 0.0).then_inc(acc_zero, 1)
                dve.wait_ge(acc_zero, zeros.next())

            def finish(part):
                dve.wait_ge(ada_sum, parts_done.next())
                dve.tensor_tensor(mod[:, part], bank[:, B_N, 496:512], adab[:, KT * part:KT * part + KT], ALU.add)\
                   .then_inc(mod_ready, 1)

            def mod_rows(dst, i):
                for n in range(4):
                    dve.wait_ge(pre_loaded[n], pre.div(4, 16, 16))
                    dve.wait_ge(pre_used, pre.at(1, 4))
                    dve.scalar_tensor_tensor(out=dst[:, :], in0=ada_pre[:, n], scalar=cact[:, ds(i * 4 + n)],
                                             in1=dst[:, :], op0=ALU.mult, op1=ALU.add).then_inc(pre_used, 1)
                    pre.next()

            def shift_term(kt):
                dve.scalar_tensor_tensor(out=y[:, ds(kt), SB], in0=xt[:, ds(kt), SB], scalar=coef[:, 0, ds(kt)],
                                         in1=rstd[:, 0:SEQ].rearrange("p (a n) -> p a n", a=1),
                                         op0=ALU.mult, op1=ALU.mult).then_inc(term_ready, 1)

            roots, hs, ys = (Count() for _ in range(3))

            def inverse(width):
                dve.wait_ge(root_ready, roots.at(1, 1))
                dve.reciprocal(rstd[:, 0:width], stat[:, 0:width]).then_inc(rstd_ready, 1)
                dve.wait_ge(rstd_ready, roots.next())

            def term(kt, cols, scale):
                dve.scalar_tensor_tensor(out=y[:, kt, cols], in0=xt[:, kt, cols], scalar=scale[:, kt:kt + 1],
                                         in1=rstd[:, 0:cols.stop - cols.start], op0=ALU.mult, op1=ALU.mult)\
                   .then_inc(term_ready, 1)

            def h_rest(kt, cols, shift=None):
                dve.wait_ge(h_hi_ready, hs.next())
                if shift is None:
                    dve.tensor_tensor(h_lo[:, kt, cols], y[:, kt, cols], fp(h_hi[:, kt, cols]), ALU.subtract)\
                       .then_inc(h_ready, 1)
                else:
                    dve.scalar_tensor_tensor(out=h_lo[:, kt, cols], in0=y[:, kt, cols], scalar=shift[:, kt:kt + 1],
                                             in1=fp(h_hi[:, kt, cols]), op0=ALU.add, op1=ALU.subtract)\
                       .then_inc(h_ready, 1)

            def h_tiles(cols, scale, shift=None):
                for kt in range(2):
                    term(kt, cols, scale)
                for kt in range(KT):
                    if kt + 2 < KT:
                        term(kt + 2, cols, scale)
                    h_rest(kt, cols, shift)

            def residual(src, cols, scale):
                width = cols.stop - cols.start

                def add(kt):
                    if POOL_X[kt]:
                        return
                    dve.wait_ge(y_scaled, ys.at(1, kt + 1))
                    dve.tensor_tensor(xt[:, kt, cols], xt[:, kt, cols], src[:, kt, cols], ALU.add).then_inc(x_ready, 1)

                for kt in range(KT):
                    dve.scalar_tensor_tensor(out=src[:, kt, cols], in0=src[:, kt, cols], scalar=scale[:, kt:kt + 1],
                                             in1=rstd[:, 0:width], op0=ALU.mult, op1=ALU.mult).then_inc(y_scaled, 1)
                    if kt:
                        add(kt - 1)
                add(KT - 1)
                ys.next(KT)
                n = ys.c // KT
                dve.wait_ge(x_ready, n * (KT - sum(POOL_X)))
                dve.wait_ge(x_added, n * sum(POOL_X))

            dve.wait_ge(cact_ready, 1)
            clear(acc)
            with loop(dve, 4, (pre, 4)) as i:
                mod_rows(acc, i)
            dve.wait_ge(tr_done, 14)
            clear(acc_b)
            mod_rows(acc_b, 0)
            finish(1)
            dve.wait_ge(mod_ready, 1)
            dve.scalar_tensor_tensor(out=coef[:, 0], in0=mod[:, 1], scalar=1.0, in1=g_mix1,
                                     op0=ALU.add, op1=ALU.mult).then_inc(coef_ready, 1)
            dve.wait_ge(coef_ready, 1)
            inverse(SEQ)
            with loop(dve, 3, (pre, 4)) as i:
                mod_rows(acc_b, i + 1)
                for n in range(4):
                    shift_term(i * 4 + n)
            for kt in range(12, KT):
                shift_term(kt)
            finish(0)
            dve.wait_ge(mod_ready, 2)
            for kt in range(KT):
                h_rest(kt, SB, mod[:, 0])
                if kt % 4 == 3 and kt < 4 * LEAD:
                    convert()
            dve.wait_ge(h_ready, KT)
            dve.memset(upad[:, :, 0:CONV_K - 1], 0.0).then_inc(conv_step, 1)
            steps = Count(1)

            def conv(t, first, last):
                def u(j):
                    return upad[:, ds(t), j:j + SEQ]

                w = lambda j: cwt[:, ds(t), j]
                dst = (cv[:, ds(t), :], cvb[:, :].rearrange("p (a n) -> p a n", a=1))
                for j in range(first, last):
                    if j in (0, 1, CONV_K):
                        dve.wait_ge(conv_step, steps.at())
                    else:
                        dve.wait_ge(conv_step, steps.at(1, -1))
                    if j == 0:
                        op = dve.tensor_scalar(dst[0], u(0), w(0), cb[:, ds(t)], ALU.mult, ALU.add)
                    elif j == 1:
                        op = dve.tensor_scalar(dst[1], u(1), w(1), None, ALU.mult)
                    elif j < CONV_K:
                        op = dve.scalar_tensor_tensor(out=dst[j % 2], in0=u(j), scalar=w(j), in1=dst[j % 2],
                                                      op0=ALU.mult, op1=ALU.add)
                    else:
                        op = dve.tensor_tensor(dst[0], dst[0], dst[1], ALU.add)
                    op.then_inc(conv_step, 1)
                    steps.next()

            def gated(body, tile):
                if tile is not None:
                    for o in range(2):
                        dve.wait_ge(bank_free[2 + o], banks.had[1].at(1, 1))
                for n in range(8):
                    convert()
                    if n in (2, 4, 6):
                        rest_row(acc, n // 2 - 1)
                    if tile is not None:
                        conv(tile, 4 * n, 4 * n + 4)
                rest_row(acc, 3)
                dve.wait_ge(half_used, done.next(8))
                g = banks.close()
                g_read = banks.read
                a = banks.close()
                for o in range(2):
                    dve.wait_ge(bank_free[g + o], g_read)
                    dve.tensor_tensor(upad[:, ds(body * 2 + o), CONV_K - 1:], bank[:, a + o:a + o + 1, 0:SEQ],
                                      sigg[:, o:o + 1], ALU.mult).then_inc(bank_free[a + o], 1)

            rests, rest_zeros = Count(), Count()

            def clear_rest(dst):
                dve.memset(dst[:, DVE_COL:], 0.0).then_inc(rest_zero, 1)
                dve.wait_ge(rest_zero, rest_zeros.next())

            def rest_row(dst, slot):
                dve.wait_ge(ada_scaled, rests.at(1, 1))
                if rests.c:
                    dve.wait_ge(ada_rest, rests.at())
                dve.tensor_tensor(dst[:, DVE_COL:], dst[:, DVE_COL:], ada_raw[:, slot, DVE_COL:], ALU.add)\
                   .then_inc(ada_rest, 1)
                rests.next()

            clear_rest(acc)
            gated(0, None)
            with loop(dve, 3, (halves, 8), (done, 8), (banks, 2), (steps, CONV_K + 1), (rests, 4)) as i:
                gated(i + 1, i)
            clear_rest(acc_b)
            for o in range(2):
                dve.wait_ge(bank_free[2 + o], banks.had[1].at(1, 1))
            scored, soft_n, exped, outs = (Count() for _ in range(4))

            def softmax_max(sm, parts, tiles, rows):
                dve.wait_ge(s_done, scored.next())
                for o, w, src in parts:
                    dve.scalar_tensor_tensor(out=sm[0:rows, o:o + w], in0=src, scalar=SCALE, in1=mask[0:rows, o:o + w],
                                             op0=ALU.mult, op1=ALU.add).then_inc(soft, 1)
                dve.wait_ge(soft, soft_n.next(len(parts)))
                for o, w, j in tiles:
                    dve.reduce_max(mx[0:rows, j:j + 1], sm[0:rows, o:o + w], AX.X).then_inc(soft, 1)
                dve.wait_ge(soft, soft_n.next(len(tiles)))
                n = len(tiles)
                dve.tensor_scalar(mx[0:rows, 0:n], mx[0:rows, 0:n], -1.0, None, ALU.mult).then_inc(p_masked, 1)

            def softmax_norm(sm, tiles, rows):
                n = len(tiles)
                dve.wait_ge(p_exp, exped.next(n))
                dve.reciprocal(rs[0:rows, 0:n], rs[0:rows, 0:n]).then_inc(soft, 1)
                dve.wait_ge(soft, soft_n.next())
                for o, w, j in tiles:
                    dve.tensor_scalar(sm[0:rows, o:o + w], sm[0:rows, o:o + w], rs[0:rows, j:j + 1], None, ALU.mult)\
                       .then_inc(p_ready, 1)

            def out_rest(a_hi, a_lo, head, width):
                dve.wait_ge(o_hi, outs.next())
                dve.tensor_tensor(a_lo[:, ds(head), 0:width], bank[:, B_P:B_P + 1, 0:width],
                                  fp(a_hi[:, ds(head), 0:width]), ALU.subtract).then_inc(o_lo, 1)

            def attend(n, pair, sm, parts, tiles, rows, a_hi, a_lo, width):
                if n in (5, 9):
                    out_rest(a_hi, a_lo, pair * 2 + n // 9, width)
                if n in (1, 5):
                    softmax_max(sm, parts, tiles, rows)
                if n in (3, 7):
                    softmax_norm(sm, tiles, rows)

            attend1 = lambda n, pair: attend(n, pair, sm1, [(0, 512, bank[:, B_S, :])], [(0, SEQ, 0), (SEQ, SEQ, 1)],
                                             128, a1_hi, a1_lo, SEQ)

            def heads1(pair, tile):
                banks.pair = 0
                for n in range(12):
                    convert()
                    if pair is not None:
                        attend1(n, pair)
                    if n == 6 and pair is None:
                        finish(2)
                        clear_rest(acc)
                    if n % 2:
                        k = n // 2
                        rest_row(acc if k >= 3 else acc_b, k % 3)
                    conv(tile, min(3 * n, 2 * n + 8), min(3 * n + 3, 2 * n + 10))
                done.next(12)
                for _ in range(3):
                    banks.close()

            heads1(None, 3)
            with loop(dve, 3, (halves, 12), (done, 12), (banks, 3), (steps, CONV_K + 1), (scored, 2), (soft_n, 8),
                      (exped, 4), (outs, 2), (rests, 6)) as i:
                heads1(i, i + 4)

            def add_group(dst, first):
                b = banks.close()
                for o in range(2):
                    dve.tensor_tensor(dst[:, first + o, SB], dst[:, first + o, SB], bank[:, b + o, 0:SEQ], ALU.add)\
                       .then_inc(bank_free[b + o], 1)

            for n in range(16):
                convert()
                if n <= 8:
                    attend1(n, 3)
                if n == 8:
                    attend1(9, 3)
                if n < 8:
                    conv(AT - 1, 4 * n, 4 * n + 4)
                if n - 1 in ADA_TAIL:
                    k = ADA_TAIL.index(n - 1)
                    rest_row(acc if k >= 4 else acc_b, k % 4)
                if n == 14:
                    finish(3)
                if n == 8:
                    done.next(8)
                    for _ in range(8):
                        banks.close()
                if n >= 9:
                    dve.wait_ge(half_used, done.next())
                    add_group(y1, 2 * (n - 9))
                if n == 9:
                    dve.wait_ge(mu_sum, 1)
                    dve.tensor_scalar(stat[:, 0:SEQ], bank[:, B_N, 0:SEQ], 1.0 / DA, None, ALU.mult).then_inc(stat_ready, 1)
                    dve.wait_ge(stat_ready, 1)
                    for t in range(AT):
                        dve.tensor_tensor(cv[:, t, :], cv[:, t, :], stat[:, 0:SEQ], ALU.subtract).then_inc(cen_ready, 1)
                if n == 11:
                    inverse(SEQ)
                    for t in range(AT):
                        dve.scalar_tensor_tensor(out=cv[:, t, :], in0=cv[:, t, :], scalar=lng[:, t:t + 1],
                                                 in1=rstd[:, 0:SEQ], op0=ALU.mult, op1=ALU.mult).then_inc(ln_term, 1)
                if n == 12:
                    for t in range(AT):
                        dve.wait_ge(mix_hi, t + 1)
                        dve.tensor_tensor(c_lo[:, t, SB], cv[:, t, :], fp(c_hi[:, t, SB]), ALU.subtract)\
                           .then_inc(mix_ready, 1)
            dve.wait_ge(half_used, done.next())
            add_group(y1, 14)
            finish(4)
            for j in range(8):
                convert()
                convert()
                dve.wait_ge(half_used, done.next(2))
                add_group(y1, 2 * j)
            dve.wait_ge(mod_ready, 5)
            dve.tensor_tensor(coef[:, 1], mod[:, 2], g_mixp1, ALU.mult).then_inc(coef_ready, 1)
            dve.scalar_tensor_tensor(out=coef[:, 2], in0=mod[:, 4], scalar=1.0, in1=g_ffn1,
                                     op0=ALU.add, op1=ALU.mult).then_inc(coef_ready, 1)
            dve.wait_ge(coef_ready, 3)
            inverse(SEQ)
            residual(y1, SB, coef[:, 1])
            inverse(SEQ)
            h_tiles(SB, coef[:, 2], mod[:, 3])
            hids, taps, nexts, gelus = (Count() for _ in range(4))

            def rest(t):
                for o in range(2):
                    dve.wait_ge(hid_hi_ready, hids.next())
                    dve.tensor_tensor(hid_lo[:, t + o], hid[:, t + o], fp(hid_hi[:, t + o]), ALU.subtract)\
                       .then_inc(hid_lo_ready, 1)

            def down(with_ada, with_mod=False):
                dve.wait_ge(y_zero, 1 if with_ada else 2)
                for j in range(8):
                    if with_mod and j == 2:
                        finish(5)
                        dve.wait_ge(mod_ready, 6)
                        dve.tensor_tensor(coef[:, 3], mod[:, 5], g_ffnp1, ALU.mult).then_inc(coef_ready, 1)
                        dve.wait_ge(coef_ready, 4)
                    convert()
                    dve.wait_ge(half_used, done.next())
                    add_group(y, 2 * j)

            def gate1(i, t):
                skip(4, 1)

            def up1(i, t):
                sg_read = banks.free()
                b = group()
                for o in range(2):
                    dve.wait_ge(bank_free[b + o], sg_read)
                    dve.tensor_tensor(hid[:, t + o], bank[:, b + o, 0:SEQ], sg[:, t + o], ALU.mult)\
                       .then_inc(bank_free[b + o], 1)
                rest(t)

            def more_taps(dst, i, b, t, first):
                for k in (1, 2):
                    for o in range(2):
                        if k == 1:
                            dve.wait_ge(tap_ready, taps.next())
                        else:
                            dve.wait_ge(tap_next, nexts.at(1, o + 1))
                        ch = i * 4 + (t + o + first)
                        dve.scalar_tensor_tensor(out=dst[:, t + o:t + o + 1, :], in0=bank[:, b + o:b + o + 1, k:k + SEQ],
                                                 scalar=pcol[:, 4 + k, ds(ch)], in1=dst[:, t + o:t + o + 1, :],
                                                 op0=ALU.mult, op1=ALU.add)\
                           .then_inc(tap_next if k == 1 else bank_free[b + o], 1)
                nexts.next(2)

            def gate2(i, t):
                more_taps(sg, i, group(), t, 0)

            def up2(i, t):
                b = group()
                more_taps(va, i, b, t, FT)
                for o in range(2):
                    dve.wait_ge(bank_free[b + o], banks.read)
                    dve.wait_ge(gelu_ready, gelus.next())
                    dve.tensor_tensor(hid[:, t + o], va[:, t + o], sg[:, t + o], ALU.mult).then_inc(hid_ready, 1)
                rest(t)

            def ffn(gate, up, n_taps, with_ada):
                def chunk(i, read):
                    for g in range(2):
                        read(i, 2 * g)
                chunk(0, gate)
                chunk(0, up)
                with loop(dve, NCHUNK - 1, (halves, 24), (done, 24), (banks, 12), (hids, 4), (taps, 2 * n_taps),
                          (nexts, 2 * n_taps), (gelus, n_taps)) as i:
                    chunk(i + 1, gate)
                    down(with_ada)
                    chunk(i + 1, up)
                down(with_ada, bool(with_ada))

            ffn(gate1, up1, 0, 1)
            inverse(SEQ)
            residual(y, SB, coef[:, 3])
            inverse(ALL)
            h_tiles(slice(0, ALL), g_mix2)
            skip(14, 3)
            dve.wait_ge(f_step, 4)
            dve.wait_ge(pads, 3)
            dve.scalar_tensor_tensor(out=lf[0][:, 256:], in0=lf[1][:, 256:], scalar=0.0, in1=sc_in[:, :],
                                     op0=ALU.min, op1=ALU.subtract).then_inc(scan, 1)
            for n in range(9):
                dve.wait_ge(scan, n + 1)
                a, b, s = lf[n % 2], lf[(n + 1) % 2], 1 << n
                dve.tensor_tensor(b[:, 256:], a[:, 256:], a[:, 256 - s:256 + ALL - s], ALU.add).then_inc(scan, 1)
            for j in range(3):
                ref = 256 + LIVE0 + QT * (j + 1) - 1
                dve.wait_ge(scan, 10)
                dve.tensor_scalar(rel[:, j, :], lf[1][:, 256:], lf[1][:, ref:ref + 1], None, ALU.subtract)\
                   .then_inc(rel_ready, 1)
            attend2 = lambda n, pair: attend(
                n, pair, sm, [(0, 384, bank[0:QT, B_S, 0:384]), (384, 272, bank[0:QT, B_N, 0:272])],
                [(QO[j], QW[j], j) for j in range(3)], QT, a_hi, a_lo, LIVE)
            skip(4, 1)
            dve.wait_ge(consts, 11)
            with loop(dve, 3, (halves, 16), (done, 16), (banks, 4), (scored, 2), (soft_n, 12), (exped, 6), (outs, 2)) as i:
                for n in range(16):
                    convert()
                    attend2(n, i)
                done.next(16)
                for _ in range(4):
                    banks.close()
            n_win = 0
            u_read = [banks.had[b // 2].at(1, 1) for b in range(4)]

            def window(t):
                nonlocal n_win
                w = WINDOWS[t // 2]
                last, s = u2[:, t, :], 1
                if t == 0:
                    for b in range(4):
                        dve.wait_ge(bank_free[b], u_read[b])
                k = 0
                while s < w:
                    dst = win[:, k % 2, :]
                    if n_win:
                        dve.wait_ge(win_step, n_win)
                    lo = 2 * s - 1
                    dve.tensor_tensor(dst[:, lo:], last[:, lo:], last[:, lo - s:META + ALL - s], ALU.add)\
                       .then_inc(win_step, 1)
                    n_win += 1
                    last, s, k = dst, 2 * s, k + 1
                dve.wait_ge(win_step, n_win)
                if t >= 2:
                    dve.wait_ge(d_lo_ready, t - 1)
                full = slice(META + LIVE0, META + ALL)
                args = dict(op0=ALU.mult, op1=ALU.subtract)
                if LIVE0 + 1 < w:
                    dve.scalar_tensor_tensor(out=sq[:, t % 2, 0:1], in0=last[:, full.start:full.start + 1],
                                             scalar=1.0 / (LIVE0 + 1), in1=u2[:, t, full.start:full.start + 1], **args)\
                       .then_inc(win_step, 1)
                    n_win += 1
                    dve.scalar_tensor_tensor(out=sq[:, t % 2, 1:LIVE], in0=last[:, full.start + 1:full.stop],
                                             scalar=1.0 / w, in1=u2[:, t, full.start + 1:full.stop], **args)\
                       .then_inc(d_ready, 1)
                else:
                    dve.scalar_tensor_tensor(out=sq[:, t % 2, 0:LIVE], in0=last[:, full], scalar=1.0 / w,
                                             in1=u2[:, t, full], **args).then_inc(d_ready, 1)

            def attn_part():
                b = banks.close()
                for o in range(2):
                    dve.tensor_tensor(ga_s[:, o:o + 1], bank[:, b + o:b + o + 1, 0:LIVE], ga_s[:, o:o + 1], ALU.mult)\
                       .then_inc(bank_free[b + o], 1)

            for n in range(10):
                convert()
                if n <= 8:
                    attend2(n, 3)
                if n == 8:
                    attend2(9, 3)
                if 1 <= n <= 8:
                    dve.wait_ge(d_hi_ready, n)
                    dve.tensor_tensor(d_lo[:, n - 1], sq[:, (n - 1) % 2, 0:LIVE], fp(d_hi[:, n - 1]), ALU.subtract)\
                       .then_inc(d_lo_ready, 1)
                if n < 8:
                    window(n)

            def gates_done():
                for _ in range(2):
                    b = banks.close()
                    for o in range(2):
                        dve.wait_ge(bank_free[b + o], banks.read)

            done.next(8)
            gates_done()
            dve.wait_ge(half_used, done.next(2))
            attn_part()
            for t in range(AT):
                if t % 4 == 0:
                    skip(1, 2)
                dve.wait_ge(pl_hi_ready, t + 1)
                dve.tensor_tensor(pl_lo[:, t], sq[:, t % 2, 0:LIVE], fp(pl_hi[:, t]), ALU.subtract).then_inc(pl_lo_ready, 1)
            ms = Count()

            def mix(body):
                b = group(2)
                for o in range(2):
                    dve.tensor_tensor(gp_s[:, o:o + 1], bank[:, b + o:b + o + 1, 0:LIVE], gp_s[:, o:o + 1], ALU.mult)\
                       .then_inc(bank_free[b + o], 1)
                for o in range(2):
                    dve.wait_ge(bank_free[b + o], banks.read)
                    dve.tensor_tensor(gp_s[:, o:o + 1], gp_s[:, o:o + 1], ga_s[:, o:o + 1], ALU.add).then_inc(m_ready, 1)
                for o in range(2):
                    dve.wait_ge(m_hi_ready, ms.next())
                    t = ds(body * 2 + o)
                    dve.tensor_tensor(m_lo[:, t], gp_s[:, o:o + 1], fp(m_hi[:, t]), ALU.subtract).then_inc(m_lo_ready, 1)

            with loop(dve, 7, (halves, 12), (done, 12), (banks, 4), (ms, 2)) as i:
                mix(i)
                for _ in range(8):
                    convert()
                done.next(8)
                gates_done()
                convert()
                convert()
                dve.wait_ge(half_used, done.next(2))
                attn_part()
            mix(7)
            with loop(dve, 4, (halves, 8), (done, 8), (banks, 2)) as i:
                skip(8, 2)
            inverse(LIVE)
            residual(y2, ST, g_mixp2)
            inverse(LIVE)
            h_tiles(ST, g_ffn2)
            ffn(gate2, up2, 4, 0)
            inverse(SEQ)
            residual(y, SB, g_ffnp2)

        @block.tensor
        def _(pe):
            halves, banks = Count(), Banks()

            def half(x_hi, x_lo, kts, width, first, last, fixed=None):
                slot = halves.mod(RING)
                b = banks.bank() if fixed is None else fixed
                pe.wait_ge(lo_ready, halves.at(1, RING + 1))
                if first and fixed is None:
                    for o in range(2):
                        pe.wait_ge(bank_free[b + o], banks.free())
                for k, kt in enumerate(kts):
                    for o in range(2 if fixed is None else 1):
                        tile = (k, o) if fixed is None else (k // 2, k % 2)
                        wh = w_hi[:, slot, tile[0], tile[1] * 128:tile[1] * 128 + 128]
                        wl = w_lo[:, slot, tile[0], tile[1] * 128:tile[1] * 128 + 128]
                        dst = bank[:, b + o, 0:width]
                        pe.matmul(dst, wh, x_hi(kt), start=first and k == 0, stop=False)
                        pe.matmul(dst, wh, x_lo(kt), start=False, stop=False)
                        mm = pe.matmul(dst, wl, x_hi(kt), start=False, stop=last and k == len(kts) - 1)
                mm.then_inc(half_used, 1)
                halves.next()
                if last and fixed is None:
                    banks.close()

            def product(x_hi, x_lo, cols, n_kt=KT, kt0=0, ready=None):
                for q in range(n_kt // 4):
                    quarter(q, x_hi, x_lo, cols, n_kt, kt0, ready)

            def quarter(q, x_hi, x_lo, cols, n_kt=KT, kt0=0, ready=None):
                if ready is not None:
                    pe.wait_ge(ready[0], ready[1] + 4 * q + 4)
                half(lambda kt: x_hi[:, kt, cols], lambda kt: x_lo[:, kt, cols],
                     range(kt0 + 4 * q, kt0 + 4 * q + 4), cols.stop - cols.start, q == 0, q == n_kt // 4 - 1)

            used = Count()

            def turn(pairs):
                n = used.c
                if n >= 4:
                    pe.wait_ge(tr_copied, n - 3)
                for dst, src in pairs:
                    rows = src.shape[0]
                    mm = pe.transpose(dst(bank[:, B_S + n % 4, :]), src, ident[0:rows, 0:rows])
                mm.then_inc(tr_done, 1)
                used.next()

            pe.wait_ge(consts, 5)
            pe.wait_ge(c_loaded, 48)
            turn([(lambda b: b[:, 0:120], prow[0:120, 0])])
            pe.wait_ge(rows_loaded, 16 * 23)
            for n in range(8):
                t, j = n // 4, n % 4
                turn([(lambda b, a=a: b[:, 128 * a:128 * a + 128], xrow[:, t, 512 * j + 128 * a:512 * j + 128 * a + 128])
                      for a in range(4)])
            turn([(lambda b: b[:, 0:88], prow[0:88, 1])])
            turn([(lambda b: b[:, 0:128], prow[:, 2])])
            turn([(lambda b, a=a: b[:, 128 * a:128 * a + 88], prow[0:88, 3 + a]) for a in range(4)])
            turn([(lambda b, a=a: b[:, META * a:META * a + META], mrow[:, 128 * a:128 * a + 128]) for a in range(KT)])
            turn([(lambda b, a=a: b[:, 32 * a:32 * a + CONV_K], cwrow[:, 128 * a:128 * a + 128]) for a in range(AT)])
            sqs = Count()

            def channel_sum(kt, width, n=KT):
                pe.wait_ge(sq_ready, sqs.next())
                pe.matmul(bank[:, B_N, 0:width], ones[:, :], sq[:, kt % 2, 0:width],
                          start=kt == 0, stop=kt == n - 1).then_inc(sq_used, 1)

            def squares_summed(width):
                pe.wait_ge(sq_used, sqs.next(KT))
                pe.matmul(bank[:, B_N, 0:width], ones[:, :], rstd[:, 0:width], start=True, stop=True).then_inc(sum_ready, 1)

            def channel_sums(width, n=KT):
                for kt in range(n):
                    channel_sum(kt, width, n)

            def ada_total(acc):
                for j in range(KT):
                    mm = pe.matmul(bank[:, B_N, 496 + j:497 + j], acc[:, 128 * j:128 * j + 128], ones[:, 0:1],
                                   start=True, stop=True)
                mm.then_inc(ada_sum, 1)

            pe.wait_ge(tr_copied, 14)
            channel_sums(SEQ)
            for n in range(2):
                pe.wait_ge(pre_used, 4 + 16 * (n + 1))
                if n:
                    pe.wait_ge(mod_ready, n)
                else:
                    pe.wait_ge(root_ready, 1)
                ada_total(acc_b if n else acc)
            with loop(pe, 4, (halves, 8), (banks, 2)):
                for n in range(2):
                    product(h_hi, h_lo, SB, ready=(h_ready, 0))
            probs_n, ptc, vtc, sels = Count(), Count(), Count(), Count()

            def scores(tiles, v_parts):
                for n, mats in enumerate(tiles):
                    for m, (dst, lhs, rhs) in enumerate(mats):
                        mm = pe.matmul(dst, lhs, rhs, start=m == 0, stop=m == len(mats) - 1)
                mm.then_inc(s_done, 1)
                for dst, src in v_parts:
                    mm = pe.transpose(dst, src, ident[:, :])
                mm.then_inc(v_done, 1)

            def turn_p(n_tiles, parts):
                pe.wait_ge(p_ready, probs_n.next(n_tiles))
                for dst, src in parts:
                    rows = src.shape[0]
                    mm = pe.transpose(dst, src, ident[0:rows, 0:rows])
                mm.then_inc(pt_done, 1)

            def weigh(n_pt, n_v, parts):
                pe.wait_ge(pt_copied, ptc.next(n_pt))
                pe.wait_ge(v_copied, vtc.next(n_v))
                for m, (dst, v, p) in enumerate(parts):
                    mm = pe.matmul(dst, v, p, start=m == 0, stop=m == len(parts) - 1)
                mm.then_inc(o_done, 1)

            B = lambda b, lo, hi, rows=128: bank[0:rows, b, lo:hi]

            def attend1(n, v_ready):
                q, k, v = (lambda o, j=j: qkv1[:, j, o, :] for j in range(3))

                def head(o):
                    scores([[(B(B_S, 256 * j, 256 * j + 256), q(o)[:, 128 * j:128 * j + 128], k(o))] for j in range(2)],
                           [(B(B_V, 128 * t, 128 * t + 128), v(o)[:, 128 * t:128 * t + 128]) for t in range(2)])

                if n == 1:
                    for o in range(2):
                        pe.wait_ge(bank_free[o], v_ready)
                    head(0)
                if n in (4, 8):
                    turn_p(2, [(B(B_P, 0, 128), sm1[:, 0:128]), (B(B_P, 128, 256), sm1[:, 256:384]),
                               (B(B_P, 256, 384), sm1[:, 384:512])])
                if n in (5, 9):
                    weigh(1, 1, [(B(B_P, 0, 256), v_t1[:, 0, :], p_t1[:, 0:256]),
                                 (B(B_P, 128, 256), v_t1[:, 1, :], p_t1[:, 256:384])])
                if n == 5:
                    head(1)

            def heads1(attended):
                banks.pair = 0
                v_ready = banks.had[0].at(1, 1)
                for n in range(12):
                    if attended:
                        attend1(n, v_ready)
                    elif n == 5:
                        pe.wait_ge(ada_used, 16)
                        pe.wait_ge(ada_rest, 16)
                        ada_total(acc)
                    quarter(n % 4, h_hi, h_lo, SB)

            heads1(False)
            with loop(pe, 3, (halves, 12), (banks, 3), (probs_n, 4), (ptc, 2), (vtc, 2)):
                heads1(True)
            v_ready = banks.had[0].at(1, 1)
            for n in range(16):
                if n <= 8:
                    attend1(n, v_ready)
                if n == 13:
                    pe.wait_ge(ada_used, 44)
                    pe.wait_ge(ada_rest, 44)
                    pe.wait_ge(ln_term, 1)
                    ada_total(acc_b)
                if n == 8:
                    pe.wait_ge(conv_step, 1 + AT * (CONV_K + 1))
                    pe.wait_ge(mod_ready, 3)
                    for t in range(AT):
                        mm = pe.matmul(bank[:, B_N, 0:SEQ], ones[:, :], cv[:, t, :], start=t == 0, stop=t == AT - 1)
                    mm.then_inc(mu_sum, 1)
                    attend1(9, v_ready)
                    pe.wait_ge(o_lo, HEADS)
                if n == 10:
                    channel_sums(SEQ, AT)
                if n == 0:
                    pe.wait_ge(o_lo, HEADS // 2)
                half(lambda kt: a1_hi[:, kt, :], lambda kt: a1_lo[:, kt, :],
                     range(n // 8 * 4, n // 8 * 4 + 4), SEQ, True, True)
            pe.wait_ge(ada_used, 48)
            pe.wait_ge(ada_rest, 48)
            pe.wait_ge(mod_ready, 4)
            ada_total(acc)
            for j in range(8):
                for q in range(2):
                    quarter(q, c_hi, c_lo, SB, AT, ready=(mix_ready, 0))
            pe.wait_ge(mod_ready, 5)
            squares_summed(SEQ)
            channel_sums(SEQ)
            downs = Count()

            def ffn(cols, h_base, with_ada):
                def chunk(ready=None):
                    for g in range(2):
                        product(h_hi, h_lo, cols, ready=ready)

                def down():
                    pe.wait_ge(hid_lo_ready, downs.next(4))
                    for j in range(8):
                        half(lambda kt: hid_hi[:, kt], lambda kt: hid_lo[:, kt], range(4), SEQ, True, True)

                chunk((h_ready, h_base))
                chunk()
                with loop(pe, NCHUNK - 1, (halves, 24), (banks, 12), (downs, 4)):
                    chunk()
                    down()
                    chunk()
                pe.wait_ge(hid_lo_ready, downs.next(4))
                for j in range(8):
                    half(lambda kt: hid_hi[:, kt], lambda kt: hid_lo[:, kt], range(4), SEQ, True, True)
                    if j == 0 and with_ada:
                        pe.wait_ge(ada_used, 64)
                        ada_total(acc)
                pe.wait_ge(mod_ready, 6)
                squares_summed(SEQ)

            ffn(SB, KT, True)
            every, narrow = slice(0, ALL), slice(0, LIVE)
            channel_sums(ALL)
            def attend2(n, v_ready):
                def head(o):
                    pe.wait_ge(sel_ready, sels.next())
                    q, k, v = (qkv[:, j, o, :] for j in range(3))
                    dst = (B(B_S, 0, 128, QT), B(B_S, 128, 384, QT), B(B_N, 0, 272, QT))
                    scores([[(dst[j], q[:, LIVE0 + QT * j:LIVE0 + QT * j + QT], k[:, 0:QW[j]]),
                             (dst[j], sel[:, o, :], rel[:, j, 0:QW[j]])] for j in range(3)],
                           [(B(B_V, 128 * t, 128 * t + 128, min(128, ALL - 128 * t)),
                             v[:, 128 * t:min(128 * t + 128, ALL)]) for t in range(3)])

                if n == 1:
                    for b in range(4):
                        pe.wait_ge(bank_free[b], v_ready[b // 2])
                    head(0)
                if n in (4, 8):
                    P = lambda j, k, w=128: sm[0:QT, QO[j] + 128 * k:QO[j] + 128 * k + w]
                    turn_p(3, [(B(B_P, 0, QT), P(0, 0)), (B(B_P, QT, 2 * QT), P(1, 0)),
                               (B(B_P, 2 * QT, 3 * QT), P(2, 0)), (B(B_P, 3 * QT, 4 * QT), P(1, 1)),
                               (B(B_P, 4 * QT, 5 * QT), P(2, 1)), (B(B_V, 384, 384 + QT, META), P(2, 2, META))])
                if n in (5, 9):
                    weigh(2, 2, [(B(B_P, 0, LIVE), v_t[:, 0, :], p_t[:, 0:3 * QT]),
                                 (B(B_P, QT, LIVE), v_t[:, 1, :], p_t[:, 3 * QT:5 * QT]),
                                 (B(B_P, 2 * QT, LIVE), v_t[0:META, 2, :], p_t[0:META, 5 * QT:6 * QT])])
                if n == 5:
                    head(1)

            for n in range(16):
                if n == 8:
                    for q in range(2):
                        half(lambda kt: h_hi[:, kt, :], lambda kt: h_lo[:, kt, :], range(8 * q, 8 * q + 8), ALL,
                             q == 0, q == 1, fixed=B_N)
                quarter(n % 4, h_hi, h_lo, every, ready=(h_ready, 2 * KT))
            pe.wait_ge(rel_ready, 3)
            with loop(pe, 3, (halves, 16), (banks, 4), (sels, 2), (probs_n, 6), (ptc, 4), (vtc, 4)):
                v_ready = [banks.had[n].at(1, 1) for n in range(2)]
                for n in range(16):
                    attend2(n, v_ready)
                    quarter(n % 4, h_hi, h_lo, every)
            v_ready = [banks.had[n].at(1, 1) for n in range(2)]
            for n in range(10):
                attend2(n, v_ready)
                if n < 8:
                    quarter(n % 4, h_hi, h_lo, ST)
            pe.wait_ge(o_lo, 2 * HEADS)
            product(a_hi, a_lo, narrow, AT)
            for h in range(2):
                slot = halves.mod(RING)
                pe.wait_ge(lo_ready, halves.at(1, RING + 1))
                pe.wait_ge(d_lo_ready, 4 * h + 4)
                for g in range(2):
                    b = banks.bank()
                    for o in range(2):
                        pe.wait_ge(bank_free[b + o], banks.free())
                        for k in range(2):
                            wh = w_hi[:, slot, 2 * g + k, o * 128:o * 128 + 128]
                            wl = w_lo[:, slot, 2 * g + k, o * 128:o * 128 + 128]
                            t = 4 * h + 2 * g + k
                            dst = bank[:, b + o, 0:LIVE]
                            pe.matmul(dst, wh, d_hi[:, t], start=k == 0, stop=False)
                            pe.matmul(dst, wh, d_lo[:, t], start=False, stop=False)
                            mm = pe.matmul(dst, wl, d_hi[:, t], start=False, stop=k == 1)
                    banks.close()
                mm.then_inc(half_used, 1)
                halves.next()
            with loop(pe, 7, (halves, 12), (banks, 4)):
                product(pl_hi, pl_lo, narrow, AT, ready=(pl_lo_ready, 0))
                product(h_hi, h_lo, ST)
                product(h_hi, h_lo, ST)
                product(a_hi, a_lo, narrow, AT)
            product(pl_hi, pl_lo, narrow, AT)
            pe.wait_ge(m_lo_ready, KT)
            with loop(pe, 3, (halves, 8), (banks, 2)):
                for n in range(2):
                    product(m_hi, m_lo, narrow)
            for n in range(8):
                quarter(n % 4, m_hi, m_lo, narrow)
            squares_summed(LIVE)
            channel_sums(LIVE)
            ffn(ST, 3 * KT, False)
            for n in range(8):
                j, t = n // 2, n % 2
                for kt in range(4 * j, 4 * j + 4):
                    wait_x(pe, kt, 3, x_ready, x_added)
                if n >= 4:
                    pe.wait_ge(last_copied, n - 3)
                for a in range(4):
                    mm = pe.transpose(bank[:, B_S + n % 4, 128 * a:128 * a + 128],
                                      xt[:, 4 * j + a, META + 128 * t:META + 128 * t + 128], ident[:, :])
                mm.then_inc(last_done, 1)


_INS = ['x', 'c', 'ada_w', 'ada_b', 'mix_pre_g', 'mix_post_g', 'w_in', 'conv_w', 'conv_b', 'conv_ln_g',
        'conv_ln_b', 'w_out', 'ffn_pre_g', 'ffn_post_g', 'w_gate', 'w_up', 'w_down', 'meta_tokens_2',
        'mix_pre_g_2', 'w_in_2', 'b_in_2', 'w_attn_o_2', 'pool_w_2', 'pool_scale_2', 'w_pool_o_2', 'w_out_2',
        'mix_post_g_2', 'ffn_pre_g_2', 'w_ffn_up_2', 'ffn_conv_w_2', 'ffn_conv_b_2', 'w_ffn_down_2',
        'ffn_post_g_2']


def kernel(**inputs):
    import numpy as _np
    import concourse.bacc as _bacc
    from concourse.bass_utils import run_bass_kernel_spmd as _run

    nc = _bacc.Bacc("TRN2", target_bir_lowering=False, num_devices=1)
    arrays, args = {}, []
    for name in _INS:
        a = _np.ascontiguousarray(inputs[name])
        if a.shape[0] == 1:
            a = a.reshape(a.shape[1:])
        arrays[f"in_{name}"] = a
        args.append(nc.dram_tensor(f"in_{name}", a.shape, mybir.dt.float32, kind="ExternalInput").ap())
    args.append(nc.dram_tensor("out", (SEQ, D), mybir.dt.float32, kind="ExternalOutput").ap())
    build(nc, *args)
    r = _run(nc, [arrays], core_ids=[0])
    return r.results[0]["out"].reshape(1, SEQ, D)
```
